# Optimizing a Trainium2 kernel written in Bass

```python
import jax, jax.numpy as jnp
from jax import lax
import numpy as np

D_MODEL = 1024
BATCH = 1
SEQ = 512
DEPTH = 2
DEC_BATCH = 8
DEC_SEQ = 8
PAST_LEN = 2048
PAGE_SIZE = 128

N_A = DEPTH // 2
N_B = DEPTH - N_A
D_CONV = D_MODEL
CONV_W = 3
N_HEADS = 16
HEAD_DIM = D_MODEL // N_HEADS
D_ATTN = N_HEADS * HEAD_DIM
Q_BLOCK = 128
EPS = 1e-6

kernel_name = 'yoco_shortconv_forgetting_attn_step'

def _rmsnorm(x, g):
    xf = x.astype(jnp.float32)
    r = lax.rsqrt(jnp.mean(xf * xf, axis=-1, keepdims=True) + EPS)
    return (xf * r).astype(x.dtype) * g

def _conv_layer(x, state, g, w_in, w_conv, w_out):
    b, c, u, z = jnp.split(_rmsnorm(x, g) @ w_in, 4, axis=-1)
    v = c * u
    ext = jnp.concatenate([state.astype(v.dtype), v], axis=1)
    L = x.shape[1]
    conv = ext[:, 0:L] * w_conv[0]
    for j in range(1, CONV_W):
        conv = conv + ext[:, j:j + L] * w_conv[j]
    y = (jax.nn.silu(z) * b * conv) @ w_out
    return x + y, ext[:, -(CONV_W - 1):]

def _shared_kv(h, g, w_kv, f_bias, g_k):
    N, L, _ = h.shape
    k, v, f = jnp.split(_rmsnorm(h, g) @ w_kv, [D_ATTN, 2 * D_ATTN], axis=-1)
    k = _rmsnorm(k.reshape(N, L, N_HEADS, HEAD_DIM), g_k)
    v = v.reshape(N, L, N_HEADS, HEAD_DIM)
    logf = jax.nn.log_sigmoid((f + f_bias).astype(jnp.float32))
    return k, v, logf

def _fox_attend(q, fq, qpos, k, v, fk, kpos):
    s = jnp.einsum('nqhd,nkhd->nhqk', q, k).astype(jnp.float32) * (HEAD_DIM ** -0.5)
    s = s + (jnp.transpose(fq, (0, 2, 1))[:, :, :, None]
             - jnp.transpose(fk, (0, 2, 1))[:, :, None, :])
    mask = kpos[None, :] <= qpos[:, None]
    s = jnp.where(mask[None, None], s, -jnp.inf)
    p = jax.nn.softmax(s, axis=-1)
    return jnp.einsum('nhqk,nkhd->nqhd', p.astype(v.dtype), v)

def _prompt_attend(q, k, v, F):
    N, L = q.shape[:2]
    kpos = jnp.arange(L)

    def blk(i):
        st = i * Q_BLOCK
        qb = lax.dynamic_slice_in_dim(q, st, Q_BLOCK, axis=1)
        fb = lax.dynamic_slice_in_dim(F, st, Q_BLOCK, axis=1)
        return _fox_attend(qb, fb, st + jnp.arange(Q_BLOCK), k, v, F, kpos)

    o = lax.map(blk, jnp.arange(L // Q_BLOCK))
    return jnp.moveaxis(o, 0, 1).reshape(q.shape)

def _fox_layer(x, attend, g, w_in, g_q, w_out):
    N, L, _ = x.shape
    q, z = jnp.split(_rmsnorm(x, g) @ w_in, 2, axis=-1)
    q = _rmsnorm(q.reshape(N, L, N_HEADS, HEAD_DIM), g_q)
    o = attend(q).reshape(N, L, D_ATTN)
    return x + (o * jax.nn.silu(z)) @ w_out

def setup_inputs(seed: int = 0) -> dict:
    key = jax.random.key(seed)
    ks = jax.random.split(key, 20)
    n_pages = PAST_LEN // PAGE_SIZE
    n_used = DEC_BATCH * n_pages
    n_pool = n_used + n_used // 4
    nrm = lambda k, shape, s=1.0: s * jax.random.normal(k, shape, jnp.float32)
    page_table = jax.random.permutation(ks[0], n_pool)[:n_used].reshape(DEC_BATCH, n_pages).astype(jnp.int32)
    return {
        'x_prompt': nrm(ks[1], (BATCH, SEQ, D_MODEL)),
        'x_sample': nrm(ks[2], (DEC_BATCH, DEC_SEQ, D_MODEL)),
        'state_conv': nrm(ks[3], (N_A, DEC_BATCH, CONV_W - 1, D_CONV)),
        'cache_k': nrm(ks[4], (n_pool, PAGE_SIZE, N_HEADS, HEAD_DIM)),
        'cache_v': nrm(ks[5], (n_pool, PAGE_SIZE, N_HEADS, HEAD_DIM)),
        'cache_logf': jax.nn.log_sigmoid(2.0 + nrm(ks[6], (n_pool, PAGE_SIZE, N_HEADS))),
        'page_table': page_table,
        'a_norm': 1.0 + nrm(ks[7], (N_A, D_MODEL), 0.02),
        'a_w_in': nrm(ks[8], (N_A, D_MODEL, 4 * D_CONV), D_MODEL ** -0.5),
        'a_conv': nrm(ks[9], (N_A, CONV_W, D_CONV), CONV_W ** -0.5),
        'a_w_out': nrm(ks[10], (N_A, D_CONV, D_MODEL), D_CONV ** -0.5),
        'kv_norm': 1.0 + nrm(ks[11], (D_MODEL,), 0.02),
        'kv_w': nrm(ks[12], (D_MODEL, 2 * D_ATTN + N_HEADS), D_MODEL ** -0.5),
        'kv_fbias': 2.0 + nrm(ks[13], (N_HEADS,), 0.1),
        'k_norm': 1.0 + nrm(ks[14], (HEAD_DIM,), 0.02),
        'b_norm': 1.0 + nrm(ks[15], (N_B, D_MODEL), 0.02),
        'b_w_in': nrm(ks[16], (N_B, D_MODEL, 2 * D_ATTN), D_MODEL ** -0.5),
        'q_norm': 1.0 + nrm(ks[17], (N_B, HEAD_DIM), 0.02),
        'b_w_out': nrm(ks[18], (N_B, D_ATTN, D_MODEL), D_ATTN ** -0.5),
    }

def reference(x_prompt, x_sample, state_conv, cache_k, cache_v, cache_logf, page_table,
              a_norm, a_w_in, a_conv, a_w_out, kv_norm, kv_w, kv_fbias, k_norm,
              b_norm, b_w_in, q_norm, b_w_out):
    nb, ts = x_sample.shape[:2]
    hp, hs = x_prompt, x_sample
    conv_p, conv_s = [], []
    prompt_attend = sample_attend = None
    for l in range(DEPTH):
        if l < N_A:
            zero_state = jnp.zeros((hp.shape[0], CONV_W - 1, D_CONV), hp.dtype)
            hp, sp = _conv_layer(hp, zero_state, a_norm[l], a_w_in[l], a_conv[l], a_w_out[l])
            hs, ss = _conv_layer(hs, state_conv[l], a_norm[l], a_w_in[l], a_conv[l], a_w_out[l])
            conv_p.append(sp)
            conv_s.append(ss)
            continue
        if l == N_A:
            k_p, v_p, lf_p = _shared_kv(hp, kv_norm, kv_w, kv_fbias, k_norm)
            k_s, v_s, lf_s = _shared_kv(hs, kv_norm, kv_w, kv_fbias, k_norm)
            F_p = jnp.cumsum(lf_p, axis=1)
            prompt_attend = lambda q: _prompt_attend(q, k_p, v_p, F_p)
            k_past = cache_k[page_table].reshape(nb, -1, N_HEADS, HEAD_DIM)
            v_past = cache_v[page_table].reshape(nb, -1, N_HEADS, HEAD_DIM)
            lf_past = cache_logf[page_table].reshape(nb, -1, N_HEADS).astype(jnp.float32)
            past = k_past.shape[1]
            k_all = jnp.concatenate([k_past, k_s.astype(k_past.dtype)], axis=1)
            v_all = jnp.concatenate([v_past, v_s.astype(v_past.dtype)], axis=1)
            F_all = jnp.cumsum(jnp.concatenate([lf_past, lf_s], axis=1), axis=1)
            kpos_all = jnp.arange(past + ts)
            qpos_s = past + jnp.arange(ts)
            sample_attend = lambda q: _fox_attend(q, F_all[:, past:], qpos_s,
                                                  k_all, v_all, F_all, kpos_all)
        j = l - N_A
        hp = _fox_layer(hp, prompt_attend, b_norm[j], b_w_in[j], q_norm[j], b_w_out[j])
        hs = _fox_layer(hs, sample_attend, b_norm[j], b_w_in[j], q_norm[j], b_w_out[j])
    conv_prompt = jnp.stack(conv_p, axis=0)
    conv_sample = jnp.stack(conv_s, axis=0)
    return (hp, hs, conv_prompt, conv_sample, k_p, v_p, lf_p, k_s, v_s, lf_s)


_drawn_inputs = setup_inputs


def setup_inputs(seed=0):
    import zlib

    import numpy as np

    out = dict(_drawn_inputs(seed))
    spreads = {}
    factors = {'kv_norm': 2.808, 'k_norm': 2.914, 'b_norm': 8.0, 'q_norm': 8.0}
    for name, (base, spread) in spreads.items():
        noise = np.random.default_rng([zlib.crc32(name.encode()), seed]).standard_normal(out[name].shape)
        drawn = base * np.exp(spread * noise) if base else spread * noise
        out[name] = __import__('jax').numpy.asarray(drawn.astype(out[name].dtype))
    for name, factor in factors.items():
        out[name] = (out[name] * factor).astype(out[name].dtype)
    return out
```

```python
from contextlib import ExitStack

import concourse.bass as bass
from concourse import mybir

F32 = mybir.dt.float32
F32R = mybir.dt.float32r
BF16 = mybir.dt.bfloat16
I32 = mybir.dt.int32
ALU = mybir.AluOpType
ACT = mybir.ActivationFunctionType
AX = mybir.AxisListType.X

P = 128
D = 1024
KT = D // P
SEQ = 512
NB = 8
NQ = 8
NS = NB * NQ
TOK = SEQ + NS
H = 16
HD = 64
CONV_W = 3
PAGE = 128
NPG = 16
PAST = NPG * PAGE
QB = SEQ // P
EPS = 1e-6
NT = 5
HALF = 256
TAIL = TOK - HALF
NEG = -1e30
RING = 8
STREAM = 2 * NPG
SLAB = 256
NSLAB = D // SLAB

C_ID, C_ONESB, C_TRI, C_CM, C_NM, C_QD, C_RST, C_ONE = 0, 128, 256, 384, 512, 1024, 1088, 1152
C_ALL = 1153
G_A, G_KV, G_B, G_CONV, G_K, G_Q = 0, 8, 16, 24, 48, 49
G_ALL = 50


def rows(t):
    return P if t < QB else NS


def toks(t):
    return slice(t * P, t * P + rows(t))


class Chain:

    def __init__(self, eng, sem):
        self.eng, self.sem, self.base, self.n = eng, sem, 0, 0

    def link(self, ins):
        self.n += 1
        ins.then_inc(self.sem, 1)
        self.eng.wait_ge(self.sem, self.base + self.n)

    def loop(self, i, per, done):
        self.base, self.n, self.per = i * per + done, 0, per

    def end(self):
        assert self.n == self.per, (self.n, self.per)


def build(nc, ctx, x_prompt, x_sample, state_conv, cache_k, cache_v, cache_logf, page_table,
          a_norm, a_w_in, a_conv, a_w_out, kv_norm, kv_w, kv_fbias, k_norm,
          b_norm, b_w_in, q_norm, b_w_out, table,
          y_prompt, y_sample, conv_prompt, conv_sample, k_prompt, v_prompt, logf_prompt,
          k_sample, v_sample, logf_sample):
    n_pool = cache_k.shape[0]

    suffix_dram = nc.dram_tensor("suffix_scratch", [NB, H, PAST], F32, kind="Internal").ap()
    f_dram = nc.dram_tensor("f_scratch", [H, TOK], F32, kind="Internal").ap()
    h_dram = nc.dram_tensor("h_scratch", [NT * P, D], F32, kind="Internal").ap()

    at = {"top": nc.sbuf_base + (-nc.sbuf_base) % 32}

    def place(name, shape, dt=F32, over=None):
        n = 4 if dt is not BF16 else 2
        for s in shape[1:]:
            n *= s
        n += (-n) % 32
        off = at["top"] if over is None else over
        if over is None:
            at["top"] += n
        at[name] = off
        return nc.alloc_sbuf_tensor_at(name, shape, dt, offset=off)

    XH = place("xn_high", [P, KT, TOK], F32R)
    XL = place("xn_low", [P, KT, TOK], F32R)
    GH = place("gated_high", [P, KT, TOK], F32R)
    GL = place("gated_low", [P, KT, TOK], F32R)
    WH = place("w_high", [P, 2, KT, P], F32R)
    WL = place("w_low", [P, 2, KT, P], F32R)
    WR = place("w_raw", [P, 2, KT, P])
    ring = place("page_ring", [P, RING, D])
    KTS = place("k_turned", [P, KT, 2 * PAGE])
    PTS = place("p_turned", [P, NPG, P])
    SS = place("sample_scores", [P, PAST])
    SFX = place("suffix", [P, 2, 512])
    QZ = place("q_spread", [P, NB, KT, 32])
    CT = place("constants", [P, C_ALL])
    QT = place("q_t", [P, SEQ])
    KN_T = place("k_t", [P, TOK])
    VT = place("v_t", [P, TOK])
    SZ = place("silu_z", [P, TOK])
    SQ = place("squares", [P, TOK])
    RR = place("rsqrt", [P, TOK])
    KN = place("k_rows", [P, NT, P])
    VN = place("v_rows", [P, QB, P])
    FB = place("f_broad", [P, 2, SEQ])
    PB = place("probs", [P, 2, SEQ])
    PT = place("probs_t", [P, 2, QB, P])
    OPAST = place("o_past", [P, NB, 4 * HD])
    KS = place("ks_t", [P, KT, NS])
    VS = place("vs_rows", [NS, D])
    SZS = place("silu_zs", [P, KT, NS])
    GAIN = place("gains", [P, G_ALL])
    GQ = place("gain_q", [P, 1])
    IDB = place("ident_b", [P, P], BF16)
    CMB = place("causal_b", [P, P], BF16)
    CST = place("conv_tail", [P, KT, 18])
    ST = place("conv_state", [P, KT, 2 * NB])
    LFN = place("logf_rows", [P, NT, H])
    FQN = place("f_rows", [P, QB, H])
    CK = place("f_new", [P, NS])
    CQ = place("f_query", [P, NB])
    TINY = place("tiny", [P, 64])
    WFR = place("wf_raw", [P, KT, H], over=at["squares"])
    WFH = place("wf_high", [P, KT, H], F32R)
    WFL = place("wf_low", [P, KT, H], F32R)
    PTAB = place("page_row", [1, NB * NPG], I32)
    PIDX = place("page_column", [P, 1], I32)
    FBIAS = place("f_bias", [H, 1])
    QC = place("q_current", [P, KT, 32])
    MS = place("max_past", [P, NB])
    LS = place("sum_past", [P, NB])
    assert at["top"] <= nc.sbuf_usable_end, at["top"]
    X = place("residual", [P, NT, D], over=at["page_ring"])
    LF = place("logf_pages", [P, PAGE, H], over=at["page_ring"] + 5 * 4 * D)
    XS = place("x_scaled", [P, D], over=at["page_ring"] + 7 * 4 * D)
    CS = place("logf_sums", [P, H, PAGE], over=at["sample_scores"])
    STN = place("state_rows", [2 * NB, D], over=at["suffix"])
    GR = place("gain_rows", [G_ALL, P], over=at["f_broad"])
    JUNK = place("junk", [P, D], over=at["probs"])
    EXT = place("conv_in", [P, SEQ + 2], over=at["probs"])
    EXTS = place("conv_in_s", [P, NB, NQ + 2], over=at["probs"] + 4 * (SEQ + 8))
    CO = place("conv_rows", [18, D], over=at["probs_t"])
    WHB = place("w_high_b", [P, KT, SLAB], F32R, over=at["k_turned"])
    WLB = place("w_low_b", [P, KT, SLAB], F32R, over=at["p_turned"])
    WHA = WH[:, :, :, :].rearrange("p s k n -> p (s k n)").rearrange("p (k n) -> p k n", k=KT)
    WLA = WL[:, :, :, :].rearrange("p s k n -> p (s k n)").rearrange("p (k n) -> p k n", k=KT)
    WRA = WR[:, :, :, :].rearrange("p s k n -> p (s k n)").rearrange("p (k n) -> p k n", k=KT)
    slab_h = [WHA, WHB[:, :, :]]
    slab_l = [WLA, WLB[:, :, :]]
    QSN = place("qs_rows", [NS, D], over=at["probs"])
    QSS = place("qs_squares", [NS, D], over=at["o_past"])
    FA = place("f_raw", [H, TOK], over=at["k_t"])
    FN = place("f_neg", [H, TOK], over=at["v_t"])
    FE = place("f_exp", [H, TOK], over=at["silu_z"])
    FL = place("f_log", [H, TOK], over=at["rsqrt"])
    FT = place("f_sum", [H, TOK], over=at["f_broad"])
    SN = place("new_scores", [P, NB, NS], over=at["suffix"])
    NBI = place("new_bias", [P, NB, NS], over=at["suffix"] + 4 * NB * NS)
    PNT = place("new_probs_t", [NS, NB, P], over=at["probs"])
    OM = place("o_merged", [P, NB, 4 * HD], over=at["sample_scores"])
    GS = place("gated_s", [P, KT, NS], over=at["probs_t"])

    ident = CT[:, C_ID:C_ID + P]
    PS = ctx.enter_context(nc.psum_tensor("psum", [P, 8, 512], F32))
    D0, D1, T0, T1, C0, C1, OP, OS = range(8)

    def sem(name):
        return ctx.enter_context(nc.semaphore(name))

    s_ch_act, s_ch_dve, s_ch_pool = sem("act_chain"), sem("dve_chain"), sem("pool_chain")
    s_const, s_rows, s_idx = sem("constants_loaded"), sem("rows_loaded"), sem("pages_loaded")
    s_x = [sem(f"x_loaded{t}") for t in range(NT)]
    s_lf = sem("logf_gathered")
    s_cs, s_rtot, s_sfx, s_sfx_st = sem("logf_summed"), sem("later_pages"), sem("suffix_ready"), sem("suffix_stored")
    s_gt, s_gain, s_stt, s_st = sem("gains_turned"), sem("gains_ready"), sem("state_turned"), sem("state_ready")
    s_bf = sem("bf16_consts")
    s_zero = sem("q_spread_zero")
    s_xs, s_xt, s_xh, s_xl = sem("x_scaled"), sem("x_turned"), sem("xn_high_ready"), sem("xn_low_ready")
    a_raw = [sem(f"a_w_loaded{s}") for s in range(2)]
    a_scaled, a_high, a_split = sem("a_w_scaled"), sem("a_w_high"), sem("a_w_split")
    a_proj, a_c, a_v, a_z, a_cvz = sem("a_projected"), sem("a_c_out"), sem("a_v_made"), sem("a_silu"), sem("a_cvz")
    a_cv, a_g, a_gh, a_gl = sem("a_conv"), sem("a_gated"), sem("a_gated_high"), sem("a_gated_low")
    l_raw, l_scaled, l_high, l_split = sem("slab_loaded"), sem("slab_scaled"), sem("slab_high"), sem("slab_split")
    l_tile, l_evac = sem("out_tile"), sem("out_added")
    s_cost = sem("conv_stored")
    s_hst, s_ctt, s_co = sem("h_stored"), sem("conv_turned"), sem("conv_rows_ready")
    s_wf, s_wfs, s_wfh, s_wfl = sem("wf_loaded"), sem("wf_scaled"), sem("wf_high"), sem("wf_low")
    s_fp, s_fa, s_fneg, s_fe = sem("f_projected"), sem("f_raw_ready"), sem("f_neg"), sem("f_exp")
    s_fl, s_ft, s_fst, s_fn, s_fnr = sem("f_log"), sem("f_sum"), sem("f_stored"), sem("f_turned"), sem("f_rows_ready")
    s_ck, s_cq = sem("f_new_loaded"), sem("f_query_ready")
    s_qsp, s_qsn, s_qss, s_qsr, s_qsc, s_qst, s_qz = (
        sem("qs_projected"), sem("qs_rows_ready"), sem("qs_squared"), sem("qs_rsqrt"), sem("qs_scaled"),
        sem("qs_turned"), sem("qs_spread"))
    b_page = [sem(f"page_loaded{s}") for s in range(RING)]
    b_used, b_qc = sem("v_page_used"), sem("q_current_ready")
    b_raw = [sem(f"b_w_loaded{s}") for s in range(2)]
    b_scaled, b_high, b_split, b_proj = sem("b_w_scaled"), sem("b_w_high"), sem("b_w_split"), sem("b_projected")
    b_dact, b_ddve = sem("proj_out_act"), sem("proj_out_dve")
    b_t0, b_t0f, b_t1, b_t1f = sem("turn0_full"), sem("turn0_free"), sem("turn1_full"), sem("turn1_free")
    b_c0, b_c0f, b_c1, b_c1f = sem("score0_full"), sem("score0_free"), sem("score1_full"), sem("score1_free")
    b_ss, b_ln, b_rr, b_normed = sem("head_squares"), sem("head_ln"), sem("head_rsqrt"), sem("head_normed")
    b_sfx = [sem(f"suffix_loaded{s}") for s in range(2)]
    b_fb, b_nbs, b_es, b_lp, b_sot = (
        sem("f_broad_loaded"), sem("sample_bias"), sem("sample_exp"), sem("sample_sum"), sem("sample_out"))
    b_nbp, b_ep, b_pn, b_po, b_sz, b_gf, b_gh, b_gl = (
        sem("prompt_bias"), sem("prompt_exp"), sem("prompt_probs"), sem("prompt_pv"), sem("silu_z_ready"),
        sem("gated"), sem("gated_h"), sem("gated_l"))
    b_kst, b_fq = sem("ks_kept"), sem("rows_f_taken")
    b_kpo, b_kso, b_vpo = sem("k_prompt_stored"), sem("k_sample_stored"), sem("v_prompt_stored")
    m_s, m_sn, m_exp, m_bias, m_p, m_t, m_ta, m_td, m_pv, m_om, m_ot, m_gs, m_gh, m_gl, m_a = (
        sem("new_scored"), sem("new_scores_ready"), sem("old_weight"), sem("new_bias_ready"), sem("new_probs"),
        sem("new_turned"), sem("new_t_act"), sem("new_t_dve"), sem("new_pv"), sem("merged"), sem("merged_turned"),
        sem("gated_s"), sem("gated_sh"), sem("gated_sl"), sem("new_aux"))
    s_hld = sem("h_loaded")
    s_out = sem("outputs_stored")

    LINKS = dict(dve_a=8, dve_b=10)

    w_in = a_w_in[0].rearrange("(k p) n -> p k n", p=P)
    wo_a = a_w_out[0].rearrange("(k p) n -> p k n", p=P)
    wkv = kv_w.rearrange("(k p) n -> p k n", p=P)
    wqz = b_w_in[0].rearrange("(k p) n -> p k n", p=P)
    wo_b = b_w_out[0].rearrange("(k p) n -> p k n", p=P)
    kpages = cache_k.rearrange("g p h d -> g p (h d)")
    vpages = cache_v.rearrange("g p h d -> g p (h d)")
    A_ORDER = (1, 2, 3, 0)

    def both(bank):
        return PS[:, bank:bank + 2, 0:HALF], PS[:, bank + 1, HALF:TAIL]

    def prompt2(ap):
        return ap.rearrange("p (a n) -> p a n", a=2)

    def gain(row):
        return GAIN[:, row:row + KT].unsqueeze(2).to_broadcast([P, KT, P])

    block = ctx.enter_context(nc.Block())

    @block.sync
    def _(sp):
        sp.dma_start(CT[:, :], table).then_inc(s_const, 16)
        sp.dma_start(X[:, 0, :], x_prompt[0, 0:P, :]).then_inc(s_x[0], 16)
        sp.dma_start(PIDX[:, :], page_table.rearrange("b (g a) -> (b g) a", a=1)).then_inc(s_idx, 16)
        for r, v in ((G_A, a_norm[0]), (G_KV, kv_norm), (G_B, b_norm[0])):
            sp.dma_start(GR[r:r + KT, :], v.rearrange("(k p) -> k p", p=P)).then_inc(s_rows, 16)
        sp.dma_start(GR[G_CONV:G_CONV + CONV_W * KT, :],
                     a_conv[0].rearrange("j (k p) -> (j k) p", p=P)).then_inc(s_rows, 16)
        for r, v in ((G_K, k_norm), (G_Q, q_norm[0])):
            for e in range(2):
                sp.dma_start(GR[r:r + 1, e * HD:(e + 1) * HD], v.unsqueeze(0)).then_inc(s_rows, 16)
        sp.dma_start(STN[:, :], state_conv[0].rearrange("b s n -> (b s) n")).then_inc(s_rows, 16)
        sp.dma_start(FBIAS[:, :], kv_fbias.unsqueeze(1)).then_inc(s_rows, 16)
        sp.dma_start(PTAB[:, :], page_table.rearrange("b g -> (b g)").unsqueeze(0)).then_inc(s_rows, 16)
        for t in range(1, QB):
            sp.dma_start(X[:, t, :], x_prompt[0, toks(t), :]).then_inc(s_x[t], 16)
        sp.dma_start(X[0:NS, QB, :], x_sample.rearrange("b q n -> (b q) n")).then_inc(s_x[QB], 16)

        def load_a(i, q):
            sp.dma_start(WR[:, q % 2, :, :], w_in[:, :, bass.ds((i + A_ORDER[q] * KT) * P, P)]).then_inc(a_raw[q % 2], 16)

        for q in range(2):
            load_a(0, q)

        def mixer(i, last):
            for q in range(4):
                if last and q >= 2:
                    continue
                sp.wait_ge(a_split, 4 * i + q + 1)
                load_a(i + q // 2, (q + 2) % 4)

        with sp.Fori(0, KT - 1) as i:
            mixer(i, False)
        mixer(KT - 1, True)

        def load_slab(w, col, n):
            sp.dma_start(WRA, w[:, :, bass.ds(col, SLAB)]).then_inc(l_raw, 16)

        sp.wait_ge(a_split, 4 * KT)
        load_slab(wo_a, 0, 0)
        with sp.Fori(1, NSLAB) as n:
            sp.wait_ge(l_split, n)
            load_slab(wo_a, n * SLAB, n)
        sp.wait_ge(s_sfx_st, 16 * NB)
        sp.wait_ge(s_st, 1)

        def load_suffix(b, c):
            src = suffix_dram[bass.ds(b, 1), :, c * 512:(c + 1) * 512].rearrange("a h n -> (a h) n")
            sp.dma_start(SFX[:, c % 2, :], src.unsqueeze(1).to_broadcast([H, NQ, 512])).then_inc(b_sfx[c % 2], 16)

        load_suffix(0, 0)
        load_suffix(0, 1)
        sp.wait_ge(a_gl, KT)
        sp.dma_start(WFR[:, :, :], wkv[:, :, 2 * D:2 * D + H]).then_inc(s_wf, 16)
        for n in range(NSLAB):
            sp.wait_ge(l_split, NSLAB + n)
            load_slab(wqz, n * SLAB, NSLAB + n)
        for t in range(NT):
            sp.wait_ge(l_evac, 5 * (NSLAB - 1) + t + 1)
            sp.dma_start(h_dram[t * P:t * P + rows(t), :], X[0:rows(t), t, :]).then_inc(s_hst, 16)
        sp.wait_ge(s_co, 1)
        sp.dma_start(conv_prompt[0, 0], CO[0:2, :]).then_inc(s_cost, 16)
        sp.dma_start(conv_sample[0].rearrange("b s n -> (b s) n"), CO[2:18, :]).then_inc(s_cost, 16)

        def load_page(b, n):
            page = sp.value_load(PTAB[0:1, bass.ds(b * NPG + n % NPG, 1)], min_val=0, max_val=n_pool - 1)
            src = (kpages if n < NPG else vpages)[bass.ds(page, 1), :, :]
            sp.dma_start(ring[:, n % RING, :], src.rearrange("a p n -> (a p) n")).then_inc(b_page[n % RING], 16)

        def load_w(i, q):
            w, col = ((wqz, 0), (wkv, 0), (wkv, D), (wqz, D))[q % 4]
            sp.dma_start(WR[:, q % 2, :, :], w[:, :, bass.ds(i * P + col, P)]).then_inc(b_raw[q % 2], 16)

        sp.wait_ge(s_rows, 16 * 11)
        sp.wait_ge(l_split, 2 * NSLAB)
        load_w(0, 0)
        load_w(0, 1)
        sp.wait_ge(s_cost, 32)
        sp.wait_ge(s_hst, 16 * NT)
        sp.wait_ge(s_xl, 2 * NT)
        for n in range(RING):
            load_page(0, n)
        sp.wait_ge(s_ft, 1)
        sp.dma_start(f_dram, FT[:, :]).then_inc(s_fst, 16)
        sp.wait_ge(s_fst, 16)
        sp.dma_start(CK[:, :], f_dram[:, SEQ:TOK].unsqueeze(1).to_broadcast([H, NQ, NS])).then_inc(s_ck, 16)
        sp.wait_ge(s_fnr, 1)
        sp.dma_start(logf_prompt[0].rearrange("(t p) h -> p t h", p=P), LFN[:, 0:QB, :]).then_inc(s_out, 16)
        sp.dma_start(logf_sample.rearrange("b q h -> (b q) h"), LFN[0:NS, QB, :]).then_inc(s_out, 16)

        def heads(i, last):
            for n in range(STREAM):
                if n == 0:
                    sp.wait_ge(b_c0f, 8 * i)
                    sp.wait_ge(b_c1f, 8 * i)
                    src = f_dram[bass.ds(2 * i, 2), 0:SEQ].unsqueeze(0).to_broadcast([P, 2, SEQ])
                    sp.dma_start(FB[:, :, :], src).then_inc(b_fb, 16)
                if n % 4 == 0 and n < NPG:
                    q = n // 4
                    if not (last and q >= 2):
                        sp.wait_ge(b_split, 4 * i + q + 1)
                        load_w(i + q // 2, q + 2)
                if n in (4, 8, 12, 16):
                    c = n // 4 + 1
                    if not (last and c >= 4):
                        sp.wait_ge(b_c1f, 8 * i + n // 4)
                        load_suffix(i + c // 4, c % 4)
                if not (last and n >= STREAM - RING):
                    sp.wait_ge(s_rows, 16 * 11)
                    if n < NPG:
                        sp.wait_ge(b_t1, 24 * i + n + 1)
                    else:
                        sp.wait_ge(b_used, NPG * i + n - NPG + 1)
                    load_page(i + (n + RING) // STREAM, (n + RING) % STREAM)

        with sp.Fori(0, NB - 1) as i:
            heads(i, False)
        heads(NB - 1, True)

        sp.wait_ge(b_used, NPG * NB)
        for t in range(NT):
            sp.dma_start(X[0:rows(t), t, :], h_dram[t * P:t * P + rows(t), :]).then_inc(s_hld, 16)
        sp.wait_ge(b_split, 4 * NB)
        load_slab(wo_b, 0, 0)
        sp.wait_ge(b_t1f, 24 * NB)
        sp.dma_start(v_sample.rearrange("b q h d -> (b q) (h d)"), VS[:, :]).then_inc(s_out, 16)
        with sp.Fori(1, NSLAB) as n:
            sp.wait_ge(l_split, n + 2 * NSLAB)
            load_slab(wo_b, n * SLAB, n)
        for t in range(NT):
            sp.wait_ge(l_evac, 5 * (2 * NSLAB - 1) + t + 1)
            if t < QB:
                sp.dma_start(y_prompt[0, toks(t), :], X[:, t, :]).then_inc(s_out, 16)
            else:
                sp.dma_start(y_sample.rearrange("b q n -> (b q) n"), X[0:NS, t, :]).then_inc(s_out, 16)
        sp.wait_ge(s_out, 16 * (2 + 1 + NT))
        sp.wait_ge(b_kpo, 16 * NB)
        sp.wait_ge(b_kso, 16 * NB)
        sp.wait_ge(b_vpo, 16 * NB)

    @block.gpsimd
    def _(pool):
        pool.wait_ge(s_idx, 16)
        pool.indirect_dma_start(
            LF[:, :, :].rearrange("p n h -> p (n h)"), None, cache_logf.rearrange("g p h -> g (p h)"),
            bass.IndirectOffsetOnAxis(ap=PIDX[:, 0:1], axis=0)).then_inc(s_lf, 16)
        pool.memset(QZ[:, :, :, :], 0.0).then_inc(s_zero, 1)

        pool.wait_ge(s_gain, 1)
        for q in range(2):
            pool.wait_ge(a_raw[q], 16)
            pool.tensor_tensor(WR[:, q, :, :], WR[:, q, :, :], gain(G_A), ALU.mult).then_inc(a_scaled, 1)

        def mixer(i, last):
            for q in range(4):
                if not (last and q >= 2):
                    pool.wait_ge(a_raw[q % 2], (2 * i + q // 2 + 2) * 16)
                    pool.tensor_tensor(WR[:, q % 2, :, :], WR[:, q % 2, :, :], gain(G_A),
                                       ALU.mult).then_inc(a_scaled, 1)
                if q == 2:
                    pool.wait_ge(a_z, i + 1)
                    pool.wait_ge(a_cv, i + 1)
                    pool.tensor_tensor(RR[:, :], RR[:, :], SZ[:, :], ALU.mult).then_inc(a_cvz, 1)

        with pool.Fori(0, KT - 1) as i:
            mixer(i, False)
        mixer(KT - 1, True)
        pool.wait_ge(s_sfx, 1)
        for b in range(NB):
            pool.dma_start(suffix_dram[b].rearrange("h (g n) -> g h n", g=NPG),
                           CS[b * NPG:(b + 1) * NPG, :, :]).then_inc(s_sfx_st, 16)
        pool.wait_ge(s_wf, 16)
        pool.tensor_tensor(WFR[:, :, :], WFR[:, :, :],
                           GAIN[:, G_KV:G_KV + KT].unsqueeze(2).to_broadcast([P, KT, H]), ALU.mult).then_inc(s_wfs, 1)
        for n in range(NSLAB):
            pool.wait_ge(l_raw, 16 * (NSLAB + n + 1))
            pool.tensor_tensor(WRA, WRA, GAIN[:, G_B:G_B + KT].unsqueeze(2).to_broadcast([P, KT, SLAB]),
                               ALU.mult).then_inc(l_scaled, 1)

        def scale_b(i, q):
            pool.wait_ge(b_raw[q % 2], (2 * i + q // 2 + 1) * 16)
            g = (G_B, G_KV, G_KV, G_B)[q % 4]
            pool.tensor_tensor(WR[:, q % 2, :, :], WR[:, q % 2, :, :], gain(g), ALU.mult).then_inc(b_scaled, 1)

        scale_b(0, 0)
        scale_b(0, 1)
        pool.wait_ge(s_qz, 8)
        pool.tensor_copy(QC[:, :, :], QZ[:, 0, :, :]).then_inc(b_qc, 1)

        def heads(i, last):
            scale_b(i, 2)
            pool.wait_ge(b_rr, 2 * i + 1)
            pool.tensor_tensor(QT[:, :], QT[:, :], RR[:, 0:SEQ], ALU.mult).then_inc(b_normed, 1)
            scale_b(i, 3)
            pool.wait_ge(b_rr, 2 * i + 2)
            pool.tensor_tensor(KN_T[:, :], KN_T[:, :], RR[:, :], ALU.mult).then_inc(b_normed, 1)
            if not last:
                scale_b(i, 4)
                scale_b(i, 5)
                pool.wait_ge(b_c1, 8 * i + 4)
                pool.tensor_copy(QC[:, :, :].rearrange("p k n -> p (k n)"),
                                 QZ[:, bass.ds(i + 1, 1), :, :].rearrange("p a k n -> p (a k n)")).then_inc(b_qc, 1)

        with pool.Fori(0, NB - 1) as i:
            heads(i, False)
        heads(NB - 1, True)

    @block.scalar
    def _(act):
        ch = Chain(act, s_ch_act)

        def norm(t, phase):
            n = NT * phase + t
            r = rows(t)
            if phase == 0:
                act.wait_ge(s_x[t], 16)
            else:
                act.wait_ge(l_evac, 5 * (NSLAB - 1) + t + 1)
            ch.link(act.activation(JUNK[0:r, :], X[0:r, t, :], ACT.Square, accum_out=TINY[0:r, 0:1]))
            ch.link(act.activation(TINY[0:r, 1:2], TINY[0:r, 0:1], ACT.Ln, bias=EPSB(r), scale=1.0 / D))
            ch.link(act.activation(TINY[0:r, 2:3], TINY[0:r, 1:2], ACT.Exp, scale=-0.5))
            if n:
                act.wait_ge(s_xt, n)
            act.activation(XS[0:r, :], X[0:r, t, :], ACT.Copy, scale=TINY[0:r, 2:3]).then_inc(s_xs, 1)

        def EPSB(r):
            return TINY[0:r, 3:4]

        def norm_high(t, phase):
            n = NT * phase + t
            b = 2 * (n % 3)
            act.wait_ge(s_xt, n + 1)
            src = PS[:, b:b + 2, :].rearrange("p a (k n) -> p (a k) n", k=4)[:, :, 0:rows(t)]
            act.activation(XH[:, :, toks(t)], src, ACT.Copy).then_inc(s_xh, 1)

        act.wait_ge(s_bf, 3)
        norm(0, 0)
        for t in range(NT):
            if t + 1 < NT:
                norm(t + 1, 0)
            norm_high(t, 0)

        def high_a(n, slot):
            act.wait_ge(a_scaled, n + 1)
            act.activation(WH[:, slot, :, :], WR[:, slot, :, :], ACT.Copy).then_inc(a_high, 1)

        for q in range(2):
            high_a(q, q)

        def mixer(i, last):
            for q in range(4):
                act.wait_ge(a_proj, 4 * i + q + 1)
                if not (last and q >= 2):
                    high_a(4 * i + q + 2, q % 2)
                pr, sa = both(2 * q)
                if q == 0:
                    act.wait_ge(a_v, i)
                    act.activation(prompt2(SQ[:, 0:SEQ]), pr, ACT.Copy)
                    act.activation(SQ[:, SEQ:TOK], sa, ACT.Copy).then_inc(a_c, 1)
                if q == 2:
                    act.wait_ge(a_cvz, i)
                    act.activation(prompt2(SZ[:, 0:SEQ]), pr, ACT.Silu)
                    act.activation(SZ[:, SEQ:TOK], sa, ACT.Silu).then_inc(a_z, 1)
                if q == 3:
                    act.wait_ge(a_g, i + 1)
                    act.activation(GH[:, bass.ds(i, 1), :].rearrange("p a n -> p (a n)"), VT[:, :],
                                   ACT.Copy).then_inc(a_gh, 1)

        with act.Fori(0, KT - 1) as i:
            mixer(i, False)
        mixer(KT - 1, True)

        def high_slab(n):
            act.activation(slab_h[n % 2], WRA, ACT.Copy).then_inc(l_high, 1)

        for n in range(NSLAB):
            act.wait_ge(l_raw, 16 * (n + 1))
            if n >= 2:
                act.wait_ge(l_tile, NT * (n - 1))
            high_slab(n)

        for t in range(NT):
            norm(t, 1)
            if t:
                norm_high(t - 1, 1)
        norm_high(NT - 1, 1)
        act.wait_ge(s_ctt, 1)
        act.activation(CO[:, :].rearrange("p (a n) -> p a n", a=2), PS[0:18, 6:8, :], ACT.Copy).then_inc(s_co, 1)
        act.wait_ge(s_wfs, 1)
        act.activation(WFH[:, :, :], WFR[:, :, :], ACT.Copy).then_inc(s_wfh, 1)
        for n in range(NSLAB):
            act.wait_ge(l_scaled, n + 1)
            if n < 2:
                act.wait_ge(l_tile, NT * (NSLAB - 1 + n))
            else:
                act.wait_ge(s_qsp, n - 1)
            high_slab(NSLAB + n)
            if n == 1:
                act.wait_ge(s_fneg, 1)
                ch.link(act.activation(FE[:, :], FN[:, :], ACT.Exp))
                act.activation(FE[:, :], FE[:, :], ACT.Ln, bias=1.0).then_inc(s_fe, 1)
        for n in range(NSLAB):
            act.wait_ge(s_qsp, n + 1)
            act.activation(QSN[:, n * SLAB:(n + 1) * SLAB], PS[0:NS, 2 + n, 0:SLAB], ACT.Copy).then_inc(s_qsn, 1)
        act.wait_ge(s_qss, 1)
        ch.link(act.activation(TINY[0:NS, 20:36], TINY[0:NS, 4:20], ACT.Ln, bias=EPSB(NS), scale=1.0 / HD))
        act.activation(TINY[0:NS, 20:36], TINY[0:NS, 20:36], ACT.Exp, scale=-0.5).then_inc(s_qsr, 1)

        def high_b(n, slot):
            act.wait_ge(b_scaled, n + 1)
            act.activation(WH[:, slot, :, :], WR[:, slot, :, :], ACT.Copy).then_inc(b_high, 1)

        high_b(0, 0)
        high_b(1, 1)

        def heads(i, last):
            t0 = [0]

            def turned0(out, src):
                act.wait_ge(b_t0, 24 * i + t0[0] + 1)
                t0[0] += 1
                return act.activation(out, src, ACT.Copy)

            def high(q):
                if not (last and q >= 2):
                    high_b(4 * i + q + 2, q % 2)

            def rsqrt(k):
                act.wait_ge(b_ss, 2 * i + k + 1)
                act.wait_ge(b_normed, 2 * i + k)
                if k == 1:
                    act.activation(RR[:, SEQ:TOK], PS[:, OS, 0:NS], ACT.Ln, bias=EPSB(P), scale=1.0 / HD)
                act.activation(RR[:, 0:SEQ], PS[:, OP, :], ACT.Ln, bias=EPSB(P), scale=1.0 / HD).then_inc(b_ln, 1)
                act.wait_ge(b_ln, 2 * i + k + 1)
                w = TOK if k else SEQ
                act.activation(RR[:, 0:w], RR[:, 0:w], ACT.Exp, scale=-0.5).then_inc(b_rr, 1)

            for k in range(NPG):
                c = (k % 2) * PAGE
                if k % 2 == 0 and k >= 2:
                    u = k // 2 - 1
                    act.wait_ge(b_c0 if u % 2 == 0 else b_c1, 8 * i + u // 2 + 1)
                turned0(KTS[:, 0:4, c:c + PAGE], PS[:, T0, :].rearrange("p (k n) -> p k n", k=4)).then_inc(b_t0f, 1)
                if k == 3:
                    act.wait_ge(b_proj, 4 * i + 1)
                    act.wait_ge(b_gl, i)
                    act.wait_ge(b_ddve, 2 * i + 1)
                    act.activation(prompt2(SQ[:, 0:SEQ]), both(D0)[0], ACT.Square).then_inc(b_dact, 1)
                    high(0)
                if k == 5:
                    rsqrt(0)
                if k == 7:
                    act.wait_ge(b_proj, 4 * i + 2)
                    pr, sa = both(D0)
                    act.wait_ge(b_ss, 2 * i + 1)
                    act.wait_ge(b_ddve, 2 * i + 2)
                    act.activation(prompt2(SQ[:, 0:SEQ]), pr, ACT.Square)
                    act.activation(SQ[:, SEQ:TOK], sa, ACT.Square).then_inc(b_dact, 1)
                    high(1)
                if k == 9:
                    rsqrt(1)
                if k == 11:
                    act.wait_ge(b_proj, 4 * i + 3)
                    pr, sa = both(D0)
                    act.activation(prompt2(VT[:, 0:SEQ]), pr, ACT.Copy)
                    act.activation(VT[:, SEQ:TOK], sa, ACT.Copy).then_inc(b_dact, 1)
                    high(2)
            act.wait_ge(b_nbs, i + 1)
            act.wait_ge(b_lp, i)
            for c in range(4):
                ins = act.activation(SS[:, c * 512:(c + 1) * 512], SS[:, c * 512:(c + 1) * 512], ACT.Exp,
                                     bias=TINY[:, 13:14], accum_out=TINY[:, 16 + c:17 + c])
                ins.then_inc(b_es, 1)
            act.wait_ge(b_kpo, 16 * i)
            act.wait_ge(b_vpo, 16 * i)
            turned0(KN[:, 0:QB, :], PS[:, T0, :].rearrange("p (k n) -> p k n", k=4)).then_inc(b_t0f, 1)
            turned0(VN[:, :, :], PS[:, T0, :].rearrange("p (k n) -> p k n", k=4)).then_inc(b_t0f, 1)
            act.wait_ge(b_proj, 4 * i + 4)
            high(3)
            for g in (0, 2):
                turned0(PTS[:, 4 * g:4 * g + 4, :], PS[:, T0, :].rearrange("p (k n) -> p k n", k=4)).then_inc(b_t0f, 1)
            cols = bass.ds(i * P, P)
            act.wait_ge(b_t0f, 24 * i + 18)
            act.wait_ge(b_t1f, 24 * i + 17)
            act.dma_start(k_prompt[0].rearrange("(t p) h d -> p t (h d)", p=P)[:, :, cols], KN[:, 0:QB, :]).then_inc(b_kpo, 16)
            act.dma_start(v_prompt[0].rearrange("(t p) h d -> p t (h d)", p=P)[:, :, cols], VN[:, :, :]).then_inc(b_vpo, 16)
            act.dma_start(k_sample.rearrange("b q h d -> (b q) (h d)")[:, cols], KN[0:NS, QB, :]).then_inc(b_kso, 16)
            for s in range(QB):
                w = (s + 1) * P
                act.wait_ge(b_nbp, 4 * i + s + 1)
                for e in range(2):
                    act.activation(PB[:, e, 0:w], PB[:, e, 0:w], ACT.Exp, bias=TINY[:, 24 + e:25 + e],
                                   accum_out=TINY[:, 28 + e:29 + e]).then_inc(b_ep, 1)
                turned0(PT[:, 0, 0:s + 1, :], PS[:, T0, 0:w].rearrange("p (k n) -> p k n", n=P)).then_inc(b_t0f, 1)
                if s == 0:
                    act.wait_ge(b_gf, i)
                    pr, sa = both(D0)
                    act.activation(prompt2(SZ[:, 0:SEQ]), pr, ACT.Silu).then_inc(b_sz, 1)
                    act.activation(SZS[:, bass.ds(i, 1), :].rearrange("p a n -> p (a n)"), sa, ACT.Silu).then_inc(b_dact, 1)
            assert t0[0] == 24
            act.wait_ge(b_used, NPG * (i + 1))
            act.activation(OPAST[:, bass.ds(i, 1), :].rearrange("p a n -> p (a n)"), PS[:, OS, 0:4 * HD],
                           ACT.Copy).then_inc(b_sot, 1)
            act.wait_ge(b_gf, i + 1)
            act.activation(GH[:, bass.ds(i, 1), 0:SEQ].rearrange("p a n -> p (a n)"), SQ[:, 0:SEQ],
                           ACT.Copy).then_inc(b_gh, 1)

        with act.Fori(0, NB - 1) as i:
            heads(i, False)
        heads(NB - 1, True)

        def high_out(n):
            act.wait_ge(l_raw, 16 * (2 * NSLAB + n + 1))
            if n >= 2:
                act.wait_ge(l_tile, NT * (NSLAB + n - 1))
            high_slab(n)

        act.wait_ge(b_proj, 4 * NB)
        act.wait_ge(m_exp, 1)
        act.activation(TINY[:, 40:48], TINY[:, 40:48], ACT.Exp).then_inc(m_a, 1)
        for b in range(NB):
            act.activation(SN[:, b, :], SN[:, b, :], ACT.Exp, bias=TINY[:, 48 + b:49 + b],
                           accum_out=TINY[:, 56 + b:57 + b]).then_inc(m_p, 1)
        act.wait_ge(m_t, 1)
        act.activation(PNT[:, 0:4, :], PS[0:NS, T0, :].rearrange("p (k n) -> p k n", k=4), ACT.Copy).then_inc(m_ta, 1)
        high_out(0)
        act.wait_ge(m_gs, 1)
        act.activation(GH[:, :, SEQ:TOK], GS[:, :, :], ACT.Copy).then_inc(m_gh, 1)
        for n in range(1, NSLAB):
            high_out(n)

    @block.vector
    def _(dve):
        ch = Chain(dve, s_ch_dve)
        dve.memset(TINY[:, 3:4], EPS).then_inc(s_bf, 1)
        dve.wait_ge(s_const, 16)
        dve.tensor_copy(IDB[:, :], ident).then_inc(s_bf, 1)
        dve.tensor_copy(CMB[:, :], CT[:, C_CM:C_CM + P]).then_inc(s_bf, 1)
        dve.wait_ge(s_gt, 1)
        dve.tensor_copy(GAIN[:, :], PS[:, 6, 0:G_ALL]).then_inc(s_gain, 1)
        dve.wait_ge(s_gain, 1)
        dve.tensor_scalar(GQ[:, :], GAIN[:, G_Q:G_Q + 1], HD ** -0.5, None, ALU.mult)
        dve.wait_ge(s_stt, 1)
        dve.tensor_copy(ST[:, :, :], PS[:, 7, 128:256].rearrange("p (k n) -> p k n", k=KT)).then_inc(s_st, 1)

        def norm_low(t, phase):
            n = NT * phase + t
            b = 2 * (n % 3)
            dve.wait_ge(s_xh, n + 1)
            src = PS[:, b:b + 2, :].rearrange("p a (k n) -> p (a k) n", k=4)[:, :, 0:rows(t)]
            dve.tensor_tensor(XL[:, :, toks(t)], src, XH[:, :, toks(t)].bitcast(F32), ALU.subtract).then_inc(s_xl, 1)

        for t in range(NT):
            norm_low(t, 0)

        def low_a(n, slot):
            dve.wait_ge(a_high, n + 1)
            dve.tensor_tensor(WL[:, slot, :, :], WR[:, slot, :, :], WH[:, slot, :, :].bitcast(F32),
                              ALU.subtract).then_inc(a_split, 1)

        for q in range(2):
            low_a(q, q)
        dve.wait_ge(s_lf, 16)
        one = CT[:, C_ONE:C_ONE + 1].to_broadcast([P, PAGE])
        for h in range(H):
            dve.tensor_tensor_scan(CS[:, h, :], one, LF[:, :, h], 0.0, ALU.mult, ALU.add).then_inc(s_cs, 1)
        dve.wait_ge(s_rtot, 1)
        dve.tensor_tensor(CS[:, :, :], PS[:, 7, 0:H].unsqueeze(2).to_broadcast([P, H, PAGE]), CS[:, :, :],
                          ALU.subtract).then_inc(s_sfx, 1)
        ch.link(dve.memset(EXT[:, 0:2], 0.0))
        done = ch.n

        def mixer(i, last):
            ch.loop(i, LINKS["dve_a"], done)
            for q in range(4):
                if not (last and q >= 2):
                    low_a(4 * i + q + 2, q % 2)
                pr, sa = both(2 * q)
                if q == 1:
                    st = ST[:, bass.ds(i, 1), :].rearrange("p a (b s) -> p (a b) s", b=NB)
                    dve.tensor_copy(EXTS[:, :, 0:2], st)
                    dve.wait_ge(a_c, i + 1)
                    dve.wait_ge(a_proj, 4 * i + 2)
                    dve.tensor_tensor(prompt2(EXT[:, 2:SEQ + 2]), pr, prompt2(SQ[:, 0:SEQ]), ALU.mult)
                    dve.tensor_tensor(EXTS[:, :, 2:NQ + 2], sa.rearrange("p (b q) -> p b q", b=NB),
                                      SQ[:, SEQ:TOK].rearrange("p (b q) -> p b q", b=NB), ALU.mult).then_inc(a_v, 1)
                    dve.wait_ge(a_v, i + 1)
                    dve.wait_ge(a_g, i)
                    ch.link(dve.tensor_copy(CST[:, bass.ds(i, 1), 0:2].rearrange("p a n -> p (a n)"), EXT[:, SEQ:SEQ + 2]))
                    ch.link(dve.tensor_copy(
                        CST[:, bass.ds(i, 1), 2:18].rearrange("p a (b s) -> p (a b) s", b=NB), EXTS[:, :, NQ:NQ + 2]))
                    cvp = RR[:, 0:SEQ]
                    cvs = RR[:, SEQ:TOK].rearrange("p (b q) -> p b q", b=NB)
                    for j in range(CONV_W):
                        w = GAIN[:, bass.ds(G_CONV + j * KT + i, 1)]
                        if j == 0:
                            ch.link(dve.tensor_scalar(cvp, EXT[:, 0:SEQ], w, None, ALU.mult))
                            ch.link(dve.tensor_scalar(cvs, EXTS[:, :, 0:NQ], w, None, ALU.mult))
                        else:
                            ch.link(dve.scalar_tensor_tensor(cvp, EXT[:, j:j + SEQ], w, cvp, ALU.mult, ALU.add))
                            ins = dve.scalar_tensor_tensor(cvs, EXTS[:, :, j:j + NQ], w, cvs, ALU.mult, ALU.add)
                            if j == 1:
                                ch.link(ins)
                            else:
                                ins.then_inc(a_cv, 1)
                if q == 3:
                    dve.wait_ge(a_proj, 4 * i + 4)
                    dve.wait_ge(a_cvz, i + 1)
                    ch.link(dve.tensor_tensor(prompt2(VT[:, 0:SEQ]), pr, prompt2(RR[:, 0:SEQ]), ALU.mult))
                    dve.tensor_tensor(VT[:, SEQ:TOK], sa, RR[:, SEQ:TOK], ALU.mult).then_inc(a_g, 1)
                    dve.wait_ge(a_gh, i + 1)
                    gl = GL[:, bass.ds(i, 1), :].rearrange("p a n -> p (a n)")
                    gh = GH[:, bass.ds(i, 1), :].rearrange("p a n -> p (a n)")
                    dve.tensor_tensor(gl, VT[:, :], gh.bitcast(F32), ALU.subtract).then_inc(a_gl, 1)
            ch.end()

        with dve.Fori(0, KT - 1) as i:
            mixer(i, False)
        mixer(KT - 1, True)
        ch.base, ch.n = 0, done + LINKS["dve_a"] * KT

        def low_slab(n, s):
            dve.wait_ge(l_high, n + 1)
            dve.tensor_tensor(slab_l[s], WRA, slab_h[s].bitcast(F32), ALU.subtract).then_inc(l_split, 1)

        def out_tile(n, g, s, t):
            dve.wait_ge(l_tile, n + 1)
            r = rows(t)
            x = X[0:r, t, bass.ds(g * SLAB, SLAB)]
            dve.tensor_tensor(x, PS[0:r, (5 * s + t) % 8, 0:SLAB], x, ALU.add).then_inc(l_evac, 1)

        low_slab(0, 0)
        low_slab(1, 1)
        with dve.Fori(0, NSLAB // 2 - 1) as j:
            for s in range(2):
                for t in range(NT):
                    out_tile(5 * s + t + 10 * j, 2 * j + s, s, t)
                low_slab(2 * j + s + 2, s)
        for s in range(2):
            for t in range(NT):
                out_tile(5 * (NSLAB - 2 + s) + t, NSLAB - 2 + s, s, t)

        for t in range(NT):
            norm_low(t, 1)
        dve.wait_ge(s_wfh, 1)
        dve.tensor_tensor(WFL[:, :, :], WFR[:, :, :], WFH[:, :, :].bitcast(F32), ALU.subtract).then_inc(s_wfl, 1)
        low_slab(NSLAB, 0)
        low_slab(NSLAB + 1, 1)
        dve.wait_ge(s_fp, 1)
        ch.link(dve.tensor_scalar(prompt2(FA[:, 0:SEQ]), PS[0:H, 0:2, 0:HALF], FBIAS[:, 0:1], None, ALU.add))
        ch.link(dve.tensor_scalar(FA[:, SEQ:TOK], PS[0:H, 1, HALF:TAIL], FBIAS[:, 0:1], None, ALU.add))
        ch.link(dve.tensor_scalar(FN[:, :], FA[:, :], -1.0, None, ALU.mult))
        dve.tensor_tensor(FN[:, :], FN[:, :], FA[:, :], ALU.min).then_inc(s_fneg, 1)
        low_slab(NSLAB + 2, 0)
        dve.wait_ge(s_fe, 1)
        dve.scalar_tensor_tensor(FL[:, :], FA[:, :], 0.0, FE[:, :], ALU.min, ALU.subtract).then_inc(s_fl, 1)
        dve.wait_ge(s_fl, 1)
        dve.wait_ge(s_gt, 1)
        ch.link(dve.tensor_tensor_scan(FT[:, 0:SEQ], CT[0:H, C_ONE:C_ONE + 1].to_broadcast([H, SEQ]), FL[:, 0:SEQ],
                                       0.0, ALU.mult, ALU.add))
        dve.tensor_tensor_scan(FT[:, SEQ:TOK], CT[0:H, C_RST:C_RST + NS], FL[:, SEQ:TOK], 0.0,
                               ALU.mult, ALU.add).then_inc(s_ft, 1)
        low_slab(NSLAB + 3, 1)
        dve.wait_ge(s_fn, 1)
        ch.link(dve.tensor_copy(LFN[:, 0:QB, :], PS[:, 7, 0:QB * H].rearrange("p (t h) -> p t h", h=H)))
        ch.link(dve.tensor_copy(LFN[0:NS, QB, :], PS[0:NS, 7, QB * H:NT * H]))
        dve.tensor_copy(FQN[:, :, :], PS[:, 7, 128:128 + QB * H].rearrange("p (t h) -> p t h", h=H)).then_inc(s_fnr, 1)
        dve.wait_ge(s_qsn, NSLAB)
        dve.wait_ge(s_co, 1)
        ch.link(dve.tensor_tensor(QSS[:, :], QSN[:, :], QSN[:, :], ALU.mult))
        dve.tensor_reduce(TINY[0:NS, 4:20], QSS[:, :].rearrange("p (h d) -> p h d", h=H), AX, ALU.add).then_inc(s_qss, 1)
        dve.wait_ge(s_qsr, 1)
        q3 = QSN[:, :].rearrange("p (h d) -> p h d", h=H)
        dve.tensor_tensor(q3, q3, TINY[0:NS, 20:36].unsqueeze(2).to_broadcast([NS, H, HD]), ALU.mult).then_inc(s_qsc, 1)
        dve.wait_ge(s_qst, 1)
        dve.wait_ge(s_zero, 1)
        for pp in range(2):
            for e in range(2):
                for b4 in range(2):
                    pr = slice(64 * e, 64 * e + 64)
                    src = PS[pr, 6, :].rearrange("p (j a b q) -> p a b j q", j=4, a=2, b=NB)[:, pp, 4 * b4:4 * b4 + 4]
                    out = QZ[:, :, :, :].rearrange("p b (j a) c -> p a b j c", a=2)[
                        pr, pp, 4 * b4:4 * b4 + 4, :, 16 * pp + 8 * e:16 * pp + 8 * e + NQ]
                    dve.tensor_scalar(out, src, GQ[pr, 0:1], None, ALU.mult).then_inc(s_qz, 1)
        dve.wait_ge(s_ck, 16)
        qd = CT[:, C_QD:C_QD + NS]
        ch.link(dve.tensor_tensor(KS[:, 0, :], CK[:, :], qd, ALU.mult))
        ch.link(dve.tensor_reduce(CQ[:, :], KS[:, 0, :].rearrange("p (b q) -> p b q", b=NB), AX, ALU.add))

        def low_b(n, slot):
            dve.wait_ge(b_high, n + 1)
            dve.tensor_tensor(WL[:, slot, :, :], WR[:, slot, :, :], WH[:, slot, :, :].bitcast(F32),
                              ALU.subtract).then_inc(b_split, 1)

        low_b(0, 0)
        low_b(1, 1)
        done_b = ch.n

        def heads(i, last):
            ch.loop(i, LINKS["dve_b"], done_b)
            t1 = [0]

            def turned1(out, src):
                dve.wait_ge(b_t1, 24 * i + t1[0] + 1)
                t1[0] += 1
                return dve.tensor_copy(out, src)

            def add_suffix(u):
                free, bank = ((b_c0f, C0), (b_c1f, C1))[u % 2]
                dve.tensor_tensor_reduce(
                    SS[:, u * 256:(u + 1) * 256], PS[:, bank, 0:256],
                    SFX[:, (u // 2) % 2, (u % 2) * 256:(u % 2) * 256 + 256],
                    1.0, NEG, ALU.add, ALU.max, TINY[:, 4 + u:5 + u]).then_inc(free, 1)

            def low(q):
                if not (last and q >= 2):
                    low_b(4 * i + q + 2, q % 2)

            for k in range(NPG):
                c = (k % 2) * PAGE
                if k % 2 == 0 and k >= 2:
                    u = k // 2 - 1
                    if u % 2 == 0:
                        dve.wait_ge(b_sfx[(u // 2) % 2], (2 * i + u // 4 + 1) * 16)
                    dve.wait_ge(b_c0 if u % 2 == 0 else b_c1, 8 * i + u // 2 + 1)
                turned1(KTS[:, 4:8, c:c + PAGE], PS[:, T1, :].rearrange("p (k n) -> p k n", k=4)).then_inc(b_t1f, 1)
                if k % 2 == 0 and k >= 2:
                    add_suffix(k // 2 - 1)
                if k == 3:
                    dve.wait_ge(b_proj, 4 * i + 1)
                    dve.tensor_scalar(prompt2(QT[:, :]), both(D0)[0], GQ[:, 0:1], None, ALU.mult).then_inc(b_ddve, 1)
                if k == 4:
                    low(0)
                if k == 7:
                    dve.wait_ge(b_proj, 4 * i + 2)
                    pr, sa = both(D0)
                    gk = GAIN[:, G_K:G_K + 1]
                    dve.tensor_scalar(prompt2(KN_T[:, 0:SEQ]), pr, gk, None, ALU.mult)
                    dve.tensor_scalar(KN_T[:, SEQ:TOK], sa, gk, None, ALU.mult).then_inc(b_ddve, 1)
                if k == 8:
                    low(1)
                if k == 12:
                    low(2)
                    dve.wait_ge(b_normed, 2 * i + 2)
                    dve.tensor_copy(KS[:, bass.ds(i, 1), :].rearrange("p a n -> p (a n)"), KN_T[:, SEQ:TOK]).then_inc(b_kst, 1)
            dve.wait_ge(s_fnr, 1)
            dve.wait_ge(b_c1, 8 * i + 4)
            add_suffix(NPG // 2 - 1)
            dve.wait_ge(b_c0f, 8 * i + 4)
            dve.wait_ge(b_c1f, 8 * i + 4)
            cq = CQ[:, bass.ds(i, 1)]
            ms = MS[:, bass.ds(i, 1)]
            ch.link(dve.tensor_reduce(TINY[:, 12:13], TINY[:, 4:12], AX, ALU.max))
            ch.link(dve.tensor_tensor(ms, TINY[:, 12:13], cq, ALU.add))
            dve.tensor_tensor(TINY[:, 13:14], cq, ms, ALU.subtract).then_inc(b_nbs, 1)
            dve.wait_ge(b_kso, 16 * i)
            turned1(KN[0:NS, QB, :], PS[0:NS, T1, 0:P]).then_inc(b_t1f, 1)
            turned1(VS[:, bass.ds(i * P, P)], PS[0:NS, T1, 0:P]).then_inc(b_t1f, 1)
            low(3)
            for g in (1, 3):
                turned1(PTS[:, 4 * g:4 * g + 4, :], PS[:, T1, :].rearrange("p (k n) -> p k n", k=4)).then_inc(b_t1f, 1)
            dve.wait_ge(b_es, 4 * i + 4)
            dve.tensor_reduce(LS[:, bass.ds(i, 1)], TINY[:, 16:20], AX, ALU.add).then_inc(b_lp, 1)
            dve.wait_ge(b_fb, 16 * (i + 1))
            for s in range(QB):
                w = (s + 1) * P
                if s:
                    dve.wait_ge(b_t0, 24 * i + 20 + s)
                    dve.wait_ge(b_t1, 24 * i + 20 + s)
                dve.wait_ge(b_c0, 8 * i + 4 + s + 1)
                dve.wait_ge(b_c1, 8 * i + 4 + s + 1)
                dve.tensor_copy(TINY[:, 32:34], FQN[:, s, bass.ds(2 * i, 2)]).then_inc(b_fq, 1)
                for e, (free, bank) in enumerate(((b_c0f, C0), (b_c1f, C1))):
                    dve.tensor_tensor_reduce(PB[:, e, 0:w], PS[:, bank, 0:w], FB[:, e, 0:w], 1.0, NEG,
                                             ALU.subtract, ALU.max, TINY[:, 20 + e:21 + e]).then_inc(free, 1)
                dve.wait_ge(b_fq, 4 * i + s + 1)
                dve.wait_ge(b_c0f, 8 * i + 4 + s + 1)
                dve.wait_ge(b_c1f, 8 * i + 4 + s + 1)
                fq = TINY[:, 32:34]
                ch.link(dve.tensor_tensor(TINY[:, 22:24], TINY[:, 20:22], fq, ALU.add))
                dve.tensor_tensor(TINY[:, 24:26], fq, TINY[:, 22:24], ALU.subtract).then_inc(b_nbp, 1)
                dve.wait_ge(b_ep, 8 * i + 2 * s + 2)
                ch.link(dve.reciprocal(TINY[:, 30:32], TINY[:, 28:30]))
                for e in range(2):
                    dve.tensor_scalar(PB[:, e, 0:w], PB[:, e, 0:w], TINY[:, 30 + e:31 + e], None,
                                      ALU.mult).then_inc(b_pn, 1)
                turned1(PT[:, 1, 0:s + 1, :], PS[:, T1, 0:w].rearrange("p (k n) -> p k n", n=P)).then_inc(b_t1f, 1)
            assert t1[0] == 24
            dve.wait_ge(b_po, i + 1)
            dve.wait_ge(b_sz, i + 1)
            dve.tensor_tensor(SQ[:, 0:SEQ], PS[:, OP, :], SZ[:, 0:SEQ], ALU.mult).then_inc(b_gf, 1)
            dve.wait_ge(b_gh, i + 1)
            gl = GL[:, bass.ds(i, 1), 0:SEQ].rearrange("p a n -> p (a n)")
            gh = GH[:, bass.ds(i, 1), 0:SEQ].rearrange("p a n -> p (a n)")
            dve.tensor_tensor(gl, SQ[:, 0:SEQ], gh.bitcast(F32), ALU.subtract).then_inc(b_gl, 1)
            ch.end()

        with dve.Fori(0, NB - 1) as i:
            heads(i, False)
        heads(NB - 1, True)
        ch.base, ch.n = 0, done_b + LINKS["dve_b"] * NB

        nm = CT[:, C_NM:C_NM + NB * NS].rearrange("p (b n) -> p b n", b=NB)
        ch.link(dve.tensor_tensor(NBI[:, :, :], nm, CK[:, :].unsqueeze(1).to_broadcast([P, NB, NS]), ALU.subtract))
        dve.wait_ge(m_s, 1)
        ch.link(dve.tensor_tensor(SN[:, :, :], PS[:, C0, :].rearrange("p (b n) -> p b n", b=NB), NBI[:, :, :], ALU.add))
        tn = TINY
        ch.link(dve.tensor_reduce(tn[:, 4:12], SN[:, :, :], AX, ALU.max))
        ch.link(dve.tensor_tensor(tn[:, 4:12], tn[:, 4:12], CQ[:, :], ALU.add))
        ch.link(dve.tensor_tensor(tn[:, 4:12], tn[:, 4:12], MS[:, :], ALU.max))
        ch.link(dve.tensor_tensor(tn[:, 40:48], MS[:, :], tn[:, 4:12], ALU.subtract))
        dve.tensor_tensor(tn[:, 48:56], CQ[:, :], tn[:, 4:12], ALU.subtract).then_inc(m_exp, 1)
        dve.wait_ge(m_a, 1)
        ch.link(dve.tensor_tensor(LS[:, :], LS[:, :], tn[:, 40:48], ALU.mult))
        dve.wait_ge(m_p, NB)
        ch.link(dve.tensor_tensor(LS[:, :], LS[:, :], tn[:, 56:64], ALU.add))
        ch.link(dve.reciprocal(LS[:, :], LS[:, :]))
        dve.wait_ge(m_t, 2)
        dve.tensor_copy(PNT[:, 4:8, :], PS[0:NS, T1, :].rearrange("p (k n) -> p k n", k=4)).then_inc(m_td, 1)
        low_slab(2 * NSLAB, 0)
        for b in range(NB):
            dve.wait_ge(m_pv, b // 2 + 1)
            ch.link(dve.scalar_tensor_tensor(OM[:, b, :], OPAST[:, b, :], tn[:, 40 + b:41 + b],
                                             PS[:, C0 + b // 2, (b % 2) * 256:(b % 2) * 256 + 256], ALU.mult, ALU.add))
            dve.tensor_scalar(OM[:, b, :], OM[:, b, :], LS[:, b:b + 1], None, ALU.mult).then_inc(m_om, 1)
        for b in range(0, NB, 2):
            dve.wait_ge(m_ot, b // 2 + 1)
            for ii2 in range(2):
                for e in range(2):
                    pr = slice(64 * e, 64 * e + 64)
                    src = PS[pr, (D0, D1, T0, T1)[b // 2], :].rearrange(
                        "p (b a j c) -> p a b j c", b=2, a=2, j=4)[:, ii2, :, :, 8 * (2 * ii2 + e):8 * (2 * ii2 + e) + NQ]
                    sel = lambda z: z[pr, :, b * NQ:(b + 2) * NQ].rearrange(
                        "p (j a) (b q) -> p a b j q", a=2, b=2)[:, ii2]
                    ins = dve.tensor_tensor(sel(GS), src, sel(SZS), ALU.mult)
        ins.then_inc(m_gs, 1)
        dve.wait_ge(m_gh, 1)
        dve.tensor_tensor(GL[:, :, SEQ:TOK], GS[:, :, :], GH[:, :, SEQ:TOK].bitcast(F32), ALU.subtract).then_inc(m_gl, 1)
        low_slab(2 * NSLAB + 1, 1)
        dve.wait_ge(s_hld, 16 * NT)
        base = 5 * NSLAB
        with dve.Fori(0, NSLAB // 2 - 1) as j:
            for s in range(2):
                for t in range(NT):
                    out_tile(5 * s + t + 10 * j + base, 2 * j + s, s, t)
                low_slab(2 * j + s + 2 + 2 * NSLAB, s)
        for s in range(2):
            for t in range(NT):
                out_tile(5 * (NSLAB - 2 + s) + t + base, NSLAB - 2 + s, s, t)

    @block.tensor
    def _(pe):
        def turn(out, src, r=P):
            return pe.transpose(out, src, CT[0:r, C_ID:C_ID + r])

        pe.wait_ge(s_const, 16)
        pe.wait_ge(s_rows, 16 * 11)
        turn(PS[:, 6, 0:G_ALL], GR[:, :], G_ALL).then_inc(s_gt, 1)
        for k in range(KT):
            mm = turn(PS[:, 7, 128 + 16 * k:144 + 16 * k], STN[:, k * P:(k + 1) * P], 2 * NB)
        mm.then_inc(s_stt, 1)

        def norm_turn(t, phase):
            n = NT * phase + t
            b = 2 * (n % 3)
            pe.wait_ge(s_xs, n + 1)
            if n >= 3:
                pe.wait_ge(s_xl, n - 2)
            for k in range(KT):
                mm = turn(PS[:, b + k // 4, (k % 4) * P:(k % 4) * P + rows(t)], XS[0:rows(t), k * P:(k + 1) * P], rows(t))
            mm.then_inc(s_xt, 1)

        for t in range(NT):
            norm_turn(t, 0)
        pe.wait_ge(s_cs, H)
        pe.wait_ge(s_st, 1)
        pe.matmul(PS[:, 7, 0:H], CT[:, C_TRI:C_TRI + P], CS[:, :, PAGE - 1], start=True, stop=True).then_inc(s_rtot, 1)

        def piece(slot, k, bank, x_h, x_l, cols=(slice(0, HALF), slice(HALF, TOK))):
            for w, x in ((WH, x_h), (WH, x_l), (WL, x_h)):
                for h, c in enumerate(cols):
                    mm = pe.matmul(PS[:, bank + h, 0:c.stop - c.start], w[:, slot, k, :], x[:, k, c],
                                   start=(k == 0 and w is WH and x is x_h), stop=(k == KT - 1 and w is WL))
            return mm

        pe.wait_ge(s_xl, NT)
        pe.wait_ge(s_sfx, 1)

        def mixer(i):
            for q in range(4):
                pe.wait_ge(a_split, 4 * i + q + 1)
                pe.wait_ge((a_c, a_v, a_z, a_g)[q], i)
                for k in range(KT):
                    mm = piece(q % 2, k, 2 * q, XH, XL)
                mm.then_inc(a_proj, 1)

        with pe.Fori(0, KT) as i:
            mixer(i)
        pe.wait_ge(a_gl, KT)

        def out_slab(g, s, n, t_range=range(NT)):
            pe.wait_ge(l_split, g + 1)
            for t in t_range:
                r = rows(t)
                pe.wait_ge(l_evac, n + t - 1) if not isinstance(n, int) or n + t > 1 else None
                for k in range(KT):
                    for w, x in ((slab_h[s], GH), (slab_h[s], GL), (slab_l[s], GH)):
                        mm = pe.matmul(PS[0:r, (5 * s + t) % 8, 0:SLAB], x[:, k, toks(t)], w[:, k, :],
                                       start=(k == 0 and w is slab_h[s] and x is GH),
                                       stop=(k == KT - 1 and w is slab_l[s]))
                mm.then_inc(l_tile, 1)

        out_slab(0, 0, 0)
        out_slab(1, 1, 5)
        with pe.Fori(1, NSLAB // 2) as j:
            for s in range(2):
                out_slab(2 * j + s, s, 10 * j + 5 * s)
        pe.wait_ge(l_evac, 5 * NSLAB)
        for t in range(NT):
            norm_turn(t, 1)
        pe.wait_ge(s_xl, 2 * NT)
        for k in range(KT):
            mm = turn(PS[0:18, 6 + k // 4, (k % 4) * P:(k % 4 + 1) * P], CST[:, k, :])
        mm.then_inc(s_ctt, 1)
        pe.wait_ge(s_wfl, 1)
        for k in range(KT):
            for w, x in ((WFH, XH), (WFH, XL), (WFL, XH)):
                for h, c in enumerate((slice(0, HALF), slice(HALF, TOK))):
                    mm = pe.matmul(PS[0:H, h, 0:c.stop - c.start], w[:, k, :], x[:, k, c],
                                   start=(k == 0 and w is WFH and x is XH), stop=(k == KT - 1 and w is WFL))
        mm.then_inc(s_fp, 1)
        for n in range(NSLAB):
            pe.wait_ge(l_split, NSLAB + n + 1)
            for k in range(KT):
                for w, x in ((slab_h[n % 2], XH), (slab_h[n % 2], XL), (slab_l[n % 2], XH)):
                    mm = pe.matmul(PS[0:NS, 2 + n, 0:SLAB], x[:, k, SEQ:TOK], w[:, k, :],
                                   start=(k == 0 and w is slab_h[n % 2] and x is XH),
                                   stop=(k == KT - 1 and w is slab_l[n % 2]))
            mm.then_inc(s_qsp, 1)
        pe.wait_ge(s_ft, 1)
        pe.wait_ge(s_co, 1)
        for t in range(NT):
            turn(PS[0:rows(t), 7, t * H:(t + 1) * H], FL[:, toks(t)], H)
        for t in range(QB):
            mm = turn(PS[:, 7, 128 + t * H:128 + (t + 1) * H], FT[:, toks(t)], H)
        mm.then_inc(s_fn, 1)
        pe.wait_ge(s_qsc, 1)
        for k in range(KT):
            mm = turn(PS[:, 6, k * NS:(k + 1) * NS], QSN[:, k * P:(k + 1) * P], NS)
        mm.then_inc(s_qst, 1)

        pe.wait_ge(s_qz, 8)
        pe.wait_ge(s_fnr, 1)

        def heads(i):
            t0, t1 = [0], [0]

            def free0():
                pe.wait_ge(b_t0f, 24 * i + t0[0])
                t0[0] += 1

            def free1():
                pe.wait_ge(b_t1f, 24 * i + t1[0])
                t1[0] += 1

            def project(q, ks):
                if ks[0] == 0:
                    pe.wait_ge(b_split, 4 * i + q + 1)
                    pe.wait_ge(b_dact, 4 * i + q)
                    if q in (1, 2):
                        pe.wait_ge(b_ddve, 2 * i + q)
                for k in ks:
                    cols = (slice(0, HALF), slice(HALF, TOK if q else SEQ))
                    mm = piece(q % 2, k, D0, XH, XL, cols)
                if ks[-1] == KT - 1:
                    mm.then_inc(b_proj, 1)

            for k in range(NPG):
                pe.wait_ge(b_page[k % RING], (4 * i + k // RING + 1) * 16)
                page = ring[:, k % RING, :]
                free0()
                for p in range(4):
                    mm = turn(PS[:, T0, p * P:(p + 1) * P], page[:, p * P:(p + 1) * P])
                mm.then_inc(b_t0, 1)
                free1()
                for p in range(4):
                    mm = turn(PS[:, T1, p * P:(p + 1) * P], page[:, (4 + p) * P:(5 + p) * P])
                mm.then_inc(b_t1, 1)
                if k in (5, 9):
                    pe.wait_ge(b_dact, 4 * i + k // 4)
                    if k == 5:
                        pe.wait_ge(b_gf, i)
                        pe.wait_ge(b_sot, i)
                    else:
                        pe.wait_ge(b_ln, 2 * i + 1)
                        pe.matmul(PS[:, OS, 0:NS], CT[:, C_ONESB:C_ONESB + P], SQ[:, SEQ:TOK], start=True, stop=True)
                    pe.matmul(PS[:, OP, :], CT[:, C_ONESB:C_ONESB + P], SQ[:, 0:SEQ], start=True, stop=True).then_inc(b_ss, 1)
                if k < 12:
                    project(k // 4, [2 * (k % 4), 2 * (k % 4) + 1])
                else:
                    project(3, [k - 12])
                if k % 2:
                    u = k // 2
                    full, free, bank = ((b_c0, b_c0f, C0), (b_c1, b_c1f, C1))[u % 2]
                    if k == 1:
                        pe.wait_ge(b_qc, i + 1)
                    pe.wait_ge(free, 8 * i + u // 2)
                    pe.wait_ge(b_t0f, 24 * i + k + 1)
                    pe.wait_ge(b_t1f, 24 * i + k + 1)
                    for pp in range(2):
                        for j in range(4):
                            mm = pe.matmul(PS[32 * j:32 * j + 32, bank, 0:256], QC[:, 2 * j + pp, :], KTS[:, 2 * j + pp, :],
                                           start=(pp == 0), stop=(pp == 1), tile_position=(0, 32 * j))
                    mm.then_inc(full, 1)
            project(3, [4, 5, 6, 7])
            pe.wait_ge(b_normed, 2 * i + 2)
            for src in (KN_T, VT):
                free0()
                free1()
                for t in range(QB):
                    mm = turn(PS[:, T0, t * P:(t + 1) * P], src[:, toks(t)])
                mm.then_inc(b_t0, 1)
                turn(PS[0:NS, T1, 0:P], src[:, SEQ:TOK]).then_inc(b_t1, 1)
            for g in range(4):
                pe.wait_ge(b_es, 4 * i + g + 1)
                (free0, free1)[g % 2]()
                for p in range(4):
                    c = (4 * g + p) * P
                    mm = turn(PS[:, T0 + g % 2, p * P:(p + 1) * P], SS[:, c:c + P])
                mm.then_inc((b_t0, b_t1)[g % 2], 1)
            for k in range(NPG):
                s, phase = divmod(k, 4)
                w = (s + 1) * P
                if phase == 0:
                    for e, (full, free, bank) in enumerate(((b_c0, b_c0f, C0), (b_c1, b_c1f, C1))):
                        pe.wait_ge(free, 8 * i + 4 + s)
                        pr = slice(64 * e, 64 * e + 64)
                        if s:
                            pe.matmul(PS[:, bank, 0:w - P], QT[pr, toks(s)], KN_T[pr, 0:w - P], start=True, stop=True)
                        pe.matmul(PS[:, bank, w - P:w], QT[pr, toks(s)], KN_T[pr, toks(s)], start=True, stop=False)
                    for e, (full, free, bank) in enumerate(((b_c0, b_c0f, C0), (b_c1, b_c1f, C1))):
                        pe.matmul(PS[:, bank, w - P:w], IDB[:, :], CMB[:, :], start=False, stop=True).then_inc(full, 1)
                if phase == 2:
                    for e in range(2):
                        pe.wait_ge(b_pn, 8 * i + 2 * s + e + 1)
                        (free0, free1)[e]()
                        for kb in range(s + 1):
                            mm = turn(PS[:, T0 + e, kb * P:(kb + 1) * P], PB[:, e, kb * P:(kb + 1) * P])
                        mm.then_inc((b_t0, b_t1)[e], 1)
                if phase == 3:
                    pe.wait_ge(b_t0f, 24 * i + 21 + s)
                    pe.wait_ge(b_t1f, 24 * i + 21 + s)
                    if s == 0:
                        pe.wait_ge(b_ln, 2 * i + 2)
                    for kb in range(s + 1):
                        for e in range(2):
                            mm = pe.matmul(PS[64 * e:64 * e + 64, OP, toks(s)], VN[:, kb, 64 * e:64 * e + 64],
                                           PT[:, e, kb, :], start=(kb == 0), stop=(kb == s))
                    if s == QB - 1:
                        mm.then_inc(b_po, 1)
                n = NPG + k
                pe.wait_ge(b_page[n % RING], (4 * i + n // RING + 1) * 16)
                if k == 0:
                    pe.wait_ge(b_ln, 2 * i + 2)
                if k % 4 == 0:
                    g = k // 4
                    pe.wait_ge((b_t0f, b_t1f)[g % 2], 24 * i + 19 + g // 2)
                for j in range(4):
                    mm = pe.matmul(PS[32 * j:32 * j + 32, OS, 0:4 * HD], PTS[:, k, 32 * j:32 * j + 32],
                                   ring[:, n % RING, 4 * HD * j:4 * HD * (j + 1)],
                                   start=(k == 0), stop=(k == NPG - 1), tile_position=(0, 32 * j))
                mm.then_inc(b_used, 1)
            assert t0[0] == t1[0] == 24

        with pe.Fori(0, NB) as i:
            heads(i)

        pe.wait_ge(b_kst, NB)
        pe.wait_ge(b_c0f, 8 * NB)
        pe.wait_ge(b_c1f, 8 * NB)
        pe.wait_ge(b_gf, NB)
        pe.wait_ge(b_dact, 4 * NB)
        for b in range(NB):
            for pp in range(2):
                for j in range(4):
                    mm = pe.matmul(PS[32 * j:32 * j + 32, C0, b * NS:(b + 1) * NS], QZ[:, b, 2 * j + pp, :],
                                   KS[:, 2 * j + pp, :], start=(pp == 0), stop=(pp == 1), tile_position=(0, 32 * j))
        mm.then_inc(m_s, 1)
        for b in range(NB):
            pe.wait_ge(m_p, b + 1)
            mm = turn(PS[0:NS, T0 + b // 4, (b % 4) * P:(b % 4 + 1) * P], SN[:, b, :])
            if b % 4 == 3:
                mm.then_inc(m_t, 1)
        pe.wait_ge(m_ta, 1)
        pe.wait_ge(m_td, 1)
        pe.wait_ge(b_sot, NB)
        for b in range(NB):
            for j in range(4):
                mm = pe.matmul(PS[32 * j:32 * j + 32, C0 + b // 2, (b % 2) * 256:(b % 2) * 256 + 256],
                               PNT[:, b, 32 * j:32 * j + 32], VS[:, 4 * HD * j:4 * HD * (j + 1)],
                               start=True, stop=True, tile_position=(0, 32 * j))
            if b % 2:
                mm.then_inc(m_pv, 1)
        for b in range(NB):
            pe.wait_ge(m_om, b + 1)
            for a in range(2):
                mm = turn(PS[:, (D0, D1, T0, T1)[b // 2], (2 * (b % 2) + a) * P:(2 * (b % 2) + a + 1) * P],
                          OM[:, b, a * P:(a + 1) * P])
            if b % 2:
                mm.then_inc(m_ot, 1)
        pe.wait_ge(m_gl, 1)
        with pe.Fori(0, NSLAB // 2) as j:
            for s in range(2):
                out_slab(2 * j + s + 2 * NSLAB, s, 10 * j + 5 * s + 5 * NSLAB)


_INS = ['x_prompt', 'x_sample', 'state_conv', 'cache_k', 'cache_v', 'cache_logf', 'page_table',
        'a_norm', 'a_w_in', 'a_conv', 'a_w_out', 'kv_norm', 'kv_w', 'kv_fbias', 'k_norm',
        'b_norm', 'b_w_in', 'q_norm', 'b_w_out']
_OUTS = [('y_prompt', (1, SEQ, D)), ('y_sample', (NB, NQ, D)), ('conv_prompt', (1, 1, CONV_W - 1, D)),
         ('conv_sample', (1, NB, CONV_W - 1, D)), ('k_prompt', (1, SEQ, H, HD)), ('v_prompt', (1, SEQ, H, HD)),
         ('logf_prompt', (1, SEQ, H)), ('k_sample', (NB, NQ, H, HD)), ('v_sample', (NB, NQ, H, HD)),
         ('logf_sample', (NB, NQ, H))]


def constants():
    import numpy as np

    c = np.zeros((P, C_ALL), np.float32)
    p = np.arange(P)
    c[:, C_ID:C_ID + P] = np.eye(P)
    c[:, C_ONESB:C_ONESB + P] = p[:, None] // HD == p[None] // HD
    same = p[:, None] // NPG == p[None] // NPG
    c[:, C_TRI:C_TRI + P] = same & (p[:, None] >= p[None])
    c[:, C_CM:C_CM + P] = np.where(p[None] <= p[:, None], 0.0, NEG)
    key = np.arange(NS)
    for b in range(NB):
        ok = (key[None] // NQ == b) & (key[None] % NQ <= p[:, None] % NQ)
        c[:, C_NM + b * NS:C_NM + (b + 1) * NS] = np.where(ok, 0.0, NEG)
    c[:, C_QD:C_QD + NS] = key[None] % NQ == p[:, None] % NQ
    c[:, C_RST:C_RST + NS] = key[None] % NQ != 0
    c[:, C_ONE] = 1.0
    return c


def kernel(**inputs):
    import numpy as _np
    import concourse.bacc as _bacc
    from concourse import mybir as _mybir
    from concourse.bass_utils import run_bass_kernel_spmd as _run

    nc = _bacc.Bacc("TRN2", target_bir_lowering=False, num_devices=1, dynamic_dma_scratch_size=4096)
    arrays, args = {}, {}
    given = {n: _np.ascontiguousarray(inputs[n]) for n in _INS}
    given["table"] = constants()
    for name, a in given.items():
        arrays[f"in_{name}"] = a
        args[name] = nc.dram_tensor(f"in_{name}", a.shape, _mybir.dt.from_np(a.dtype), kind="ExternalInput").ap()
    for name, shape in _OUTS:
        args[name] = nc.dram_tensor(f"out_{name}", shape, _mybir.dt.float32, kind="ExternalOutput").ap()
    with ExitStack() as ctx:
        build(nc, ctx, **args)
    r = _run(nc, [arrays], core_ids=[0])
    return tuple(r.results[0][f"out_{name}"] for name, _ in _OUTS)
```

```python
from contextlib import ExitStack

import concourse.bass as bass
from concourse import mybir

F32 = mybir.dt.float32
F32R = mybir.dt.float32r
BF16 = mybir.dt.bfloat16
I32 = mybir.dt.int32
ALU = mybir.AluOpType
ACT = mybir.ActivationFunctionType
AX = mybir.AxisListType.X

P = 128
D = 1024
KT = D // P
SEQ = 512
NB = 8
NQ = 8
NS = NB * NQ
TOK = SEQ + NS
H = 16
HD = 64
CONV_W = 3
PAGE = 128
NPG = 16
PAST = NPG * PAGE
QB = SEQ // P
EPS = 1e-6
NT = 5
HALF = 256
TAIL = TOK - HALF
NEG = -1e30
RING = 8
STREAM = 2 * NPG
SLAB = 256
NSLAB = D // SLAB

C_ID, C_ONESB, C_TRI, C_CM, C_NM, C_QD, C_RST, C_ONE = 0, 128, 256, 384, 512, 1024, 1088, 1152
C_ALL = 1153
G_A, G_KV, G_B, G_CONV, G_K, G_Q = 0, 8, 16, 24, 48, 49
G_ALL = 50


def rows(t):
    return P if t < QB else NS


def toks(t):
    return slice(t * P, t * P + rows(t))


class Chain:

    def __init__(self, eng, sem):
        self.eng, self.sem, self.base, self.n = eng, sem, 0, 0

    def link(self, ins):
        self.n += 1
        ins.then_inc(self.sem, 1)
        self.eng.wait_ge(self.sem, self.base + self.n)

    def loop(self, i, per, done):
        self.base, self.n, self.per = i * per + done, 0, per

    def end(self):
        assert self.n == self.per, (self.n, self.per)


def build(nc, ctx, x_prompt, x_sample, state_conv, cache_k, cache_v, cache_logf, page_table,
          a_norm, a_w_in, a_conv, a_w_out, kv_norm, kv_w, kv_fbias, k_norm,
          b_norm, b_w_in, q_norm, b_w_out, table,
          y_prompt, y_sample, conv_prompt, conv_sample, k_prompt, v_prompt, logf_prompt,
          k_sample, v_sample, logf_sample):
    n_pool = cache_k.shape[0]

    suffix_dram = nc.dram_tensor("suffix_scratch", [NB, H, PAST], F32, kind="Internal").ap()
    f_dram = nc.dram_tensor("f_scratch", [H, TOK], F32, kind="Internal").ap()
    h_dram = nc.dram_tensor("h_scratch", [NT * P, D], F32, kind="Internal").ap()

    at = {"top": nc.sbuf_base + (-nc.sbuf_base) % 32}

    def place(name, shape, dt=F32, over=None):
        n = 4 if dt is not BF16 else 2
        for s in shape[1:]:
            n *= s
        n += (-n) % 32
        off = at["top"] if over is None else over
        if over is None:
            at["top"] += n
        at[name] = off
        return nc.alloc_sbuf_tensor_at(name, shape, dt, offset=off)

    XH = place("xn_high", [P, KT, TOK], F32R)
    XL = place("xn_low", [P, KT, TOK], F32R)
    GH = place("gated_high", [P, KT, TOK], F32R)
    GL = place("gated_low", [P, KT, TOK], F32R)
    WH = place("w_high", [P, 2, KT, P], F32R)
    WL = place("w_low", [P, 2, KT, P], F32R)
    WR = place("w_raw", [P, 2, KT, P])
    ring = place("page_ring", [P, RING, D])
    KTS = [place("k_turned", [P, KT, 2 * PAGE])]
    PTS = place("p_turned", [P, NPG, P])
    KTS.append(place("k_turned_odd", [P, KT, 2 * PAGE], over=at["p_turned"]))
    SS = place("sample_scores", [P, PAST])
    SFX = place("suffix", [P, 2, 512])
    QZ = place("q_spread", [P, NB, KT, 32])
    CT = place("constants", [P, C_ALL])
    QT = place("q_t", [P, SEQ])
    KN_T = place("k_t", [P, TOK])
    VT = place("v_t", [P, TOK])
    SZ = place("silu_z", [P, TOK])
    SQ = place("squares", [P, TOK])
    RR = place("rsqrt", [P, TOK])
    KN = place("k_rows", [P, NT, P])
    VN = place("v_rows", [P, QB, P])
    FB = place("f_broad", [P, 2, SEQ])
    PB = [place("probs", [P, 2, SEQ]), place("probs_odd", [P, 2, SEQ - P], over=at["squares"])]
    PT = place("probs_t", [P, 2, QB, P])
    OPAST = place("o_past", [P, NB, 4 * HD])
    KS = place("ks_t", [P, KT, NS])
    VS = place("vs_rows", [NS, D])
    SZS = place("silu_zs", [P, KT, NS])
    GAIN = place("gains", [P, G_ALL])
    GQ = place("gain_q", [P, 1])
    IDB = place("ident_b", [P, P], BF16)
    CMB = place("causal_b", [P, P], BF16)
    CST = place("conv_tail", [P, KT, 18])
    ST = place("conv_state", [P, KT, 2 * NB])
    LFN = place("logf_rows", [P, NT, H])
    FQN = place("f_rows", [P, QB, H])
    CK = place("f_new", [P, NS])
    CQ = place("f_query", [P, NB])
    TINY = place("tiny", [P, 64])
    WFR = place("wf_raw", [P, KT, H], over=at["squares"])
    WFH = place("wf_high", [P, KT, H], F32R)
    WFL = place("wf_low", [P, KT, H], F32R)
    PTAB = place("page_row", [1, NB * NPG], I32)
    PIDX = place("page_column", [P, 1], I32)
    FBIAS = place("f_bias", [H, 1])
    QC = place("q_current", [P, KT, 32])
    MS = place("max_past", [P, NB])
    LS = place("sum_past", [P, NB])
    assert at["top"] <= nc.sbuf_usable_end, at["top"]
    X = place("residual", [P, NT, D], over=at["page_ring"])
    LF = place("logf_pages", [P, PAGE, H], over=at["page_ring"] + 5 * 4 * D)
    XS = place("x_scaled", [P, D], over=at["page_ring"] + 7 * 4 * D)
    CS = place("logf_sums", [P, H, PAGE], over=at["sample_scores"])
    STN = place("state_rows", [2 * NB, D], over=at["suffix"])
    GR = place("gain_rows", [G_ALL, P], over=at["f_broad"])
    JUNK = place("junk", [P, D], over=at["probs"])
    EXT = place("conv_in", [P, SEQ + 2], over=at["probs"])
    EXTS = place("conv_in_s", [P, NB, NQ + 2], over=at["probs"] + 4 * (SEQ + 8))
    CO = place("conv_rows", [18, D], over=at["probs_t"])
    WHB = place("w_high_b", [P, KT, SLAB], F32R, over=at["k_turned"])
    WLB = place("w_low_b", [P, KT, SLAB], F32R, over=at["p_turned"])
    WHA = WH[:, :, :, :].rearrange("p s k n -> p (s k n)").rearrange("p (k n) -> p k n", k=KT)
    WLA = WL[:, :, :, :].rearrange("p s k n -> p (s k n)").rearrange("p (k n) -> p k n", k=KT)
    WRA = WR[:, :, :, :].rearrange("p s k n -> p (s k n)").rearrange("p (k n) -> p k n", k=KT)
    first_q = [(WHB[:, :, s * P:(s + 1) * P], WLB[:, :, s * P:(s + 1) * P]) for s in range(2)]
    slab_h = [WHA, WHB[:, :, :]]
    slab_l = [WLA, WLB[:, :, :]]
    QF = place("queries", [P, KT, TOK], over=at["gated_high"])
    FA = place("f_raw", [H, TOK], over=at["k_t"])
    FN = place("f_neg", [H, TOK], over=at["v_t"])
    FE = place("f_exp", [H, TOK], over=at["silu_z"])
    FL = place("f_log", [H, TOK], over=at["probs"])
    FT = place("f_sum", [H, TOK], over=at["f_broad"])
    SN = place("new_scores", [P, NB, NS], over=at["suffix"])
    NBI = place("new_bias", [P, NB, NS], over=at["suffix"] + 4 * NB * NS)
    PNT = place("new_probs_t", [NS, NB, P], over=at["probs"])
    OM = place("o_merged", [P, NB, 4 * HD], over=at["sample_scores"])
    GS = place("gated_s", [P, KT, NS], over=at["probs_t"])

    ident = CT[:, C_ID:C_ID + P]
    PS = ctx.enter_context(nc.psum_tensor("psum", [P, 8, 512], F32))
    D0, D1, T0, T1, C0, C1, OP, OS = range(8)

    def sem(name):
        return ctx.enter_context(nc.semaphore(name))

    s_ch_act, s_ch_dve, s_ch_pool = sem("act_chain"), sem("dve_chain"), sem("pool_chain")
    s_const, s_rows, s_idx = sem("constants_loaded"), sem("rows_loaded"), sem("pages_loaded")
    s_x = [sem(f"x_loaded{t}") for t in range(NT)]
    s_lf = sem("logf_gathered")
    s_cs, s_rtot, s_sfx, s_sfx_st = sem("logf_summed"), sem("later_pages"), sem("suffix_ready"), sem("suffix_stored")
    s_gt, s_gain, s_stt, s_st = sem("gains_turned"), sem("gains_ready"), sem("state_turned"), sem("state_ready")
    s_bf = sem("bf16_consts")
    s_zero, s_rms = sem("q_spread_zero"), sem("rms_ready")
    s_xs, s_xt, s_xh, s_xl = sem("x_scaled"), sem("x_turned"), sem("xn_high_ready"), sem("xn_low_ready")
    a_raw = [sem(f"a_w_loaded{s}") for s in range(2)]
    a_scaled, a_high, a_split = sem("a_w_scaled"), sem("a_w_high"), sem("a_w_split")
    a_proj, a_c, a_v, a_z, a_cvz = sem("a_projected"), sem("a_c_out"), sem("a_v_made"), sem("a_silu"), sem("a_cvz")
    a_cv, a_g, a_gh, a_gl = sem("a_conv"), sem("a_gated"), sem("a_gated_high"), sem("a_gated_low")
    l_raw, l_scaled, l_high, l_split = sem("slab_loaded"), sem("slab_scaled"), sem("slab_high"), sem("slab_split")
    l_tile, l_evac = sem("out_tile"), sem("out_added")
    s_cost = sem("conv_stored")
    s_hst, s_ctt, s_co = sem("h_stored"), sem("conv_turned"), sem("conv_rows_ready")
    s_wf, s_wfs, s_wfh, s_wfl = sem("wf_loaded"), sem("wf_scaled"), sem("wf_high"), sem("wf_low")
    s_fp, s_fa, s_fneg, s_fe = sem("f_projected"), sem("f_raw_ready"), sem("f_neg"), sem("f_exp")
    s_fl, s_ft, s_fst, s_fn, s_fnr = sem("f_log"), sem("f_sum"), sem("f_stored"), sem("f_turned"), sem("f_rows_ready")
    s_ck, s_cq = sem("f_new_loaded"), sem("f_query_ready")
    q_sq, q_ss, q_ln, q_rr, q_out = sem("q_squares"), sem("q_summed"), sem("q_ln"), sem("q_rsqrt"), sem("q_ready")
    b_page = [sem(f"page_loaded{s}") for s in range(RING)]
    b_used, b_qc, b_qt = sem("v_page_used"), sem("q_current_ready"), sem("q_pair_ready")
    b_raw = [sem(f"b_w_loaded{s}") for s in range(2)]
    b_scaled, b_high, b_split, b_proj = sem("b_w_scaled"), sem("b_w_high"), sem("b_w_split"), sem("b_projected")
    b_dact, b_ddve = sem("proj_out_act"), sem("proj_out_dve")
    b_t0, b_t0f, b_t1, b_t1f = sem("turn0_full"), sem("turn0_free"), sem("turn1_full"), sem("turn1_free")
    b_c0, b_c0f, b_c1, b_c1f = sem("score0_full"), sem("score0_free"), sem("score1_full"), sem("score1_free")
    b_ss, b_ln, b_rr, b_normed = sem("head_squares"), sem("head_ln"), sem("head_rsqrt"), sem("head_normed")
    b_sfx = [sem(f"suffix_loaded{s}") for s in range(2)]
    b_fb, b_nbs, b_es, b_lp, b_sot = (
        sem("f_broad_loaded"), sem("sample_bias"), sem("sample_exp"), sem("sample_sum"), sem("sample_out"))
    b_nbp, b_ep, b_pn, b_po, b_sz, b_gf, b_gh, b_gl = (
        sem("prompt_bias"), sem("prompt_exp"), sem("prompt_probs"), sem("prompt_pv"), sem("silu_z_ready"),
        sem("gated"), sem("gated_h"), sem("gated_l"))
    b_zl, b_zm, b_ze = sem("z_logs"), sem("z_exponent"), sem("z_sigmoid")
    b_kst, b_fq = sem("ks_kept"), sem("rows_f_taken")
    b_kpo, b_kso, b_vpo = sem("k_prompt_stored"), sem("k_sample_stored"), sem("v_prompt_stored")
    m_s, m_sn, m_exp, m_bias, m_p, m_t, m_ta, m_td, m_pv, m_om, m_ot, m_gs, m_gh, m_gl, m_a = (
        sem("new_scored"), sem("new_scores_ready"), sem("old_weight"), sem("new_bias_ready"), sem("new_probs"),
        sem("new_turned"), sem("new_t_act"), sem("new_t_dve"), sem("new_pv"), sem("merged"), sem("merged_turned"),
        sem("gated_s"), sem("gated_sh"), sem("gated_sl"), sem("new_aux"))
    s_hld = sem("h_loaded")
    s_out = sem("outputs_stored")

    LINKS = dict(dve_a=8, dve_b=10, act_b=2)

    w_in = a_w_in[0].rearrange("(k p) n -> p k n", p=P)
    wo_a = a_w_out[0].rearrange("(k p) n -> p k n", p=P)
    wkv = kv_w.rearrange("(k p) n -> p k n", p=P)
    wqz = b_w_in[0].rearrange("(k p) n -> p k n", p=P)
    wo_b = b_w_out[0].rearrange("(k p) n -> p k n", p=P)
    kpages = cache_k.rearrange("g p h d -> g p (h d)")
    vpages = cache_v.rearrange("g p h d -> g p (h d)")
    A_ORDER = (1, 2, 3, 0)

    def both(bank):
        return PS[:, bank:bank + 2, 0:HALF], PS[:, bank + 1, HALF:TAIL]

    def prompt2(ap):
        return ap.rearrange("p (a n) -> p a n", a=2)

    def gain(row):
        return GAIN[:, row:row + KT].unsqueeze(2).to_broadcast([P, KT, P])

    block = ctx.enter_context(nc.Block())

    @block.sync
    def _(sp):
        sp.dma_start(X[:, 0, :], x_prompt[0, 0:P, :]).then_inc(s_x[0], 16)
        sp.dma_start(CT[:, :], table).then_inc(s_const, 16)
        sp.dma_start(PIDX[:, :], page_table.rearrange("b (g a) -> (b g) a", a=1)).then_inc(s_idx, 16)
        sp.dma_start(X[:, 1, :], x_prompt[0, toks(1), :]).then_inc(s_x[1], 16)
        for r, v in ((G_A, a_norm[0]), (G_KV, kv_norm), (G_B, b_norm[0])):
            sp.dma_start(GR[r:r + KT, :], v.rearrange("(k p) -> k p", p=P)).then_inc(s_rows, 16)
        sp.dma_start(GR[G_CONV:G_CONV + CONV_W * KT, :],
                     a_conv[0].rearrange("j (k p) -> (j k) p", p=P)).then_inc(s_rows, 16)
        for t in range(2, QB):
            sp.dma_start(X[:, t, :], x_prompt[0, toks(t), :]).then_inc(s_x[t], 16)
        sp.dma_start(X[0:NS, QB, :], x_sample.rearrange("b q n -> (b q) n")).then_inc(s_x[QB], 16)

        def load_a(i, q):
            sp.dma_start(WR[:, q % 2, :, :], w_in[:, :, bass.ds((i + A_ORDER[q] * KT) * P, P)]).then_inc(a_raw[q % 2], 16)

        for q in range(2):
            load_a(0, q)

        def mixer(i, last):
            for q in range(4):
                if last and q >= 2:
                    continue
                sp.wait_ge(a_split, 4 * i + q + 1)
                load_a(i + q // 2, (q + 2) % 4)

        with sp.Fori(0, KT - 1) as i:
            mixer(i, False)
        mixer(KT - 1, True)

        def load_slab(w, col, n):
            sp.dma_start(WRA, w[:, :, bass.ds(col, SLAB)]).then_inc(l_raw, 16)

        sp.wait_ge(a_split, 4 * KT)
        load_slab(wo_a, 0, 0)
        sp.wait_ge(a_gl, KT)
        sp.dma_start(WFR[:, :, :], wkv[:, :, 2 * D:2 * D + H]).then_inc(s_wf, 16)
        with sp.Fori(1, NSLAB) as n:
            sp.wait_ge(l_split, n)
            load_slab(wo_a, n * SLAB, n)
        sp.wait_ge(s_sfx_st, 16 * NB)
        sp.wait_ge(s_st, 1)

        def load_suffix(b, c):
            src = suffix_dram[bass.ds(b, 1), :, c * 512:(c + 1) * 512].rearrange("a h n -> (a h) n")
            sp.dma_start(SFX[:, c % 2, :], src.unsqueeze(1).to_broadcast([H, NQ, 512])).then_inc(b_sfx[c % 2], 16)

        load_suffix(0, 0)
        load_suffix(0, 1)

        def load_w(w, col, slot):
            sp.dma_start(WR[:, slot, :, :], w[:, :, bass.ds(col, P)]).then_inc(b_raw[slot], 16)

        sp.wait_ge(l_split, NSLAB)
        for n in range(4):
            if n >= 2:
                sp.wait_ge(b_split, n - 1)
            load_w(wqz, n * P, n % 2)
        for t in range(NT):
            sp.wait_ge(l_evac, 5 * (NSLAB - 1) + t + 1)
            sp.dma_start(h_dram[t * P:t * P + rows(t), :], X[0:rows(t), t, :]).then_inc(s_hst, 16)
        sp.wait_ge(s_co, 1)
        sp.dma_start(conv_prompt[0, 0], CO[0:2, :]).then_inc(s_cost, 16)
        sp.dma_start(conv_sample[0].rearrange("b s n -> (b s) n"), CO[2:18, :]).then_inc(s_cost, 16)

        def load_page(b, n):
            page = sp.value_load(PTAB[0:1, bass.ds(b * NPG + n % NPG, 1)], min_val=0, max_val=n_pool - 1)
            src = (kpages if n < NPG else vpages)[bass.ds(page, 1), :, :]
            sp.dma_start(ring[:, n % RING, :], src.rearrange("a p n -> (a p) n")).then_inc(b_page[n % RING], 16)

        sp.wait_ge(s_rows, 16 * 11)
        sp.wait_ge(s_cost, 32)
        sp.wait_ge(s_hst, 16 * NT)
        sp.wait_ge(s_xl, 2 * NT)
        for n in range(RING // 2):
            load_page(0, n)
        sp.wait_ge(s_ft, 1)
        sp.dma_start(f_dram, FT[:, :]).then_inc(s_fst, 16)
        sp.wait_ge(s_fst, 16)
        sp.dma_start(CK[:, :], f_dram[:, SEQ:TOK].unsqueeze(1).to_broadcast([H, NQ, NS])).then_inc(s_ck, 16)
        for n in range(4, 10):
            sp.wait_ge(b_split, n - 1)
            load_w(*((wqz, n * P), (wkv, D), (wkv, 0))[max(n - 7, 0)], n % 2)
            if n < 8:
                load_page(0, n)
        sp.wait_ge(s_fnr, 1)
        sp.dma_start(logf_prompt[0].rearrange("(t p) h -> p t h", p=P), LFN[:, 0:QB, :]).then_inc(s_out, 16)
        sp.dma_start(logf_sample.rearrange("b q h -> (b q) h"), LFN[0:NS, QB, :]).then_inc(s_out, 16)

        def heads(i, last):
            for n in range(STREAM):
                if n == 0:
                    sp.wait_ge(b_c0f, 8 * i)
                    sp.wait_ge(b_c1f, 8 * i)
                    src = f_dram[bass.ds(2 * i, 2), 0:SEQ].unsqueeze(0).to_broadcast([P, 2, SEQ])
                    sp.dma_start(FB[:, :, :], src).then_inc(b_fb, 16)
                if n == 0:
                    sp.wait_ge(b_split, KT + 3 * i + 2)
                    load_w(wqz, (i + KT) * P, 1)
                if n == 4 and not last:
                    sp.wait_ge(b_split, KT + 3 * i + 1)
                    load_w(wkv, (i + 1 + KT) * P, 0)
                if n == 12 and not last:
                    sp.wait_ge(b_split, KT + 3 * i + 3)
                    load_w(wkv, (i + 1) * P, 1)
                if n in (4, 8, 12, 16):
                    c = n // 4 + 1
                    if not (last and c >= 4):
                        sp.wait_ge(b_c1f, 8 * i + n // 4)
                        load_suffix(i + c // 4, c % 4)
                if not (last and n >= STREAM - RING):
                    sp.wait_ge(s_rows, 16 * 11)
                    if n < NPG:
                        sp.wait_ge(b_t1, 24 * i + n + 1)
                    else:
                        sp.wait_ge(b_used, NPG * i + n - NPG + 1)
                    load_page(i + (n + RING) // STREAM, (n + RING) % STREAM)

        with sp.Fori(0, NB - 1) as i:
            heads(i, False)
        heads(NB - 1, True)

        sp.wait_ge(b_used, NPG * NB)
        for t in range(NT):
            sp.dma_start(X[0:rows(t), t, :], h_dram[t * P:t * P + rows(t), :]).then_inc(s_hld, 16)
        sp.wait_ge(b_split, KT + 3 * NB)
        load_slab(wo_b, 0, 0)
        sp.wait_ge(b_t1f, 24 * NB)
        sp.dma_start(v_sample.rearrange("b q h d -> (b q) (h d)"), VS[:, :]).then_inc(s_out, 16)
        with sp.Fori(1, NSLAB) as n:
            sp.wait_ge(l_split, n + NSLAB)
            load_slab(wo_b, n * SLAB, n)
        for t in range(NT):
            sp.wait_ge(l_evac, 5 * (2 * NSLAB - 1) + t + 1)
            if t < QB:
                sp.dma_start(y_prompt[0, toks(t), :], X[:, t, :]).then_inc(s_out, 16)
            else:
                sp.dma_start(y_sample.rearrange("b q n -> (b q) n"), X[0:NS, t, :]).then_inc(s_out, 16)
        sp.wait_ge(s_out, 16 * (2 + 1 + NT))
        sp.wait_ge(b_kpo, 16 * NB)
        sp.wait_ge(b_kso, 16 * NB)
        sp.wait_ge(b_vpo, 16 * NB)

    @block.gpsimd
    def _(pool):
        pool.wait_ge(s_idx, 16)
        pool.indirect_dma_start(
            LF[:, :, :].rearrange("p n h -> p (n h)"), None, cache_logf.rearrange("g p h -> g (p h)"),
            bass.IndirectOffsetOnAxis(ap=PIDX[:, 0:1], axis=0)).then_inc(s_lf, 16)
        pool.memset(QZ[:, :, :, :], 0.0).then_inc(s_zero, 1)

        pool.wait_ge(s_gain, 1)
        for q in range(2):
            pool.wait_ge(a_raw[q], 16)
            pool.tensor_tensor(WR[:, q, :, :], WR[:, q, :, :], gain(G_A), ALU.mult).then_inc(a_scaled, 1)

        def mixer(i, last):
            for q in range(4):
                if not (last and q >= 2):
                    pool.wait_ge(a_raw[q % 2], (2 * i + q // 2 + 2) * 16)
                    pool.tensor_tensor(WR[:, q % 2, :, :], WR[:, q % 2, :, :], gain(G_A),
                                       ALU.mult).then_inc(a_scaled, 1)
                if q == 2:
                    pool.wait_ge(a_z, i + 1)
                    pool.wait_ge(a_cv, i + 1)
                    pool.tensor_tensor(RR[:, :], RR[:, :], SZ[:, :], ALU.mult).then_inc(a_cvz, 1)

        with pool.Fori(0, KT - 1) as i:
            mixer(i, False)
        mixer(KT - 1, True)
        pool.wait_ge(s_sfx, 1)
        for b in range(NB):
            pool.dma_start(suffix_dram[b].rearrange("h (g n) -> g h n", g=NPG),
                           CS[b * NPG:(b + 1) * NPG, :, :]).then_inc(s_sfx_st, 16)
        pool.wait_ge(s_wf, 16)
        pool.tensor_tensor(WFR[:, :, :], WFR[:, :, :],
                           GAIN[:, G_KV:G_KV + KT].unsqueeze(2).to_broadcast([P, KT, H]), ALU.mult).then_inc(s_wfs, 1)

        def scale_b(slot, count, g):
            pool.wait_ge(b_raw[slot], 16 * count)
            pool.tensor_tensor(WR[:, slot, :, :], WR[:, slot, :, :], gain(g), ALU.mult).then_inc(b_scaled, 1)

        for n in range(10):
            scale_b(n % 2, n // 2 + 1, G_B if n < KT else G_KV)
        pool.wait_ge(q_out, KT)
        pool.tensor_copy(QC[:, :, :], QZ[:, 0, :, :]).then_inc(b_qc, 1)
        pool.tensor_copy(QT[:, :], QF[:, 0, 0:SEQ]).then_inc(b_qt, 1)

        def heads(i, last):
            scale_b(1, 6 + 2 * i, G_B)
            if not last:
                scale_b(0, 6 + i, G_KV)
            pool.wait_ge(b_rr, i + 1)
            pool.tensor_tensor(KN_T[:, :], KN_T[:, :], RR[:, :], ALU.mult).then_inc(b_normed, 1)
            if not last:
                scale_b(1, 7 + 2 * i, G_KV)
                pool.wait_ge(b_c1, 8 * i + 4)
                pool.tensor_copy(QC[:, :, :].rearrange("p k n -> p (k n)"),
                                 QZ[:, bass.ds(i + 1, 1), :, :].rearrange("p a k n -> p (a k n)")).then_inc(b_qc, 1)
                pool.wait_ge(b_c0, 8 * i + 8)
                pool.wait_ge(b_c1, 8 * i + 8)
                pool.tensor_copy(QT[:, :], QF[:, bass.ds(i + 1, 1), 0:SEQ].rearrange("p a n -> p (a n)")).then_inc(b_qt, 1)

        with pool.Fori(0, NB - 1) as i:
            heads(i, False)
        heads(NB - 1, True)

    @block.scalar
    def _(act):
        ch = Chain(act, s_ch_act)

        def norm(t, phase):
            n = NT * phase + t
            r = rows(t)
            if phase == 0:
                act.wait_ge(s_x[t], 16)
            else:
                act.wait_ge(l_evac, 5 * (NSLAB - 1) + t + 1)
            c = 6 * (t % 2)
            if n >= 2:
                act.wait_ge(s_xs, n - 1)
            ch.link(act.activation(JUNK[0:r, :], X[0:r, t, :], ACT.Square, accum_out=TINY[0:r, 4 + c:5 + c]))
            act.activation(TINY[0:r, 5 + c:6 + c], TINY[0:r, 4 + c:5 + c], ACT.Sqrt, bias=EPSB(r),
                           scale=1.0 / D).then_inc(s_rms, 1)

        def EPSB(r):
            return TINY[0:r, 3:4]

        def norm_high(t, phase):
            n = NT * phase + t
            b = 2 * (n % 3)
            act.wait_ge(s_xt, n + 1)
            src = PS[:, b:b + 2, :].rearrange("p a (k n) -> p (a k) n", k=4)[:, :, 0:rows(t)]
            act.activation(XH[:, :, toks(t)], src, ACT.Copy).then_inc(s_xh, 1)

        for r, v in ((G_K, k_norm), (G_Q, q_norm[0])):
            for e in range(2):
                act.dma_start(GR[r:r + 1, e * HD:(e + 1) * HD], v.unsqueeze(0)).then_inc(s_rows, 16)
        act.dma_start(STN[:, :], state_conv[0].rearrange("b s n -> (b s) n")).then_inc(s_rows, 16)
        act.dma_start(FBIAS[:, :], kv_fbias.unsqueeze(1)).then_inc(s_rows, 16)
        act.dma_start(PTAB[:, :], page_table.rearrange("b g -> (b g)").unsqueeze(0)).then_inc(s_rows, 16)
        act.wait_ge(s_bf, 3)
        norm(0, 0)
        for t in range(NT):
            if t + 1 < NT:
                norm(t + 1, 0)
            norm_high(t, 0)

        def high_a(n, slot):
            act.wait_ge(a_scaled, n + 1)
            act.activation(WH[:, slot, :, :], WR[:, slot, :, :], ACT.Copy).then_inc(a_high, 1)

        for q in range(2):
            high_a(q, q)

        def high_slab(s):
            act.activation(slab_h[s], WRA, ACT.Copy).then_inc(l_high, 1)

        def mixer(i, last):
            for q in range(4):
                act.wait_ge(a_proj, 4 * i + q + 1)
                if not (last and q >= 2):
                    high_a(4 * i + q + 2, q % 2)
                pr, sa = both(2 * q)
                if q == 0:
                    act.wait_ge(a_v, i)
                    act.activation(prompt2(SQ[:, 0:SEQ]), pr, ACT.Copy)
                    act.activation(SQ[:, SEQ:TOK], sa, ACT.Copy).then_inc(a_c, 1)
                if q == 2:
                    act.wait_ge(a_cvz, i)
                    act.activation(prompt2(SZ[:, 0:SEQ]), pr, ACT.Silu)
                    act.activation(SZ[:, SEQ:TOK], sa, ACT.Silu).then_inc(a_z, 1)
                    if last:
                        act.wait_ge(l_raw, 16)
                        high_slab(1)
                if q == 3:
                    act.wait_ge(a_g, i + 1)
                    act.activation(GH[:, bass.ds(i, 1), :].rearrange("p a n -> p (a n)"), VT[:, :],
                                   ACT.Copy).then_inc(a_gh, 1)

        with act.Fori(0, KT - 1) as i:
            mixer(i, False)
        mixer(KT - 1, True)

        for n in range(1, NSLAB):
            act.wait_ge(l_raw, 16 * (n + 1))
            if n >= 2:
                act.wait_ge(l_tile, NT * (n - 1))
            high_slab(1 - n % 2)
            if n == 1:
                act.wait_ge(s_wfs, 1)
                act.activation(WFH[:, :, :], WFR[:, :, :], ACT.Copy).then_inc(s_wfh, 1)

        def high_b(n, slot, to=None):
            act.wait_ge(b_scaled, n + 1)
            act.activation(to or WH[:, slot, :, :], WR[:, slot, :, :], ACT.Copy).then_inc(b_high, 1)

        act.wait_ge(l_tile, NT * (NSLAB - 1))
        high_b(0, 0, first_q[0][0])
        high_b(1, 1, first_q[1][0])

        for t in range(NT):
            norm(t, 1)
            if t:
                norm_high(t - 1, 1)
        norm_high(NT - 1, 1)
        log_exp = "natural_log_exp_and_others"
        act.preload_act_table_set(log_exp)
        act.wait_ge(s_ctt, 1)
        act.activation(CO[:, :].rearrange("p (a n) -> p a n", a=2), PS[0:18, 6:8, :], ACT.Copy).then_inc(s_co, 1)
        act.wait_ge(s_fneg, 1)
        ch.link(act.activation(FE[:, :], FN[:, :], ACT.Exp))
        act.activation(FE[:, :], FE[:, :], ACT.Ln, bias=1.0).then_inc(s_fe, 1)

        def query(m, s):
            pr, sa = both(C0 * s)
            act.wait_ge(b_proj, m + 1)
            act.wait_ge(q_ss, m)
            act.activation(prompt2(SQ[:, 0:SEQ]), pr, ACT.Square)
            act.activation(SQ[:, SEQ:TOK], sa, ACT.Square).then_inc(q_sq, 1)
            high_b(m + 2, s)
            act.wait_ge(q_ss, m + 1)
            act.wait_ge(q_out, m)
            act.activation(RR[:, 0:SEQ], PS[:, OP, :], ACT.Ln, bias=EPSB(P), scale=1.0 / HD)
            act.activation(RR[:, SEQ:TOK], PS[:, OS, 0:NS], ACT.Ln, bias=EPSB(P), scale=1.0 / HD).then_inc(q_ln, 1)
            act.wait_ge(q_ln, m + 1)
            act.activation(RR[:, :], RR[:, :], ACT.Exp, scale=-0.5).then_inc(q_rr, 1)

        act.wait_ge(s_wfl, 1)
        with act.Fori(0, KT // 2) as j:
            for s in range(2):
                query(2 * j + s, s)

        act_done = ch.n

        def heads(i, last):
            t0 = [0]

            def turned0(out, src):
                act.wait_ge(b_t0, 24 * i + t0[0] + 1)
                t0[0] += 1
                return act.activation(out, src, ACT.Copy)

            for k in range(NPG):
                c = (k % 2) * PAGE
                if k % 2 == 0 and k >= 4:
                    act.wait_ge((b_c0, b_c1)[k // 2 % 2], 8 * i + k // 4)
                turned0(KTS[k // 2 % 2][:, 0:4, c:c + PAGE],
                        PS[:, T0, :].rearrange("p (k n) -> p k n", k=4)).then_inc(b_t0f, 1)
                if k == 6:
                    pr, sa = both(D0)
                    act.wait_ge(b_proj, KT + 3 * i + 1)
                    act.wait_ge(b_gl, i)
                    act.wait_ge(b_ddve, i + 1)
                    act.activation(prompt2(SQ[:, 0:SEQ]), pr, ACT.Square)
                    act.activation(SQ[:, SEQ:TOK], sa, ACT.Square).then_inc(b_dact, 1)
                if k == 10:
                    high_b(KT + 3 * i + 2, 1)
                if k == 14:
                    pr, sa = both(D0)
                    act.wait_ge(b_proj, KT + 3 * i + 2)
                    act.activation(prompt2(VT[:, 0:SEQ]), pr, ACT.Copy)
                    act.activation(VT[:, SEQ:TOK], sa, ACT.Copy).then_inc(b_dact, 1)
                if k == 9:
                    act.wait_ge(b_ss, i + 1)
                    act.wait_ge(b_normed, i)
                    act.activation(RR[:, SEQ:TOK], PS[:, OS, 0:NS], ACT.Ln, bias=EPSB(P), scale=1.0 / HD)
                    act.activation(RR[:, 0:SEQ], PS[:, OP, :], ACT.Ln, bias=EPSB(P), scale=1.0 / HD).then_inc(b_ln, 1)
                    act.wait_ge(b_ln, i + 1)
                    act.activation(RR[:, :], RR[:, :], ACT.Exp, scale=-0.5).then_inc(b_rr, 1)
            if not last:
                high_b(KT + 3 * i + 3, 0)
            act.wait_ge(b_kpo, 16 * i)
            act.wait_ge(b_vpo, 16 * i)
            turned0(KN[:, 0:QB, :], PS[:, T0, :].rearrange("p (k n) -> p k n", k=4)).then_inc(b_t0f, 1)
            turned0(VN[:, :, :], PS[:, T0, :].rearrange("p (k n) -> p k n", k=4)).then_inc(b_t0f, 1)
            act.wait_ge(b_nbs, i + 1)
            act.wait_ge(b_lp, i)
            for c in range(4):
                ins = act.activation(SS[:, c * 512:(c + 1) * 512], SS[:, c * 512:(c + 1) * 512], ACT.Exp,
                                     bias=TINY[:, 13:14], accum_out=TINY[:, 16 + c:17 + c])
                ins.then_inc(b_es, 1)
            for g in (0, 2):
                turned0(PTS[:, 4 * g:4 * g + 4, :], PS[:, T0, :].rearrange("p (k n) -> p k n", k=4)).then_inc(b_t0f, 1)
            cols = bass.ds(i * P, P)
            act.wait_ge(b_t0f, 24 * i + 18)
            act.wait_ge(b_t1f, 24 * i + 17)
            act.dma_start(k_prompt[0].rearrange("(t p) h d -> p t (h d)", p=P)[:, :, cols], KN[:, 0:QB, :]).then_inc(b_kpo, 16)
            act.dma_start(v_prompt[0].rearrange("(t p) h d -> p t (h d)", p=P)[:, :, cols], VN[:, :, :]).then_inc(b_vpo, 16)
            act.dma_start(k_sample.rearrange("b q h d -> (b q) (h d)")[:, cols], KN[0:NS, QB, :]).then_inc(b_kso, 16)

            def block_exp(r):
                w = (QB - r) * P
                c = 20 + 20 * (r % 2)
                act.wait_ge(b_nbp, 4 * i + r + 1)
                for e in range(2):
                    act.activation(PB[r % 2][:, e, 0:w], PB[r % 2][:, e, 0:w], ACT.Exp, bias=TINY[:, c + 4 + e:c + 5 + e],
                                   accum_out=TINY[:, c + 6 + e:c + 7 + e]).then_inc(b_ep, 1)

            def block_turned(r):
                w = (QB - r) * P
                turned0(PT[:, 0, 0:QB - r, :], PS[:, T0, 0:w].rearrange("p (k n) -> p k n", n=P)).then_inc(b_t0f, 1)

            def gate_log():
                pr, sa = both(D0)
                act.wait_ge(b_proj, KT + 3 * i + 3)
                act.wait_ge(b_gf, i)
                act.activation(prompt2(SZ[:, 0:SEQ]), pr, ACT.Abs)
                ch.link(act.activation(SZ[:, SEQ:TOK], sa, ACT.Abs))
                ch.link(act.activation(SZ[:, :], SZ[:, :], ACT.Exp, scale=-1.0))
                act.activation(SZ[:, :], SZ[:, :], ACT.Ln, bias=1.0).then_inc(b_zl, 1)

            ch.loop(i, LINKS["act_b"], act_done)
            block_exp(0)
            block_exp(1)
            block_turned(0)
            block_exp(2)
            block_turned(1)
            gate_log()
            block_exp(3)
            if not last:
                high_b(KT + 3 * i + 4, 1)
            block_turned(2)
            act.wait_ge(b_zm, i + 1)
            act.activation(SZ[:, :], SZ[:, :], ACT.Exp).then_inc(b_ze, 1)
            block_turned(3)
            ch.end()
            assert t0[0] == 24
            act.wait_ge(b_used, NPG * (i + 1))
            act.activation(OPAST[:, bass.ds(i, 1), :].rearrange("p a n -> p (a n)"), PS[:, OS, 0:4 * HD],
                           ACT.Copy).then_inc(b_sot, 1)
            act.wait_ge(b_gf, i + 1)
            act.activation(GH[:, bass.ds(i, 1), 0:SEQ].rearrange("p a n -> p (a n)"), SQ[:, 0:SEQ],
                           ACT.Copy).then_inc(b_gh, 1)

        with act.Fori(0, NB - 1) as i:
            heads(i, False)
        heads(NB - 1, True)

        def high_out(n):
            act.wait_ge(l_raw, 16 * (NSLAB + n + 1))
            if n >= 2:
                act.wait_ge(l_tile, NT * (NSLAB + n - 1))
            high_slab(n % 2)

        act.wait_ge(b_proj, KT + 3 * NB)
        act.wait_ge(m_exp, 1)
        act.activation(TINY[:, 40:48], TINY[:, 40:48], ACT.Exp).then_inc(m_a, 1)
        for b in range(NB):
            act.activation(SN[:, b, :], SN[:, b, :], ACT.Exp, bias=TINY[:, 48 + b:49 + b],
                           accum_out=TINY[:, 56 + b:57 + b]).then_inc(m_p, 1)
        act.wait_ge(m_t, 1)
        act.activation(PNT[:, 0:4, :], PS[0:NS, T0, :].rearrange("p (k n) -> p k n", k=4), ACT.Copy).then_inc(m_ta, 1)
        high_out(0)
        act.wait_ge(m_gs, 1)
        act.activation(GH[:, :, SEQ:TOK], GS[:, :, :], ACT.Copy).then_inc(m_gh, 1)
        for n in range(1, NSLAB):
            high_out(n)

    @block.vector
    def _(dve):
        ch = Chain(dve, s_ch_dve)
        dve.memset(TINY[:, 3:4], EPS).then_inc(s_bf, 1)
        dve.wait_ge(s_const, 16)
        dve.tensor_copy(IDB[:, :], ident).then_inc(s_bf, 1)
        dve.tensor_copy(CMB[:, :], CT[:, C_CM:C_CM + P]).then_inc(s_bf, 1)
        dve.wait_ge(s_gt, 1)
        dve.tensor_copy(GAIN[:, :], PS[:, 6, 0:G_ALL]).then_inc(s_gain, 1)
        dve.wait_ge(s_gain, 1)
        dve.tensor_scalar(GQ[:, :], GAIN[:, G_Q:G_Q + 1], HD ** -0.5, None, ALU.mult)
        dve.wait_ge(s_stt, 1)
        dve.tensor_copy(ST[:, :, :], PS[:, 7, 128:256].rearrange("p (k n) -> p k n", k=KT)).then_inc(s_st, 1)

        def norm_scale(t, phase):
            n = NT * phase + t
            r = rows(t)
            c = 6 * (t % 2) + 4
            v, y, z = TINY[0:r, c:c + 1], TINY[0:r, c + 2:c + 3], TINY[0:r, c + 3:c + 4]
            dve.wait_ge(s_rms, n + 1)
            ch.link(dve.reciprocal(y, TINY[0:r, c + 1:c + 2]))
            ch.link(dve.tensor_scalar(v, v, 1.0 / D, EPS, ALU.mult, ALU.add))
            ch.link(dve.scalar_tensor_tensor(z, y, y, v, ALU.mult, ALU.mult))
            ch.link(dve.tensor_scalar(z, z, -0.5, 1.5, ALU.mult, ALU.add))
            if n:
                dve.wait_ge(s_xt, n)
            dve.tensor_scalar(XS[0:r, :], X[0:r, t, :], y, z, ALU.mult, ALU.mult).then_inc(s_xs, 1)

        def norm_low(t, phase):
            n = NT * phase + t
            b = 2 * (n % 3)
            dve.wait_ge(s_xh, n + 1)
            src = PS[:, b:b + 2, :].rearrange("p a (k n) -> p (a k) n", k=4)[:, :, 0:rows(t)]
            dve.tensor_tensor(XL[:, :, toks(t)], src, XH[:, :, toks(t)].bitcast(F32), ALU.subtract).then_inc(s_xl, 1)

        norm_scale(0, 0)
        for t in range(NT):
            if t + 1 < NT:
                norm_scale(t + 1, 0)
            norm_low(t, 0)

        def low_a(n, slot):
            dve.wait_ge(a_high, n + 1)
            dve.tensor_tensor(WL[:, slot, :, :], WR[:, slot, :, :], WH[:, slot, :, :].bitcast(F32),
                              ALU.subtract).then_inc(a_split, 1)

        for q in range(2):
            low_a(q, q)
        dve.wait_ge(s_lf, 16)
        one = CT[:, C_ONE:C_ONE + 1].to_broadcast([P, PAGE])
        for h in range(H):
            dve.tensor_tensor_scan(CS[:, h, :], one, LF[:, :, h], 0.0, ALU.mult, ALU.add).then_inc(s_cs, 1)
        ch.link(dve.memset(EXT[:, 0:2], 0.0))
        done = ch.n

        def low_slab(n, s):
            dve.wait_ge(l_high, n + 1)
            dve.tensor_tensor(slab_l[s], WRA, slab_h[s].bitcast(F32), ALU.subtract).then_inc(l_split, 1)

        def mixer(i, last):
            ch.loop(i, LINKS["dve_a"], done)
            for q in range(4):
                if not (last and q >= 2):
                    low_a(4 * i + q + 2, q % 2)
                pr, sa = both(2 * q)
                if q == 1:
                    st = ST[:, bass.ds(i, 1), :].rearrange("p a (b s) -> p (a b) s", b=NB)
                    dve.tensor_copy(EXTS[:, :, 0:2], st)
                    dve.wait_ge(a_c, i + 1)
                    dve.wait_ge(a_proj, 4 * i + 2)
                    dve.tensor_tensor(prompt2(EXT[:, 2:SEQ + 2]), pr, prompt2(SQ[:, 0:SEQ]), ALU.mult)
                    dve.tensor_tensor(EXTS[:, :, 2:NQ + 2], sa.rearrange("p (b q) -> p b q", b=NB),
                                      SQ[:, SEQ:TOK].rearrange("p (b q) -> p b q", b=NB), ALU.mult).then_inc(a_v, 1)
                    dve.wait_ge(a_v, i + 1)
                    dve.wait_ge(a_g, i)
                    ch.link(dve.tensor_copy(CST[:, bass.ds(i, 1), 0:2].rearrange("p a n -> p (a n)"), EXT[:, SEQ:SEQ + 2]))
                    ch.link(dve.tensor_copy(
                        CST[:, bass.ds(i, 1), 2:18].rearrange("p a (b s) -> p (a b) s", b=NB), EXTS[:, :, NQ:NQ + 2]))
                    cvp = RR[:, 0:SEQ]
                    cvs = RR[:, SEQ:TOK].rearrange("p (b q) -> p b q", b=NB)
                    for j in range(CONV_W):
                        w = GAIN[:, bass.ds(G_CONV + j * KT + i, 1)]
                        if j == 0:
                            ch.link(dve.tensor_scalar(cvp, EXT[:, 0:SEQ], w, None, ALU.mult))
                            ch.link(dve.tensor_scalar(cvs, EXTS[:, :, 0:NQ], w, None, ALU.mult))
                        else:
                            ch.link(dve.scalar_tensor_tensor(cvp, EXT[:, j:j + SEQ], w, cvp, ALU.mult, ALU.add))
                            ins = dve.scalar_tensor_tensor(cvs, EXTS[:, :, j:j + NQ], w, cvs, ALU.mult, ALU.add)
                            if j == 1:
                                ch.link(ins)
                            else:
                                ins.then_inc(a_cv, 1)
                if q == 3:
                    if last:
                        low_slab(0, 1)
                    dve.wait_ge(a_proj, 4 * i + 4)
                    dve.wait_ge(a_cvz, i + 1)
                    ch.link(dve.tensor_tensor(prompt2(VT[:, 0:SEQ]), pr, prompt2(RR[:, 0:SEQ]), ALU.mult))
                    dve.tensor_tensor(VT[:, SEQ:TOK], sa, RR[:, SEQ:TOK], ALU.mult).then_inc(a_g, 1)
                    dve.wait_ge(a_gh, i + 1)
                    gl = GL[:, bass.ds(i, 1), :].rearrange("p a n -> p (a n)")
                    gh = GH[:, bass.ds(i, 1), :].rearrange("p a n -> p (a n)")
                    dve.tensor_tensor(gl, VT[:, :], gh.bitcast(F32), ALU.subtract).then_inc(a_gl, 1)
            ch.end()

        with dve.Fori(0, KT - 1) as i:
            mixer(i, False)
        mixer(KT - 1, True)
        ch.base, ch.n = 0, done + LINKS["dve_a"] * KT

        def out_tile(n, g, s, t):
            dve.wait_ge(l_tile, n + 1)
            r = rows(t)
            x = X[0:r, t, bass.ds(g * SLAB, SLAB)]
            dve.tensor_tensor(x, PS[0:r, (5 * s + t) % 8, 0:SLAB], x, ALU.add).then_inc(l_evac, 1)

        def low_b(n, slot, to=None):
            h, lo = to or (WH[:, slot, :, :], WL[:, slot, :, :])
            dve.wait_ge(b_high, n + 1)
            dve.tensor_tensor(lo, WR[:, slot, :, :], h.bitcast(F32), ALU.subtract).then_inc(b_split, 1)

        dve.wait_ge(s_rtot, 1)
        dve.tensor_tensor(CS[:, :, :], PS[:, 7, 0:H].unsqueeze(2).to_broadcast([P, H, PAGE]), CS[:, :, :],
                          ALU.subtract).then_inc(s_sfx, 1)
        low_slab(1, 0)
        dve.wait_ge(s_wfh, 1)
        dve.tensor_tensor(WFL[:, :, :], WFR[:, :, :], WFH[:, :, :].bitcast(F32), ALU.subtract).then_inc(s_wfl, 1)
        with dve.Fori(0, NSLAB // 2 - 1) as j:
            for s in range(2):
                for t in range(NT):
                    out_tile(5 * s + t + 10 * j, 2 * j + s, s, t)
                low_slab(2 * j + s + 2, 1 - s)
        for s in range(2):
            for t in range(NT):
                out_tile(5 * (NSLAB - 2 + s) + t, NSLAB - 2 + s, s, t)
            if s == 0:
                low_b(0, 0, first_q[0])
                low_b(1, 1, first_q[1])

        norm_scale(0, 1)
        for t in range(NT):
            if t + 1 < NT:
                norm_scale(t + 1, 1)
            norm_low(t, 1)
        dve.wait_ge(s_fp, 1)
        ch.link(dve.tensor_scalar(prompt2(FA[:, 0:SEQ]), PS[0:H, 2:4, 0:HALF], FBIAS[:, 0:1], None, ALU.add))
        ch.link(dve.tensor_scalar(FA[:, SEQ:TOK], PS[0:H, 3, HALF:TAIL], FBIAS[:, 0:1], None, ALU.add))
        ch.link(dve.tensor_scalar(FN[:, :], FA[:, :], -1.0, None, ALU.mult))
        dve.tensor_tensor(FN[:, :], FN[:, :], FA[:, :], ALU.min).then_inc(s_fneg, 1)
        dve.wait_ge(s_fe, 1)
        dve.scalar_tensor_tensor(FL[:, :], FA[:, :], 0.0, FE[:, :], ALU.min, ALU.subtract).then_inc(s_fl, 1)
        dve.wait_ge(s_fl, 1)
        dve.wait_ge(s_gt, 1)
        ch.link(dve.tensor_tensor_scan(FT[:, 0:SEQ], CT[0:H, C_ONE:C_ONE + 1].to_broadcast([H, SEQ]), FL[:, 0:SEQ],
                                       0.0, ALU.mult, ALU.add))
        dve.tensor_tensor_scan(FT[:, SEQ:TOK], CT[0:H, C_RST:C_RST + NS], FL[:, SEQ:TOK], 0.0,
                               ALU.mult, ALU.add).then_inc(s_ft, 1)

        dve.wait_ge(s_zero, 1)

        def query(m, s):
            low_b(m + 2, s)
            dve.wait_ge(q_rr, m + 1)
            pr, sa = both(C0 * s)
            dve.scalar_tensor_tensor(prompt2(QF[:, bass.ds(m, 1), 0:SEQ].rearrange("p a n -> p (a n)")), pr, GQ[:, 0:1],
                                     prompt2(RR[:, 0:SEQ]), ALU.mult, ALU.mult)
            for e in range(2):
                h = slice(64 * e, 64 * e + 64)
                c = 16 * s + 8 * e
                ins = dve.scalar_tensor_tensor(
                    QZ[h, :, bass.ds(m, 1), c:c + NQ].rearrange("p b a q -> p (b a) q"),
                    sa[h].rearrange("p (b q) -> p b q", b=NB), GQ[h, 0:1],
                    RR[h, SEQ:TOK].rearrange("p (b q) -> p b q", b=NB), ALU.mult, ALU.mult)
            ins.then_inc(q_out, 1)

        with dve.Fori(0, KT // 2 - 1) as j:
            for s in range(2):
                query(2 * j + s, s)
        query(KT - 2, 0)
        dve.wait_ge(s_fn, 1)
        ch.link(dve.tensor_copy(LFN[:, 0:QB, :], PS[:, T0, 0:QB * H].rearrange("p (t h) -> p t h", h=H)))
        ch.link(dve.tensor_copy(LFN[0:NS, QB, :], PS[0:NS, T0, QB * H:NT * H]))
        dve.tensor_copy(FQN[:, :, :], PS[:, T0, 128:128 + QB * H].rearrange("p (t h) -> p t h", h=H)).then_inc(s_fnr, 1)
        query(KT - 1, 1)
        dve.wait_ge(s_ck, 16)
        qd = CT[:, C_QD:C_QD + NS]
        ch.link(dve.tensor_tensor(KS[:, 0, :], CK[:, :], qd, ALU.mult))
        ch.link(dve.tensor_reduce(CQ[:, :], KS[:, 0, :].rearrange("p (b q) -> p b q", b=NB), AX, ALU.add))

        done_b = ch.n

        def heads(i, last):
            ch.loop(i, LINKS["dve_b"], done_b)
            t1 = [0]

            def turned1(out, src):
                dve.wait_ge(b_t1, 24 * i + t1[0] + 1)
                t1[0] += 1
                return dve.tensor_copy(out, src)

            def add_suffix(u):
                free, bank = ((b_c0f, C0), (b_c1f, C1))[u % 2]
                dve.tensor_tensor_reduce(
                    SS[:, u * 256:(u + 1) * 256], PS[:, bank, 0:256],
                    SFX[:, (u // 2) % 2, (u % 2) * 256:(u % 2) * 256 + 256],
                    1.0, NEG, ALU.add, ALU.max, TINY[:, 4 + u:5 + u]).then_inc(free, 1)

            for k in range(NPG):
                c = (k % 2) * PAGE
                if k % 2 and k >= 3:
                    u = k // 2 - 1
                    if u % 2 == 0:
                        dve.wait_ge(b_sfx[(u // 2) % 2], (2 * i + u // 4 + 1) * 16)
                    dve.wait_ge((b_c0, b_c1)[u % 2], 8 * i + u // 2 + 1)
                turned1(KTS[k // 2 % 2][:, 4:8, c:c + PAGE],
                        PS[:, T1, :].rearrange("p (k n) -> p k n", k=4)).then_inc(b_t1f, 1)
                if k % 2 and k >= 3:
                    add_suffix(k // 2 - 1)
                if k == 6:
                    dve.wait_ge(b_proj, KT + 3 * i + 1)
                    pr, sa = both(D0)
                    gk = GAIN[:, G_K:G_K + 1]
                    dve.tensor_scalar(prompt2(KN_T[:, 0:SEQ]), pr, gk, None, ALU.mult)
                    dve.tensor_scalar(KN_T[:, SEQ:TOK], sa, gk, None, ALU.mult).then_inc(b_ddve, 1)
                if k == 11:
                    low_b(KT + 3 * i + 2, 1)
                if k == 13:
                    dve.wait_ge(b_normed, i + 1)
                    dve.tensor_copy(KS[:, bass.ds(i, 1), :].rearrange("p a n -> p (a n)"), KN_T[:, SEQ:TOK]).then_inc(b_kst, 1)
            dve.wait_ge(s_fnr, 1)
            dve.wait_ge(b_c1, 8 * i + 4)
            add_suffix(NPG // 2 - 1)
            dve.wait_ge(b_c0f, 8 * i + 4)
            dve.wait_ge(b_c1f, 8 * i + 4)
            cq = CQ[:, bass.ds(i, 1)]
            ms = MS[:, bass.ds(i, 1)]
            ch.link(dve.tensor_reduce(TINY[:, 12:13], TINY[:, 4:12], AX, ALU.max))
            ch.link(dve.tensor_tensor(ms, TINY[:, 12:13], cq, ALU.add))
            dve.tensor_tensor(TINY[:, 13:14], cq, ms, ALU.subtract).then_inc(b_nbs, 1)
            dve.wait_ge(b_kso, 16 * i)
            turned1(KN[0:NS, QB, :], PS[0:NS, T1, 0:P]).then_inc(b_t1f, 1)
            turned1(VS[:, bass.ds(i * P, P)], PS[0:NS, T1, 0:P]).then_inc(b_t1f, 1)

            if not last:
                low_b(KT + 3 * i + 3, 0)

            def block_max(r):
                w = (QB - r) * P
                c = 20 + 20 * (r % 2)
                dve.wait_ge(b_c0, 8 * i + 4 + r + 1)
                dve.wait_ge(b_c1, 8 * i + 4 + r + 1)
                if r >= 2:
                    dve.wait_ge(b_t0, 24 * i + 19 + r)
                    dve.wait_ge(b_t1, 24 * i + 19 + r)
                fq = TINY[:, c + 10:c + 12]
                dve.tensor_copy(fq, FQN[:, QB - 1 - r, bass.ds(2 * i, 2)]).then_inc(b_fq, 1)
                for e, (free, bank) in enumerate(((b_c0f, C0), (b_c1f, C1))):
                    dve.tensor_tensor_reduce(PB[r % 2][:, e, 0:w], PS[:, bank, 0:w], FB[:, e, 0:w], 1.0, NEG,
                                             ALU.subtract, ALU.max, TINY[:, c + e:c + e + 1]).then_inc(free, 1)
                dve.wait_ge(b_fq, 4 * i + r + 1)
                dve.wait_ge(b_c0f, 8 * i + 4 + r + 1)
                dve.wait_ge(b_c1f, 8 * i + 4 + r + 1)
                ch.link(dve.tensor_tensor(TINY[:, c + 2:c + 4], TINY[:, c:c + 2], fq, ALU.add))
                dve.tensor_tensor(TINY[:, c + 4:c + 6], fq, TINY[:, c + 2:c + 4], ALU.subtract).then_inc(b_nbp, 1)

            def block_divide(r):
                w = (QB - r) * P
                c = 20 + 20 * (r % 2)
                dve.wait_ge(b_ep, 8 * i + 2 * r + 2)
                ch.link(dve.reciprocal(TINY[:, c + 8:c + 10], TINY[:, c + 6:c + 8]))
                for e in range(2):
                    dve.tensor_scalar(PB[r % 2][:, e, 0:w], PB[r % 2][:, e, 0:w], TINY[:, c + 8 + e:c + 9 + e], None,
                                      ALU.mult).then_inc(b_pn, 1)

            def block_turned(r):
                w = (QB - r) * P
                turned1(PT[:, 1, 0:QB - r, :], PS[:, T1, 0:w].rearrange("p (k n) -> p k n", n=P)).then_inc(b_t1f, 1)

            dve.wait_ge(b_fb, 16 * (i + 1))
            block_max(0)
            for g in (1, 3):
                turned1(PTS[:, 4 * g:4 * g + 4, :], PS[:, T1, :].rearrange("p (k n) -> p k n", k=4)).then_inc(b_t1f, 1)
            dve.wait_ge(b_es, 4 * i + 4)
            dve.tensor_reduce(LS[:, bass.ds(i, 1)], TINY[:, 16:20], AX, ALU.add).then_inc(b_lp, 1)
            block_max(1)
            block_divide(0)
            block_turned(0)
            block_max(2)
            block_divide(1)
            block_turned(1)
            block_divide(2)
            block_max(3)
            pr, sa = both(D0)
            dve.wait_ge(b_zl, i + 1)
            dve.scalar_tensor_tensor(prompt2(SZ[:, 0:SEQ]), pr, 0.0, prompt2(SZ[:, 0:SEQ]), ALU.min, ALU.subtract)
            dve.scalar_tensor_tensor(SZ[:, SEQ:TOK], sa, 0.0, SZ[:, SEQ:TOK], ALU.min, ALU.subtract).then_inc(b_zm, 1)
            block_turned(2)
            block_divide(3)
            block_turned(3)
            dve.wait_ge(b_ze, i + 1)
            dve.tensor_tensor(SZS[:, bass.ds(i, 1), :].rearrange("p a n -> p (a n)"), sa, SZ[:, SEQ:TOK], ALU.mult)
            dve.tensor_tensor(prompt2(SZ[:, 0:SEQ]), pr, prompt2(SZ[:, 0:SEQ]), ALU.mult).then_inc(b_sz, 1)
            if not last:
                low_b(KT + 3 * i + 4, 1)
            assert t1[0] == 24
            dve.wait_ge(b_po, i + 1)
            dve.wait_ge(b_sz, i + 1)
            dve.tensor_tensor(SQ[:, 0:SEQ], PS[:, OP, :], SZ[:, 0:SEQ], ALU.mult).then_inc(b_gf, 1)
            dve.wait_ge(b_gh, i + 1)
            gl = GL[:, bass.ds(i, 1), 0:SEQ].rearrange("p a n -> p (a n)")
            gh = GH[:, bass.ds(i, 1), 0:SEQ].rearrange("p a n -> p (a n)")
            dve.tensor_tensor(gl, SQ[:, 0:SEQ], gh.bitcast(F32), ALU.subtract).then_inc(b_gl, 1)
            ch.end()

        with dve.Fori(0, NB - 1) as i:
            heads(i, False)
        heads(NB - 1, True)
        ch.base, ch.n = 0, done_b + LINKS["dve_b"] * NB

        nm = CT[:, C_NM:C_NM + NB * NS].rearrange("p (b n) -> p b n", b=NB)
        ch.link(dve.tensor_tensor(NBI[:, :, :], nm, CK[:, :].unsqueeze(1).to_broadcast([P, NB, NS]), ALU.subtract))
        dve.wait_ge(m_s, 1)
        ch.link(dve.tensor_tensor(SN[:, :, :], PS[:, C0, :].rearrange("p (b n) -> p b n", b=NB), NBI[:, :, :], ALU.add))
        tn = TINY
        ch.link(dve.tensor_reduce(tn[:, 4:12], SN[:, :, :], AX, ALU.max))
        ch.link(dve.tensor_tensor(tn[:, 4:12], tn[:, 4:12], CQ[:, :], ALU.add))
        ch.link(dve.tensor_tensor(tn[:, 4:12], tn[:, 4:12], MS[:, :], ALU.max))
        ch.link(dve.tensor_tensor(tn[:, 40:48], MS[:, :], tn[:, 4:12], ALU.subtract))
        dve.tensor_tensor(tn[:, 48:56], CQ[:, :], tn[:, 4:12], ALU.subtract).then_inc(m_exp, 1)
        dve.wait_ge(m_a, 1)
        ch.link(dve.tensor_tensor(LS[:, :], LS[:, :], tn[:, 40:48], ALU.mult))
        dve.wait_ge(m_p, NB)
        ch.link(dve.tensor_tensor(LS[:, :], LS[:, :], tn[:, 56:64], ALU.add))
        ch.link(dve.reciprocal(LS[:, :], LS[:, :]))
        dve.wait_ge(m_t, 2)
        dve.tensor_copy(PNT[:, 4:8, :], PS[0:NS, T1, :].rearrange("p (k n) -> p k n", k=4)).then_inc(m_td, 1)
        low_slab(NSLAB, 0)
        for b in range(NB):
            dve.wait_ge(m_pv, b // 2 + 1)
            ch.link(dve.scalar_tensor_tensor(OM[:, b, :], OPAST[:, b, :], tn[:, 40 + b:41 + b],
                                             PS[:, C0 + b // 2, (b % 2) * 256:(b % 2) * 256 + 256], ALU.mult, ALU.add))
            dve.tensor_scalar(OM[:, b, :], OM[:, b, :], LS[:, b:b + 1], None, ALU.mult).then_inc(m_om, 1)
        for b in range(0, NB, 2):
            dve.wait_ge(m_ot, b // 2 + 1)
            for ii2 in range(2):
                for e in range(2):
                    pr = slice(64 * e, 64 * e + 64)
                    src = PS[pr, (D0, D1, T0, T1)[b // 2], :].rearrange(
                        "p (b a j c) -> p a b j c", b=2, a=2, j=4)[:, ii2, :, :, 8 * (2 * ii2 + e):8 * (2 * ii2 + e) + NQ]
                    sel = lambda z: z[pr, :, b * NQ:(b + 2) * NQ].rearrange(
                        "p (j a) (b q) -> p a b j q", a=2, b=2)[:, ii2]
                    ins = dve.tensor_tensor(sel(GS), src, sel(SZS), ALU.mult)
        ins.then_inc(m_gs, 1)
        dve.wait_ge(m_gh, 1)
        dve.tensor_tensor(GL[:, :, SEQ:TOK], GS[:, :, :], GH[:, :, SEQ:TOK].bitcast(F32), ALU.subtract).then_inc(m_gl, 1)
        low_slab(NSLAB + 1, 1)
        dve.wait_ge(s_hld, 16 * NT)
        base = 5 * NSLAB
        with dve.Fori(0, NSLAB // 2 - 1) as j:
            for s in range(2):
                for t in range(NT):
                    out_tile(5 * s + t + 10 * j + base, 2 * j + s, s, t)
                low_slab(2 * j + s + 2 + NSLAB, s)
        for s in range(2):
            for t in range(NT):
                out_tile(5 * (NSLAB - 2 + s) + t + base, NSLAB - 2 + s, s, t)

    @block.tensor
    def _(pe):
        def turn(out, src, r=P):
            return pe.transpose(out, src, CT[0:r, C_ID:C_ID + r])

        pe.wait_ge(s_const, 16)
        pe.wait_ge(s_rows, 16 * 11)
        turn(PS[:, 6, 0:G_ALL], GR[:, :], G_ALL).then_inc(s_gt, 1)
        for k in range(KT):
            mm = turn(PS[:, 7, 128 + 16 * k:144 + 16 * k], STN[:, k * P:(k + 1) * P], 2 * NB)
        mm.then_inc(s_stt, 1)

        def norm_turn(t, phase):
            n = NT * phase + t
            b = 2 * (n % 3)
            pe.wait_ge(s_xs, n + 1)
            if n >= 3:
                pe.wait_ge(s_xl, n - 2)
            for k in range(KT):
                mm = turn(PS[:, b + k // 4, (k % 4) * P:(k % 4) * P + rows(t)], XS[0:rows(t), k * P:(k + 1) * P], rows(t))
            mm.then_inc(s_xt, 1)

        for t in range(NT):
            norm_turn(t, 0)
        def piece(slot, k, bank, weights=None):
            wh, wl = weights or (WH[:, slot, :, :], WL[:, slot, :, :])
            for n, (w, x) in enumerate(((wh, XH), (wh, XL), (wl, XH))):
                for h, c in enumerate((slice(0, HALF), slice(HALF, TOK))):
                    mm = pe.matmul(PS[:, bank + h, 0:c.stop - c.start], w[:, k, :], x[:, k, c],
                                   start=(k == 0 and n == 0), stop=(k == KT - 1 and n == 2))
            return mm

        pe.wait_ge(s_xl, NT)
        pe.wait_ge(s_st, 1)

        def mixer(i):
            for q in range(4):
                pe.wait_ge(a_split, 4 * i + q + 1)
                pe.wait_ge((a_c, a_v, a_z, a_g)[q], i)
                for k in range(KT):
                    mm = piece(q % 2, k, 2 * q)
                mm.then_inc(a_proj, 1)

        with pe.Fori(0, KT) as i:
            mixer(i)
        pe.wait_ge(s_cs, H)
        pe.wait_ge(a_g, KT)
        pe.matmul(PS[:, 7, 0:H], CT[:, C_TRI:C_TRI + P], CS[:, :, PAGE - 1], start=True, stop=True).then_inc(s_rtot, 1)
        pe.wait_ge(a_gl, KT)

        def out_slab(g, s, n, w, first=False):
            pe.wait_ge(l_split, g + 1)
            for t in range(NT):
                r = rows(t)
                if not first:
                    pe.wait_ge(l_evac, n + t - 1)
                for k in range(KT):
                    for p, (wp, x) in enumerate(((slab_h[w], GH), (slab_h[w], GL), (slab_l[w], GH))):
                        mm = pe.matmul(PS[0:r, (5 * s + t) % 8, 0:SLAB], x[:, k, toks(t)], wp[:, k, :],
                                       start=(k == 0 and p == 0), stop=(k == KT - 1 and p == 2))
                mm.then_inc(l_tile, 1)

        out_slab(0, 0, 0, 1, True)
        pe.wait_ge(s_sfx, 1)
        out_slab(1, 1, 5, 0)
        with pe.Fori(1, NSLAB // 2) as j:
            for s in range(2):
                out_slab(2 * j + s, s, 10 * j + 5 * s, 1 - s)
        pe.wait_ge(l_evac, 5 * NSLAB)
        for t in range(NT):
            norm_turn(t, 1)
        pe.wait_ge(s_xl, 2 * NT)
        for k in range(KT):
            mm = turn(PS[0:18, 6 + k // 4, (k % 4) * P:(k % 4 + 1) * P], CST[:, k, :])
        mm.then_inc(s_ctt, 1)
        pe.wait_ge(s_wfl, 1)
        for k in range(KT):
            for w, x in ((WFH, XH), (WFH, XL), (WFL, XH)):
                for h, c in enumerate((slice(0, HALF), slice(HALF, TOK))):
                    mm = pe.matmul(PS[0:H, 2 + h, 0:c.stop - c.start], w[:, k, :], x[:, k, c],
                                   start=(k == 0 and w is WFH and x is XH), stop=(k == KT - 1 and w is WFL))
        mm.then_inc(s_fp, 1)

        def q_sum():
            pe.matmul(PS[:, OS, 0:NS], CT[:, C_ONESB:C_ONESB + P], SQ[:, SEQ:TOK], start=True, stop=True)
            pe.matmul(PS[:, OP, :], CT[:, C_ONESB:C_ONESB + P], SQ[:, 0:SEQ], start=True, stop=True).then_inc(q_ss, 1)

        def query(m, s, first=False):
            pe.wait_ge(b_split, m + 1)
            if not (first and m == 0):
                pe.wait_ge(q_out, m - 1)
            for k in range(KT):
                mm = piece(s, k, C0 * s, first_q[m] if first else None)
                if k == 2 and not (first and m == 0):
                    pe.wait_ge(q_sq, m)
                    pe.wait_ge(q_rr, m - 1)
                    q_sum()
            mm.then_inc(b_proj, 1)

        query(0, 0, True)
        pe.wait_ge(s_co, 1)
        query(1, 1, True)
        with pe.Fori(1, KT // 2 - 1) as j:
            for s in range(2):
                query(2 * j + s, s)
        query(KT - 2, 0)
        pe.wait_ge(s_ft, 1)
        for t in range(NT):
            turn(PS[0:rows(t), T0, t * H:(t + 1) * H], FL[:, toks(t)], H)
        for t in range(QB):
            mm = turn(PS[:, T0, 128 + t * H:128 + (t + 1) * H], FT[:, toks(t)], H)
        mm.then_inc(s_fn, 1)
        query(KT - 1, 1)
        pe.wait_ge(q_sq, KT)
        pe.wait_ge(q_rr, KT - 1)
        q_sum()
        pe.wait_ge(s_fnr, 1)

        def heads(i):
            t0, t1 = [0], [0]

            def free0():
                pe.wait_ge(b_t0f, 24 * i + t0[0])
                t0[0] += 1

            def free1():
                pe.wait_ge(b_t1f, 24 * i + t1[0])
                t1[0] += 1

            def project(q, ks):
                if ks[0] == 0:
                    pe.wait_ge(b_split, KT + 3 * i + (2, 1, 3)[q])
                    if q == 0:
                        pe.wait_ge(b_sz, i)
                    else:
                        pe.wait_ge(b_dact, 2 * i + q)
                    if q == 1:
                        pe.wait_ge(b_ddve, i + 1)
                for k in ks:
                    mm = piece((1, 0, 1)[q], k, D0)
                if ks[-1] == KT - 1:
                    mm.then_inc(b_proj, 1)

            def unit_scores(u):
                full, free, bank = ((b_c0, b_c0f, C0), (b_c1, b_c1f, C1))[u % 2]
                if u == 0:
                    pe.wait_ge(b_qc, i + 1)
                    pe.wait_ge(q_out, KT)
                pe.wait_ge(free, 8 * i + u // 2)
                pe.wait_ge(b_t0f, 24 * i + 2 * u + 2)
                pe.wait_ge(b_t1f, 24 * i + 2 * u + 2)
                for pp in range(2):
                    for j in range(4):
                        mm = pe.matmul(PS[32 * j:32 * j + 32, bank, 0:256], QC[:, 2 * j + pp, :],
                                       KTS[u % 2][:, 2 * j + pp, :],
                                       start=(pp == 0), stop=(pp == 1), tile_position=(0, 32 * j))
                mm.then_inc(full, 1)

            for k in range(NPG):
                pe.wait_ge(b_page[k % RING], (4 * i + k // RING + 1) * 16)
                page = ring[:, k % RING, :]
                free0()
                for p in range(4):
                    mm = turn(PS[:, T0, p * P:(p + 1) * P], page[:, p * P:(p + 1) * P])
                mm.then_inc(b_t0, 1)
                free1()
                for p in range(4):
                    mm = turn(PS[:, T1, p * P:(p + 1) * P], page[:, (4 + p) * P:(5 + p) * P])
                mm.then_inc(b_t1, 1)
                if k == 9:
                    pe.wait_ge(b_dact, 2 * i + 1)
                    pe.wait_ge(b_gf, i)
                    pe.wait_ge(b_sot, i)
                    pe.matmul(PS[:, OS, 0:NS], CT[:, C_ONESB:C_ONESB + P], SQ[:, SEQ:TOK], start=True, stop=True)
                    pe.matmul(PS[:, OP, :], CT[:, C_ONESB:C_ONESB + P], SQ[:, 0:SEQ], start=True, stop=True).then_inc(b_ss, 1)
                if k < 6:
                    project(0, ([0, 1], [2, 3], [4], [5], [6], [7])[k])
                if 7 <= k < 15:
                    project(1, [k - 7])
                if k % 2 == 0 and k >= 2:
                    unit_scores(k // 2 - 1)

            def block_scores(r):
                s = QB - 1 - r
                w = (s + 1) * P
                for e, (full, free, bank) in enumerate(((b_c0, b_c0f, C0), (b_c1, b_c1f, C1))):
                    pe.wait_ge(free, 8 * i + 4 + r)
                    pr = slice(64 * e, 64 * e + 64)
                    if s:
                        pe.matmul(PS[:, bank, 0:w - P], QT[pr, toks(s)], KN_T[pr, 0:w - P], start=True, stop=True)
                    pe.matmul(PS[:, bank, w - P:w], QT[pr, toks(s)], KN_T[pr, toks(s)], start=True, stop=False)
                    pe.matmul(PS[:, bank, w - P:w], IDB[:, :], CMB[:, :], start=False, stop=True).then_inc(full, 1)

            def block_turn(r):
                for e in range(2):
                    pe.wait_ge(b_pn, 8 * i + 2 * r + e + 1)
                    (free0, free1)[e]()
                    for kb in range(QB - r):
                        mm = turn(PS[:, T0 + e, kb * P:(kb + 1) * P], PB[r % 2][:, e, kb * P:(kb + 1) * P])
                    mm.then_inc((b_t0, b_t1)[e], 1)

            def block_out(r):
                s = QB - 1 - r
                pe.wait_ge(b_t0f, 24 * i + 21 + r)
                pe.wait_ge(b_t1f, 24 * i + 21 + r)
                for kb in range(s + 1):
                    for e in range(2):
                        mm = pe.matmul(PS[64 * e:64 * e + 64, OP, toks(s)], VN[:, kb, 64 * e:64 * e + 64],
                                       PT[:, e, kb, :], start=(kb == 0), stop=(kb == s))
                if r == QB - 1:
                    mm.then_inc(b_po, 1)

            project(2, [0])
            unit_scores(NPG // 2 - 1)
            project(2, [1])
            pe.wait_ge(b_normed, i + 1)
            for src in (KN_T, VT):
                free0()
                free1()
                for t in range(QB):
                    mm = turn(PS[:, T0, t * P:(t + 1) * P], src[:, toks(t)])
                mm.then_inc(b_t0, 1)
                turn(PS[0:NS, T1, 0:P], src[:, SEQ:TOK]).then_inc(b_t1, 1)
                if src is KN_T:
                    project(2, [2])
            pe.wait_ge(b_qt, i + 1)
            block_scores(0)
            project(2, [3])
            for g in range(4):
                pe.wait_ge(b_es, 4 * i + g + 1)
                (free0, free1)[g % 2]()
                for p in range(4):
                    c = (4 * g + p) * P
                    mm = turn(PS[:, T0 + g % 2, p * P:(p + 1) * P], SS[:, c:c + P])
                mm.then_inc((b_t0, b_t1)[g % 2], 1)
                if g == 1:
                    project(2, [4])
            steps = {0: [(block_scores, 1)], 3: [(block_turn, 0)], 4: [(block_scores, 2)], 5: [(block_out, 0)],
                     7: [(block_turn, 1)], 8: [(block_scores, 3), (block_out, 1)], 10: [(block_turn, 2)],
                     12: [(block_out, 2)], 13: [(block_turn, 3)], 15: [(block_out, 3)]}
            for k in range(NPG):
                for step, r in steps.get(k, []):
                    step(r)
                if k in (1, 2, 4):
                    project(2, [{1: 5, 2: 6, 4: 7}[k]])
                n = NPG + k
                pe.wait_ge(b_page[n % RING], (4 * i + n // RING + 1) * 16)
                if k == 0:
                    pe.wait_ge(b_ln, i + 1)
                if k % 4 == 0:
                    g = k // 4
                    pe.wait_ge((b_t0f, b_t1f)[g % 2], 24 * i + 19 + g // 2)
                for j in range(4):
                    mm = pe.matmul(PS[32 * j:32 * j + 32, OS, 0:4 * HD], PTS[:, k, 32 * j:32 * j + 32],
                                   ring[:, n % RING, 4 * HD * j:4 * HD * (j + 1)],
                                   start=(k == 0), stop=(k == NPG - 1), tile_position=(0, 32 * j))
                mm.then_inc(b_used, 1)
            assert t0[0] == t1[0] == 24

        with pe.Fori(0, NB) as i:
            heads(i)

        pe.wait_ge(b_kst, NB)
        pe.wait_ge(b_c0f, 8 * NB)
        pe.wait_ge(b_c1f, 8 * NB)
        pe.wait_ge(b_gf, NB)
        pe.wait_ge(b_sz, NB)
        for b in range(NB):
            for pp in range(2):
                for j in range(4):
                    mm = pe.matmul(PS[32 * j:32 * j + 32, C0, b * NS:(b + 1) * NS], QZ[:, b, 2 * j + pp, :],
                                   KS[:, 2 * j + pp, :], start=(pp == 0), stop=(pp == 1), tile_position=(0, 32 * j))
        mm.then_inc(m_s, 1)
        for b in range(NB):
            pe.wait_ge(m_p, b + 1)
            mm = turn(PS[0:NS, T0 + b // 4, (b % 4) * P:(b % 4 + 1) * P], SN[:, b, :])
            if b % 4 == 3:
                mm.then_inc(m_t, 1)
        pe.wait_ge(m_ta, 1)
        pe.wait_ge(m_td, 1)
        pe.wait_ge(b_sot, NB)
        for b in range(NB):
            for j in range(4):
                mm = pe.matmul(PS[32 * j:32 * j + 32, C0 + b // 2, (b % 2) * 256:(b % 2) * 256 + 256],
                               PNT[:, b, 32 * j:32 * j + 32], VS[:, 4 * HD * j:4 * HD * (j + 1)],
                               start=True, stop=True, tile_position=(0, 32 * j))
            if b % 2:
                mm.then_inc(m_pv, 1)
        for b in range(NB):
            pe.wait_ge(m_om, b + 1)
            for a in range(2):
                mm = turn(PS[:, (D0, D1, T0, T1)[b // 2], (2 * (b % 2) + a) * P:(2 * (b % 2) + a + 1) * P],
                          OM[:, b, a * P:(a + 1) * P])
            if b % 2:
                mm.then_inc(m_ot, 1)
        pe.wait_ge(m_gl, 1)
        with pe.Fori(0, NSLAB // 2) as j:
            for s in range(2):
                out_slab(2 * j + s + NSLAB, s, 10 * j + 5 * s + 5 * NSLAB, s)


_INS = ['x_prompt', 'x_sample', 'state_conv', 'cache_k', 'cache_v', 'cache_logf', 'page_table',
        'a_norm', 'a_w_in', 'a_conv', 'a_w_out', 'kv_norm', 'kv_w', 'kv_fbias', 'k_norm',
        'b_norm', 'b_w_in', 'q_norm', 'b_w_out']
_OUTS = [('y_prompt', (1, SEQ, D)), ('y_sample', (NB, NQ, D)), ('conv_prompt', (1, 1, CONV_W - 1, D)),
         ('conv_sample', (1, NB, CONV_W - 1, D)), ('k_prompt', (1, SEQ, H, HD)), ('v_prompt', (1, SEQ, H, HD)),
         ('logf_prompt', (1, SEQ, H)), ('k_sample', (NB, NQ, H, HD)), ('v_sample', (NB, NQ, H, HD)),
         ('logf_sample', (NB, NQ, H))]


def constants():
    import numpy as np

    c = np.zeros((P, C_ALL), np.float32)
    p = np.arange(P)
    c[:, C_ID:C_ID + P] = np.eye(P)
    c[:, C_ONESB:C_ONESB + P] = p[:, None] // HD == p[None] // HD
    same = p[:, None] // NPG == p[None] // NPG
    c[:, C_TRI:C_TRI + P] = same & (p[:, None] >= p[None])
    c[:, C_CM:C_CM + P] = np.where(p[None] <= p[:, None], 0.0, NEG)
    key = np.arange(NS)
    for b in range(NB):
        ok = (key[None] // NQ == b) & (key[None] % NQ <= p[:, None] % NQ)
        c[:, C_NM + b * NS:C_NM + (b + 1) * NS] = np.where(ok, 0.0, NEG)
    c[:, C_QD:C_QD + NS] = key[None] % NQ == p[:, None] % NQ
    c[:, C_RST:C_RST + NS] = key[None] % NQ != 0
    c[:, C_ONE] = 1.0
    return c


def kernel(**inputs):
    import numpy as _np
    import concourse.bacc as _bacc
    from concourse import mybir as _mybir
    from concourse.bass_utils import run_bass_kernel_spmd as _run

    nc = _bacc.Bacc("TRN2", target_bir_lowering=False, num_devices=1, dynamic_dma_scratch_size=4096)
    arrays, args = {}, {}
    given = {n: _np.ascontiguousarray(inputs[n]) for n in _INS}
    given["table"] = constants()
    for name, a in given.items():
        arrays[f"in_{name}"] = a
        args[name] = nc.dram_tensor(f"in_{name}", a.shape, _mybir.dt.from_np(a.dtype), kind="ExternalInput").ap()
    for name, shape in _OUTS:
        args[name] = nc.dram_tensor(f"out_{name}", shape, _mybir.dt.float32, kind="ExternalOutput").ap()
    with ExitStack() as ctx:
        build(nc, ctx, **args)
    r = _run(nc, [arrays], core_ids=[0])
    return tuple(r.results[0][f"out_{name}"] for name, _ in _OUTS)
```

```python
from contextlib import ExitStack

import concourse.bass as bass
from concourse import mybir

F32 = mybir.dt.float32
F32R = mybir.dt.float32r
BF16 = mybir.dt.bfloat16
I32 = mybir.dt.int32
ALU = mybir.AluOpType
ACT = mybir.ActivationFunctionType
AX = mybir.AxisListType.X

P = 128
D = 1024
KT = D // P
SEQ = 512
NB = 8
NQ = 8
NS = NB * NQ
TOK = SEQ + NS
H = 16
HD = 64
CONV_W = 3
PAGE = 128
NPG = 16
PAST = NPG * PAGE
QB = SEQ // P
EPS = 1e-6
NT = 5
HALF = 256
TAIL = TOK - HALF
NEG = -1e30
RING = 8
STREAM = 2 * NPG
SLAB = 256
NSLAB = D // SLAB

C_ID, C_ONESB, C_TRI, C_CM, C_NM, C_QD, C_RST, C_ONE = 0, 128, 256, 384, 512, 1024, 1088, 1152
C_ALL = 1153
G_A, G_KV, G_B, G_CONV, G_K, G_Q = 0, 8, 16, 24, 48, 49
G_ALL = 50


def rows(t):
    return P if t < QB else NS


def toks(t):
    return slice(t * P, t * P + rows(t))


NORM_BANKS = (0, 2, 4, 0, 2) + (2, 4, 2, 4, 2)
NORM_BANKS_FREE = {3: 1, 4: 2, 7: 6, 8: 7, 9: 8}

EARLY = ((0, 0), (0, 1), (0, 2), (0, 3), (1, 0), (1, 1), (1, 2), (0, 4), (1, 3), (1, 4))


class Chain:

    def __init__(self, eng, sem):
        self.eng, self.sem, self.base, self.n = eng, sem, 0, 0

    def link(self, ins):
        self.n += 1
        ins.then_inc(self.sem, 1)
        self.eng.wait_ge(self.sem, self.base + self.n)

    def loop(self, i, per, done):
        self.base, self.n, self.per = i * per + done, 0, per

    def end(self):
        assert self.n == self.per, (self.n, self.per)


def build(nc, ctx, x_prompt, x_sample, state_conv, cache_k, cache_v, cache_logf, page_table,
          a_norm, a_w_in, a_conv, a_w_out, kv_norm, kv_w, kv_fbias, k_norm,
          b_norm, b_w_in, q_norm, b_w_out, table,
          y_prompt, y_sample, conv_prompt, conv_sample, k_prompt, v_prompt, logf_prompt,
          k_sample, v_sample, logf_sample):
    n_pool = cache_k.shape[0]

    suffix_dram = nc.dram_tensor("suffix_scratch", [NB, H, PAST], F32, kind="Internal").ap()
    f_dram = nc.dram_tensor("f_scratch", [H, TOK], F32, kind="Internal").ap()
    h_dram = nc.dram_tensor("h_scratch", [NT * P, D], F32, kind="Internal").ap()

    at = {"top": nc.sbuf_base + (-nc.sbuf_base) % 32}

    def place(name, shape, dt=F32, over=None):
        n = 4 if dt is not BF16 else 2
        for s in shape[1:]:
            n *= s
        n += (-n) % 32
        off = at["top"] if over is None else over
        if over is None:
            at["top"] += n
        at[name] = off
        return nc.alloc_sbuf_tensor_at(name, shape, dt, offset=off)

    XH = place("xn_high", [P, KT, TOK], F32R)
    XL = place("xn_low", [P, KT, TOK], F32R)
    GH = place("gated_high", [P, KT, TOK], F32R)
    GL = place("gated_low", [P, KT, TOK], F32R)
    WH = place("w_high", [P, 2, KT, P], F32R)
    WL = place("w_low", [P, 2, KT, P], F32R)
    WR = place("w_raw", [P, 2, KT, P])
    ring = place("page_ring", [P, RING, D])
    KTS = [place("k_turned", [P, KT, 2 * PAGE])]
    PTS = place("p_turned", [P, NPG, P])
    KTS.append(place("k_turned_odd", [P, KT, 2 * PAGE], over=at["p_turned"]))
    SS = place("sample_scores", [P, PAST])
    SFX = place("suffix", [P, 2, 512])
    QZ = place("q_spread", [P, NB, KT, 32])
    CT = place("constants", [P, C_ALL])
    QT = place("q_t", [P, SEQ])
    KN_T = place("k_t", [P, TOK])
    VT = place("v_t", [P, TOK])
    SZ = place("silu_z", [P, TOK])
    SQ = place("squares", [P, TOK])
    RR = place("rsqrt", [P, TOK])
    KN = place("k_rows", [P, NT, P])
    VN = place("v_rows", [P, QB, P])
    FB = place("f_broad", [P, 2, SEQ])
    PB = [place("probs", [P, 2, SEQ]), place("probs_odd", [P, 2, SEQ - P], over=at["squares"])]
    PT = place("probs_t", [P, 2, QB, P])
    OPAST = place("o_past", [P, NB, 4 * HD])
    KS = place("ks_t", [P, KT, NS])
    VS = place("vs_rows", [NS, D])
    SZS = place("silu_zs", [P, KT, NS])
    GAIN = place("gains", [P, G_ALL])
    GQ = place("gain_q", [P, 1])
    IDB = place("ident_b", [P, P], BF16)
    CMB = place("causal_b", [P, P], BF16)
    CST = place("conv_tail", [P, KT, 18])
    ST = place("conv_state", [P, KT, 2 * NB])
    LFN = place("logf_rows", [P, NT, H])
    FQN = place("f_rows", [P, QB, H])
    CK = place("f_new", [P, NS])
    CQ = place("f_query", [P, NB])
    TINY = place("tiny", [P, 64])
    WFR = place("wf_raw", [P, KT, H], over=at["squares"])
    WFH = place("wf_high", [P, KT, H], F32R)
    WFL = place("wf_low", [P, KT, H], F32R)
    PTAB = place("page_row", [1, NB * NPG], I32)
    PIDX = place("page_column", [P, 1], I32)
    FBIAS = place("f_bias", [H, 1])
    QC = place("q_current", [P, KT, 32])
    MS = place("max_past", [P, NB])
    LS = place("sum_past", [P, NB])
    assert at["top"] <= nc.sbuf_usable_end, at["top"]
    X = place("residual", [P, NT, D], over=at["page_ring"])
    LF = place("logf_pages", [P, PAGE, H], over=at["page_ring"] + 5 * 4 * D)
    XS = [place("x_scaled", [P, D], over=at["page_ring"] + 7 * 4 * D), place("x_scaled_odd", [P, D], over=at["o_past"])]
    CS = place("logf_sums", [P, H, PAGE], over=at["sample_scores"])
    STN = place("state_rows", [2 * NB, D], over=at["suffix"])
    GR = place("gain_rows", [G_ALL, P], over=at["f_broad"])
    JUNK = place("junk", [P, D], over=at["probs"])
    EXT = place("conv_in", [P, SEQ + 2], over=at["probs"])
    EXTS = place("conv_in_s", [P, NB, NQ + 2], over=at["probs"] + 4 * (SEQ + 8))
    CO = place("conv_rows", [18, D], over=at["probs_t"])
    WHB = place("w_high_b", [P, KT, SLAB], F32R, over=at["k_turned"])
    WLB = place("w_low_b", [P, KT, SLAB], F32R, over=at["p_turned"])
    WHA = WH[:, :, :, :].rearrange("p s k n -> p (s k n)").rearrange("p (k n) -> p k n", k=KT)
    WLA = WL[:, :, :, :].rearrange("p s k n -> p (s k n)").rearrange("p (k n) -> p k n", k=KT)
    WRA = WR[:, :, :, :].rearrange("p s k n -> p (s k n)").rearrange("p (k n) -> p k n", k=KT)
    first_q = [(WHB[:, :, s * P:(s + 1) * P], WLB[:, :, s * P:(s + 1) * P]) for s in range(2)]
    slab_h = [WHA, WHB[:, :, :]]
    slab_l = [WLA, WLB[:, :, :]]
    QF = place("queries", [P, KT, TOK], over=at["gated_high"])
    FA = place("f_raw", [H, TOK], over=at["k_t"])
    FN = place("f_neg", [H, TOK], over=at["v_t"])
    FE = place("f_exp", [H, TOK], over=at["silu_z"])
    FL = place("f_log", [H, TOK], over=at["probs"])
    FT = place("f_sum", [H, TOK], over=at["f_broad"])
    SN = place("new_scores", [P, NB, NS], over=at["suffix"])
    NBI = place("new_bias", [P, NB, NS], over=at["suffix"] + 4 * NB * NS)
    PNT = place("new_probs_t", [NS, NB, P], over=at["probs"])
    OM = place("o_merged", [P, NB, 4 * HD], over=at["sample_scores"])
    GS = place("gated_s", [P, KT, NS], over=at["probs_t"])

    ident = CT[:, C_ID:C_ID + P]
    PS = ctx.enter_context(nc.psum_tensor("psum", [P, 8, 512], F32))
    D0, D1, T0, T1, C0, C1, OP, OS = range(8)

    def sem(name):
        return ctx.enter_context(nc.semaphore(name))

    s_ch_act, s_ch_dve = sem("act_chain"), sem("dve_chain")
    s_const, s_rows, s_idx = sem("constants_loaded"), sem("rows_loaded"), sem("pages_loaded")
    s_x = [sem(f"x_loaded{t}") for t in range(NT)]
    s_lf = sem("logf_gathered")
    s_cs, s_rtot, s_sfx, s_sfx_st = sem("logf_summed"), sem("later_pages"), sem("suffix_ready"), sem("suffix_stored")
    s_gt, s_gain, s_stt, s_st = sem("gains_turned"), sem("gains_ready"), sem("state_turned"), sem("state_ready")
    s_bf = sem("bf16_consts")
    s_zero, s_rms = sem("q_spread_zero"), sem("rms_ready")
    s_xs, s_xt, s_xh, s_xl = sem("x_scaled"), sem("x_turned"), sem("xn_high_ready"), sem("xn_low_ready")
    a_raw = [sem(f"a_w_loaded{s}") for s in range(2)]
    a_scaled, a_high, a_split = sem("a_w_scaled"), sem("a_w_high"), sem("a_w_split")
    a_proj, a_c, a_v, a_z, a_cvz = sem("a_projected"), sem("a_c_out"), sem("a_v_made"), sem("a_silu"), sem("a_cvz")
    a_cv, a_g, a_gh, a_gl = sem("a_conv"), sem("a_gated"), sem("a_gated_high"), sem("a_gated_low")
    l_raw, l_high, l_split = sem("slab_loaded"), sem("slab_high"), sem("slab_split")
    l_tile, l_evac = sem("out_tile"), sem("out_added")
    s_cost = sem("conv_stored")
    s_hst, s_ctt, s_co = sem("h_stored"), sem("conv_turned"), sem("conv_rows_ready")
    s_wf, s_wfs, s_wfh, s_wfl = sem("wf_loaded"), sem("wf_scaled"), sem("wf_high"), sem("wf_low")
    s_fp, s_fneg, s_fe = sem("f_projected"), sem("f_neg"), sem("f_exp")
    s_fl, s_ft, s_fst, s_fn, s_fnr = sem("f_log"), sem("f_sum"), sem("f_stored"), sem("f_turned"), sem("f_rows_ready")
    s_ck = sem("f_new_loaded")
    q_sq, q_ss, q_ln, q_rr, q_out = sem("q_squares"), sem("q_summed"), sem("q_ln"), sem("q_rsqrt"), sem("q_ready")
    b_page = [sem(f"page_loaded{s}") for s in range(RING)]
    b_used, b_qc, b_qt = sem("v_page_used"), sem("q_current_ready"), sem("q_pair_ready")
    b_raw = [sem(f"b_w_loaded{s}") for s in range(2)]
    b_scaled, b_high, b_split, b_proj = sem("b_w_scaled"), sem("b_w_high"), sem("b_w_split"), sem("b_projected")
    b_dact, b_ddve = sem("proj_out_act"), sem("proj_out_dve")
    b_t0, b_t0f, b_t1, b_t1f = sem("turn0_full"), sem("turn0_free"), sem("turn1_full"), sem("turn1_free")
    b_c0, b_c0f, b_c1, b_c1f = sem("score0_full"), sem("score0_free"), sem("score1_full"), sem("score1_free")
    b_ss, b_ln, b_rr, b_normed = sem("head_squares"), sem("head_ln"), sem("head_rsqrt"), sem("head_normed")
    b_sfx = [sem(f"suffix_loaded{s}") for s in range(2)]
    b_fb, b_nbs, b_es, b_lp, b_sot = (
        sem("f_broad_loaded"), sem("sample_bias"), sem("sample_exp"), sem("sample_sum"), sem("sample_out"))
    b_nbp, b_ep, b_pn, b_po, b_sz, b_gf, b_gh, b_gl = (
        sem("prompt_bias"), sem("prompt_exp"), sem("prompt_probs"), sem("prompt_pv"), sem("silu_z_ready"),
        sem("gated"), sem("gated_h"), sem("gated_l"))
    b_zl, b_zm, b_ze = sem("z_logs"), sem("z_exponent"), sem("z_sigmoid")
    b_kst, b_fq = sem("ks_kept"), sem("rows_f_taken")
    b_kpo, b_kso, b_vpo = sem("k_prompt_stored"), sem("k_sample_stored"), sem("v_prompt_stored")
    m_s, m_exp, m_p, m_t, m_ta, m_td, m_pv, m_om, m_ot, m_gs, m_gh, m_gl, m_a = (
        sem("new_scored"), sem("new_shifts_ready"), sem("new_probs"), sem("new_turned"), sem("new_t_act"),
        sem("new_t_dve"), sem("new_pv"), sem("merged"), sem("merged_turned"), sem("gated_s"), sem("gated_sh"),
        sem("gated_sl"), sem("past_weight"))
    s_hld = sem("h_loaded")
    s_out = sem("outputs_stored")

    LINKS = dict(dve_a=8, dve_b=10, act_b=2)

    w_in = a_w_in[0].rearrange("(k p) n -> p k n", p=P)
    wo_a = a_w_out[0].rearrange("(k p) n -> p k n", p=P)
    wkv = kv_w.rearrange("(k p) n -> p k n", p=P)
    wqz = b_w_in[0].rearrange("(k p) n -> p k n", p=P)
    wo_b = b_w_out[0].rearrange("(k p) n -> p k n", p=P)
    kpages = cache_k.rearrange("g p h d -> g p (h d)")
    vpages = cache_v.rearrange("g p h d -> g p (h d)")
    A_ORDER = (1, 2, 3, 0)

    def both(bank):
        return PS[:, bank:bank + 2, 0:HALF], PS[:, bank + 1, HALF:TAIL]

    def prompt2(ap):
        return ap.rearrange("p (a n) -> p a n", a=2)

    def gain(row):
        return GAIN[:, row:row + KT].unsqueeze(2).to_broadcast([P, KT, P])

    block = ctx.enter_context(nc.Block())

    @block.sync
    def _(sp):
        sp.dma_start(X[:, 0, :], x_prompt[0, 0:P, :]).then_inc(s_x[0], 16)
        sp.dma_start(CT[:, :], table).then_inc(s_const, 16)
        sp.dma_start(PIDX[:, :], page_table.rearrange("b (g a) -> (b g) a", a=1)).then_inc(s_idx, 16)
        sp.dma_start(X[:, 1, :], x_prompt[0, toks(1), :]).then_inc(s_x[1], 16)
        for r, v in ((G_A, a_norm[0]), (G_KV, kv_norm), (G_B, b_norm[0])):
            sp.dma_start(GR[r:r + KT, :], v.rearrange("(k p) -> k p", p=P)).then_inc(s_rows, 16)
        sp.dma_start(GR[G_CONV:G_CONV + CONV_W * KT, :],
                     a_conv[0].rearrange("j (k p) -> (j k) p", p=P)).then_inc(s_rows, 16)
        sp.dma_start(X[:, 2, :], x_prompt[0, toks(2), :]).then_inc(s_x[2], 16)
        for r, v in ((G_K, k_norm), (G_Q, q_norm[0])):
            sp.dma_start(GR[r:r + 1, :].rearrange("p (e d) -> p e d", e=2),
                          v.unsqueeze(0).unsqueeze(0).to_broadcast([1, 2, HD])).then_inc(s_rows, 16)
        sp.dma_start(STN[:, :], state_conv[0].rearrange("b s n -> (b s) n")).then_inc(s_rows, 16)
        sp.dma_start(FBIAS[:, :], kv_fbias.unsqueeze(1)).then_inc(s_rows, 16)
        sp.dma_start(PTAB[:, :], page_table.rearrange("b g -> (b g)").unsqueeze(0)).then_inc(s_rows, 16)
        for t in range(3, QB):
            sp.dma_start(X[:, t, :], x_prompt[0, toks(t), :]).then_inc(s_x[t], 16)
        sp.dma_start(X[0:NS, QB, :], x_sample.rearrange("b q n -> (b q) n")).then_inc(s_x[QB], 16)

        def load_a(i, q):
            sp.dma_start(WR[:, q % 2, :, :], w_in[:, :, bass.ds((i + A_ORDER[q] * KT) * P, P)]).then_inc(a_raw[q % 2], 16)

        for q in range(2):
            load_a(0, q)

        def mixer(i, last):
            for q in range(4):
                if last and q >= 2:
                    continue
                sp.wait_ge(a_split, 4 * i + q + 1)
                load_a(i + q // 2, (q + 2) % 4)

        with sp.Fori(0, KT - 1) as i:
            mixer(i, False)
        mixer(KT - 1, True)

        def load_slab(w, col):
            sp.dma_start(WRA, w[:, :, bass.ds(col, SLAB)]).then_inc(l_raw, 16)

        sp.wait_ge(a_split, 4 * KT)
        load_slab(wo_a, 0)
        for n in range(1, NSLAB):
            sp.wait_ge(l_split, n)
            load_slab(wo_a, n * SLAB)
            if n == 1:
                sp.wait_ge(a_gl, KT)
                sp.dma_start(WFR[:, :, :], wkv[:, :, 2 * D:2 * D + H]).then_inc(s_wf, 16)
        sp.wait_ge(s_sfx_st, 16 * NB)
        sp.wait_ge(s_st, 1)

        def load_suffix(b, c):
            src = suffix_dram[bass.ds(b, 1), :, c * 512:(c + 1) * 512].rearrange("a h n -> (a h) n")
            sp.dma_start(SFX[:, c % 2, :], src.unsqueeze(1).to_broadcast([H, NQ, 512])).then_inc(b_sfx[c % 2], 16)

        for c in range(2):
            load_suffix(0, c)

        def load_w(w, col, slot):
            sp.dma_start(WR[:, slot, :, :], w[:, :, bass.ds(col, P)]).then_inc(b_raw[slot], 16)

        sp.wait_ge(l_split, NSLAB)
        for n in range(4):
            if n >= 2:
                sp.wait_ge(b_split, n - 1)
            load_w(wqz, n * P, n % 2)
        for t in range(NT):
            sp.wait_ge(l_evac, 5 * (NSLAB - 1) + t + 1)
            sp.dma_start(h_dram[t * P:t * P + rows(t), :], X[0:rows(t), t, :]).then_inc(s_hst, 16)
        sp.wait_ge(s_co, 1)
        sp.dma_start(conv_prompt[0, 0], CO[0:2, :]).then_inc(s_cost, 16)
        sp.dma_start(conv_sample[0].rearrange("b s n -> (b s) n"), CO[2:18, :]).then_inc(s_cost, 16)

        def load_page(b, n):
            page = sp.value_load(PTAB[0:1, bass.ds(b * NPG + n % NPG, 1)], min_val=0, max_val=n_pool - 1)
            src = (kpages if n < NPG else vpages)[bass.ds(page, 1), :, :]
            sp.dma_start(ring[:, n % RING, :], src.rearrange("a p n -> (a p) n")).then_inc(b_page[n % RING], 16)

        sp.wait_ge(s_rows, 16 * 9)
        sp.wait_ge(s_cost, 32)
        sp.wait_ge(s_hst, 16 * NT)
        sp.wait_ge(s_xl, 2 * NT)
        for n in range(RING // 2):
            load_page(0, n)
        sp.wait_ge(s_ft, 1)
        sp.dma_start(f_dram, FT[:, :]).then_inc(s_fst, 16)
        sp.wait_ge(s_fst, 16)
        sp.dma_start(CK[:, :], f_dram[:, SEQ:TOK].unsqueeze(1).to_broadcast([H, NQ, NS])).then_inc(s_ck, 16)
        for n in range(4, KT + 2):
            sp.wait_ge(b_split, n - 1)
            if n < KT:
                load_w(wqz, n * P, n % 2)
                load_page(0, n)
            else:
                load_w(wkv, (D, 0)[n - KT], n % 2)
        sp.wait_ge(s_fnr, 1)
        sp.dma_start(logf_prompt[0].rearrange("(t p) h -> p t h", p=P), LFN[:, 0:QB, :]).then_inc(s_out, 16)
        sp.dma_start(logf_sample.rearrange("b q h -> (b q) h"), LFN[0:NS, QB, :]).then_inc(s_out, 16)

        def heads(i, last):
            for n in range(STREAM):
                if n == 0:
                    sp.wait_ge(b_c0f, 8 * i)
                    sp.wait_ge(b_c1f, 8 * i)
                    src = f_dram[bass.ds(2 * i, 2), 0:SEQ].unsqueeze(0).to_broadcast([P, 2, SEQ])
                    sp.dma_start(FB[:, :, :], src).then_inc(b_fb, 16)
                    sp.wait_ge(b_split, KT + 3 * i + 2)
                    load_w(wqz, (i + KT) * P, 1)
                if n == 4 and not last:
                    sp.wait_ge(b_split, KT + 3 * i + 1)
                    load_w(wkv, (i + 1 + KT) * P, 0)
                if n == 12 and not last:
                    sp.wait_ge(b_split, KT + 3 * i + 3)
                    load_w(wkv, (i + 1) * P, 1)
                if n in (4, 8, 12, 16):
                    c = n // 4 + 1
                    if not (last and c >= 4):
                        sp.wait_ge(b_c1f, 8 * i + n // 4)
                        load_suffix(i + c // 4, c % 4)
                if last and n == 12:
                    sp.wait_ge(b_split, KT + 3 * NB)
                    load_slab(wo_b, 0)
                if last and n >= STREAM - RING:
                    t = n - (STREAM - RING)
                    if t < NT:
                        sp.wait_ge(b_used, NPG * i + n - NPG + 1)
                        sp.dma_start(X[0:rows(t), t, :], h_dram[t * P:t * P + rows(t), :]).then_inc(s_hld, 16)
                else:
                    sp.wait_ge(s_rows, 16 * 9)
                    if n < NPG:
                        sp.wait_ge(b_t1, 24 * i + n + 1)
                    else:
                        sp.wait_ge(b_used, NPG * i + n - NPG + 1)
                    load_page(i + (n + RING) // STREAM, (n + RING) % STREAM)

        with sp.Fori(0, NB - 1) as i:
            heads(i, False)
        heads(NB - 1, True)

        sp.wait_ge(b_t1f, 24 * NB)
        sp.dma_start(v_sample.rearrange("b q h d -> (b q) (h d)"), VS[:, :]).then_inc(s_out, 16)
        with sp.Fori(1, NSLAB) as n:
            sp.wait_ge(l_split, n + NSLAB)
            load_slab(wo_b, n * SLAB)
        for t in range(NT):
            sp.wait_ge(l_evac, 5 * (2 * NSLAB - 1) + t + 1)
            if t < QB:
                sp.dma_start(y_prompt[0, toks(t), :], X[:, t, :]).then_inc(s_out, 16)
            else:
                sp.dma_start(y_sample.rearrange("b q n -> (b q) n"), X[0:NS, t, :]).then_inc(s_out, 16)
        sp.wait_ge(s_out, 16 * (2 + 1 + NT))
        sp.wait_ge(b_kpo, 16 * NB)
        sp.wait_ge(b_kso, 16 * NB)
        sp.wait_ge(b_vpo, 16 * NB)

    @block.gpsimd
    def _(pool):
        pool.wait_ge(s_idx, 16)
        pool.indirect_dma_start(
            LF[:, :, :].rearrange("p n h -> p (n h)"), None, cache_logf.rearrange("g p h -> g (p h)"),
            bass.IndirectOffsetOnAxis(ap=PIDX[:, 0:1], axis=0)).then_inc(s_lf, 16)
        pool.memset(QZ[:, :, :, :], 0.0).then_inc(s_zero, 1)

        pool.wait_ge(s_gain, 1)
        for q in range(2):
            pool.wait_ge(a_raw[q], 16)
            pool.tensor_tensor(WR[:, q, :, :], WR[:, q, :, :], gain(G_A), ALU.mult).then_inc(a_scaled, 1)

        def mixer(i, last):
            for q in range(4):
                if not (last and q >= 2):
                    pool.wait_ge(a_raw[q % 2], (2 * i + q // 2 + 2) * 16)
                    pool.tensor_tensor(WR[:, q % 2, :, :], WR[:, q % 2, :, :], gain(G_A),
                                       ALU.mult).then_inc(a_scaled, 1)
                if q == 2:
                    pool.wait_ge(a_z, i + 1)
                    pool.wait_ge(a_cv, i + 1)
                    pool.tensor_tensor(RR[:, :], RR[:, :], SZ[:, :], ALU.mult).then_inc(a_cvz, 1)

        with pool.Fori(0, KT - 1) as i:
            mixer(i, False)
        mixer(KT - 1, True)
        pool.wait_ge(s_sfx, 1)
        for b in range(NB):
            pool.dma_start(suffix_dram[b].rearrange("h (g n) -> g h n", g=NPG),
                           CS[b * NPG:(b + 1) * NPG, :, :]).then_inc(s_sfx_st, 16)
        pool.wait_ge(s_wf, 16)
        pool.tensor_tensor(WFR[:, :, :], WFR[:, :, :],
                           GAIN[:, G_KV:G_KV + KT].unsqueeze(2).to_broadcast([P, KT, H]), ALU.mult).then_inc(s_wfs, 1)

        def scale_b(slot, count, g):
            pool.wait_ge(b_raw[slot], 16 * count)
            pool.tensor_tensor(WR[:, slot, :, :], WR[:, slot, :, :], gain(g), ALU.mult).then_inc(b_scaled, 1)

        for n in range(10):
            scale_b(n % 2, n // 2 + 1, G_B if n < KT else G_KV)
        pool.wait_ge(q_out, KT)
        pool.tensor_copy(QC[:, :, :], QZ[:, 0, :, :]).then_inc(b_qc, 1)
        pool.tensor_copy(QT[:, :], QF[:, 0, 0:SEQ]).then_inc(b_qt, 1)

        def heads(i, last):
            scale_b(1, 6 + 2 * i, G_B)
            if not last:
                scale_b(0, 6 + i, G_KV)
            pool.wait_ge(b_rr, i + 1)
            pool.tensor_tensor(KN_T[:, :], KN_T[:, :], RR[:, :], ALU.mult).then_inc(b_normed, 1)
            if not last:
                scale_b(1, 7 + 2 * i, G_KV)
                pool.wait_ge(b_c1, 8 * i + 4)
                pool.tensor_copy(QC[:, :, :].rearrange("p k n -> p (k n)"),
                                 QZ[:, bass.ds(i + 1, 1), :, :].rearrange("p a k n -> p (a k n)")).then_inc(b_qc, 1)
                pool.wait_ge(b_c0, 8 * i + 8)
                pool.wait_ge(b_c1, 8 * i + 8)
                pool.tensor_copy(QT[:, :], QF[:, bass.ds(i + 1, 1), 0:SEQ].rearrange("p a n -> p (a n)")).then_inc(b_qt, 1)

        with pool.Fori(0, NB - 1) as i:
            heads(i, False)
        heads(NB - 1, True)

    @block.scalar
    def _(act):
        ch = Chain(act, s_ch_act)

        def norm(t, phase):
            n = NT * phase + t
            r = rows(t)
            if phase == 0:
                act.wait_ge(s_x[t], 16)
            else:
                act.wait_ge(l_evac, 5 * (NSLAB - 1) + t + 1)
            c = 6 * (t % 2)
            if n >= 2:
                act.wait_ge(s_xs, n - 1)
            ch.link(act.activation(JUNK[0:r, :], X[0:r, t, :], ACT.Square, accum_out=TINY[0:r, 4 + c:5 + c]))
            act.activation(TINY[0:r, 5 + c:6 + c], TINY[0:r, 4 + c:5 + c], ACT.Sqrt, bias=EPSB(r),
                           scale=1.0 / D).then_inc(s_rms, 1)

        def EPSB(r):
            return TINY[0:r, 3:4]

        def norm_high(t, phase):
            n = NT * phase + t
            b = NORM_BANKS[n]
            act.wait_ge(s_xt, n + 1)
            src = PS[:, b:b + 2, :].rearrange("p a (k n) -> p (a k) n", k=4)[:, :, 0:rows(t)]
            act.activation(XH[:, :, toks(t)], src, ACT.Copy).then_inc(s_xh, 1)

        act.preload_act_table_set("sqrt_and_friends")
        act.wait_ge(s_bf, 3)

        def high_a(n, slot):
            act.wait_ge(a_scaled, n + 1)
            act.activation(WH[:, slot, :, :], WR[:, slot, :, :], ACT.Copy).then_inc(a_high, 1)

        norm(0, 0)
        for t in range(NT):
            if t + 1 < NT:
                norm(t + 1, 0)
            norm_high(t, 0)
            if t == 2:
                high_a(0, 0)
        high_a(1, 1)

        def high_slab(s):
            act.activation(slab_h[s], WRA, ACT.Copy).then_inc(l_high, 1)

        def mixer(i, last):
            for q in range(4):
                act.wait_ge(a_proj, 4 * i + q + 1)
                if not (last and q >= 2):
                    high_a(4 * i + q + 2, q % 2)
                pr, sa = both(2 * q)
                if q == 0:
                    act.wait_ge(a_v, i)
                    act.activation(prompt2(SQ[:, 0:SEQ]), pr, ACT.Copy)
                    act.activation(SQ[:, SEQ:TOK], sa, ACT.Copy).then_inc(a_c, 1)
                if q == 2:
                    act.wait_ge(a_cvz, i)
                    act.activation(prompt2(SZ[:, 0:SEQ]), pr, ACT.Silu)
                    act.activation(SZ[:, SEQ:TOK], sa, ACT.Silu).then_inc(a_z, 1)
                    if last:
                        act.wait_ge(l_raw, 16)
                        high_slab(1)
                if q == 3:
                    act.wait_ge(a_g, i + 1)
                    act.activation(GH[:, bass.ds(i, 1), :].rearrange("p a n -> p (a n)"), VT[:, :],
                                   ACT.Copy).then_inc(a_gh, 1)

        with act.Fori(0, KT - 1) as i:
            mixer(i, False)
        mixer(KT - 1, True)

        for n in range(1, NSLAB):
            act.wait_ge(l_raw, 16 * (n + 1))
            if n >= 2:
                act.wait_ge(l_tile, NT * (n - 1))
            high_slab(1 - n % 2)
        act.wait_ge(s_wfs, 1)
        act.activation(WFH[:, :, :], WFR[:, :, :], ACT.Copy).then_inc(s_wfh, 1)

        def high_b(n, slot, to=None):
            act.wait_ge(b_scaled, n + 1)
            act.activation(to or WH[:, slot, :, :], WR[:, slot, :, :], ACT.Copy).then_inc(b_high, 1)

        act.wait_ge(l_tile, NT * (NSLAB - 1))
        high_b(0, 0, first_q[0][0])
        high_b(1, 1, first_q[1][0])

        act.preload_act_table_set("sqrt_and_friends")
        for t in range(NT):
            norm(t, 1)
            if t:
                norm_high(t - 1, 1)
        norm_high(NT - 1, 1)
        log_exp = "natural_log_exp_and_others"
        act.preload_act_table_set(log_exp)
        act.wait_ge(s_ctt, 1)
        act.activation(CO[:, :].rearrange("p (a n) -> p a n", a=2), PS[0:18, 2:4, :], ACT.Copy).then_inc(s_co, 1)
        act.wait_ge(s_fneg, 1)
        ch.link(act.activation(FE[:, :], FN[:, :], ACT.Exp))
        act.activation(FE[:, :], FE[:, :], ACT.Ln, bias=1.0).then_inc(s_fe, 1)

        def query(m, s):
            pr, sa = both(C0 * s)
            act.wait_ge(b_proj, m + 1)
            act.wait_ge(q_ss, m)
            act.activation(prompt2(SQ[:, 0:SEQ]), pr, ACT.Square)
            act.activation(SQ[:, SEQ:TOK], sa, ACT.Square).then_inc(q_sq, 1)
            high_b(m + 2, s)
            act.wait_ge(q_ss, m + 1)
            act.wait_ge(q_out, m)
            act.activation(RR[:, 0:SEQ], PS[:, OP, :], ACT.Ln, bias=EPSB(P), scale=1.0 / HD)
            act.activation(RR[:, SEQ:TOK], PS[:, OS, 0:NS], ACT.Ln, bias=EPSB(P), scale=1.0 / HD).then_inc(q_ln, 1)
            act.wait_ge(q_ln, m + 1)
            act.activation(RR[:, :], RR[:, :], ACT.Exp, scale=-0.5).then_inc(q_rr, 1)

        act.wait_ge(s_wfl, 1)
        with act.Fori(0, KT // 2) as j:
            for s in range(2):
                query(2 * j + s, s)

        act_done = ch.n

        def heads(i, last):
            t0 = [0]

            def turned0(out, src):
                act.wait_ge(b_t0, 24 * i + t0[0] + 1)
                t0[0] += 1
                return act.activation(out, src, ACT.Copy)

            for k in range(NPG):
                c = (k % 2) * PAGE
                if k % 2 == 0 and k >= 4:
                    act.wait_ge((b_c0, b_c1)[k // 2 % 2], 8 * i + k // 4)
                turned0(KTS[k // 2 % 2][:, 0:4, c:c + PAGE],
                        PS[:, T0, :].rearrange("p (k n) -> p k n", k=4)).then_inc(b_t0f, 1)
                if k == 6:
                    pr, sa = both(D0)
                    act.wait_ge(b_proj, KT + 3 * i + 1)
                    act.wait_ge(b_gl, i)
                    act.wait_ge(b_ddve, i + 1)
                    act.activation(prompt2(SQ[:, 0:SEQ]), pr, ACT.Square)
                    act.activation(SQ[:, SEQ:TOK], sa, ACT.Square).then_inc(b_dact, 1)
                if k == 10:
                    high_b(KT + 3 * i + 2, 1)
                if k == 14:
                    pr, sa = both(D0)
                    act.wait_ge(b_proj, KT + 3 * i + 2)
                    act.activation(prompt2(VT[:, 0:SEQ]), pr, ACT.Copy)
                    act.activation(VT[:, SEQ:TOK], sa, ACT.Copy).then_inc(b_dact, 1)
                if k == 9:
                    act.wait_ge(b_ss, i + 1)
                    act.wait_ge(b_normed, i)
                    act.activation(RR[:, SEQ:TOK], PS[:, OS, 0:NS], ACT.Ln, bias=EPSB(P), scale=1.0 / HD)
                    act.activation(RR[:, 0:SEQ], PS[:, OP, :], ACT.Ln, bias=EPSB(P), scale=1.0 / HD).then_inc(b_ln, 1)
                    act.wait_ge(b_ln, i + 1)
                    act.activation(RR[:, :], RR[:, :], ACT.Exp, scale=-0.5).then_inc(b_rr, 1)
            if not last:
                high_b(KT + 3 * i + 3, 0)
            act.wait_ge(b_kpo, 16 * i)
            act.wait_ge(b_vpo, 16 * i)
            turned0(KN[:, 0:QB, :], PS[:, T0, :].rearrange("p (k n) -> p k n", k=4)).then_inc(b_t0f, 1)
            turned0(VN[:, :, :], PS[:, T0, :].rearrange("p (k n) -> p k n", k=4)).then_inc(b_t0f, 1)
            act.wait_ge(b_nbs, i + 1)
            act.wait_ge(b_lp, i)
            for c in range(4):
                ins = act.activation(SS[:, c * 512:(c + 1) * 512], SS[:, c * 512:(c + 1) * 512], ACT.Exp,
                                     bias=TINY[:, 13:14], accum_out=TINY[:, 16 + c:17 + c])
                ins.then_inc(b_es, 1)
            for g in (0, 2):
                turned0(PTS[:, 4 * g:4 * g + 4, :], PS[:, T0, :].rearrange("p (k n) -> p k n", k=4)).then_inc(b_t0f, 1)
            cols = bass.ds(i * P, P)
            act.wait_ge(b_t0f, 24 * i + 18)
            act.wait_ge(b_t1f, 24 * i + 17)
            act.dma_start(k_prompt[0].rearrange("(t p) h d -> p t (h d)", p=P)[:, :, cols], KN[:, 0:QB, :]).then_inc(b_kpo, 16)
            act.dma_start(v_prompt[0].rearrange("(t p) h d -> p t (h d)", p=P)[:, :, cols], VN[:, :, :]).then_inc(b_vpo, 16)
            act.dma_start(k_sample.rearrange("b q h d -> (b q) (h d)")[:, cols], KN[0:NS, QB, :]).then_inc(b_kso, 16)

            def block_exp(r):
                w = (QB - r) * P
                c = 20 + 20 * (r % 2)
                act.wait_ge(b_nbp, 4 * i + r + 1)
                for e in range(2):
                    act.activation(PB[r % 2][:, e, 0:w], PB[r % 2][:, e, 0:w], ACT.Exp, bias=TINY[:, c + 4 + e:c + 5 + e],
                                   accum_out=TINY[:, c + 6 + e:c + 7 + e]).then_inc(b_ep, 1)

            def block_turned(r):
                w = (QB - r) * P
                turned0(PT[:, 0, 0:QB - r, :], PS[:, T0, 0:w].rearrange("p (k n) -> p k n", n=P)).then_inc(b_t0f, 1)

            def gate_log():
                pr, sa = both(D0)
                act.wait_ge(b_proj, KT + 3 * i + 3)
                act.wait_ge(b_gf, i)
                act.activation(prompt2(SZ[:, 0:SEQ]), pr, ACT.Abs)
                ch.link(act.activation(SZ[:, SEQ:TOK], sa, ACT.Abs))
                ch.link(act.activation(SZ[:, :], SZ[:, :], ACT.Exp, scale=-1.0))
                act.activation(SZ[:, :], SZ[:, :], ACT.Ln, bias=1.0).then_inc(b_zl, 1)

            ch.loop(i, LINKS["act_b"], act_done)
            block_exp(0)
            block_exp(1)
            block_turned(0)
            block_exp(2)
            block_turned(1)
            gate_log()
            block_exp(3)
            block_turned(2)
            if not last:
                high_b(KT + 3 * i + 4, 1)
            act.wait_ge(b_zm, i + 1)
            act.activation(SZ[:, :], SZ[:, :], ACT.Exp).then_inc(b_ze, 1)
            block_turned(3)
            if last:
                act.wait_ge(l_raw, 16 * (NSLAB + 1))
                high_slab(0)
            ch.end()
            assert t0[0] == 24
            act.wait_ge(b_used, NPG * (i + 1))
            act.activation(OPAST[:, bass.ds(i, 1), :].rearrange("p a n -> p (a n)"), PS[:, OS, 0:4 * HD],
                           ACT.Copy).then_inc(b_sot, 1)
            act.wait_ge(b_gf, i + 1)
            act.activation(GH[:, bass.ds(i, 1), 0:SEQ].rearrange("p a n -> p (a n)"), SQ[:, 0:SEQ],
                           ACT.Copy).then_inc(b_gh, 1)

        with act.Fori(0, NB - 1) as i:
            heads(i, False)
        heads(NB - 1, True)

        act.wait_ge(m_exp, 1)
        act.activation(TINY[:, 40:48], TINY[:, 40:48], ACT.Exp).then_inc(m_a, 1)
        for b in range(NB):
            act.activation(SN[:, b, :], SN[:, b, :], ACT.Exp, bias=TINY[:, 48 + b:49 + b],
                           accum_out=TINY[:, 56 + b:57 + b]).then_inc(m_p, 1)
        act.wait_ge(m_t, 1)
        act.activation(PNT[:, 0:4, :], PS[0:NS, T0, :].rearrange("p (k n) -> p k n", k=4), ACT.Copy).then_inc(m_ta, 1)
        act.wait_ge(l_raw, 16 * (NSLAB + 2))
        act.wait_ge(b_used, NPG * NB)
        high_slab(1)
        act.wait_ge(m_gs, 1)
        act.activation(GH[:, :, SEQ:TOK], GS[:, :, :], ACT.Copy).then_inc(m_gh, 1)
        for n in (2, 3):
            act.wait_ge(l_raw, 16 * (NSLAB + n + 1))
            act.wait_ge(l_tile, NT * NSLAB + 4 + 2 * n)
            high_slab(n % 2)

    @block.vector
    def _(dve):
        ch = Chain(dve, s_ch_dve)
        dve.memset(TINY[:, 3:4], EPS).then_inc(s_bf, 1)
        dve.wait_ge(s_const, 16)
        dve.tensor_copy(IDB[:, :], ident).then_inc(s_bf, 1)
        dve.tensor_copy(CMB[:, :], CT[:, C_CM:C_CM + P]).then_inc(s_bf, 1)
        def norm_scale(t, phase):
            n = NT * phase + t
            r = rows(t)
            c = 6 * (t % 2) + 4
            v, y, z = TINY[0:r, c:c + 1], TINY[0:r, c + 2:c + 3], TINY[0:r, c + 3:c + 4]
            dve.wait_ge(s_rms, n + 1)
            ch.link(dve.reciprocal(y, TINY[0:r, c + 1:c + 2]))
            ch.link(dve.tensor_scalar(v, v, 1.0 / D, EPS, ALU.mult, ALU.add))
            ch.link(dve.scalar_tensor_tensor(z, y, y, v, ALU.mult, ALU.mult))
            ch.link(dve.tensor_scalar(z, z, -0.5, 1.5, ALU.mult, ALU.add))
            if n >= 2:
                dve.wait_ge(s_xt, n - 1)
            dve.tensor_scalar(XS[n % 2][0:r, :], X[0:r, t, :], y, z, ALU.mult, ALU.mult).then_inc(s_xs, 1)

        def norm_low(t, phase):
            n = NT * phase + t
            b = NORM_BANKS[n]
            dve.wait_ge(s_xh, n + 1)
            src = PS[:, b:b + 2, :].rearrange("p a (k n) -> p (a k) n", k=4)[:, :, 0:rows(t)]
            dve.tensor_tensor(XL[:, :, toks(t)], src, XH[:, :, toks(t)].bitcast(F32), ALU.subtract).then_inc(s_xl, 1)

        norm_scale(0, 0)
        norm_scale(1, 0)
        norm_low(0, 0)
        dve.wait_ge(s_gt, 1)
        dve.tensor_copy(GAIN[:, :], PS[:, 6, 0:G_ALL]).then_inc(s_gain, 1)
        dve.wait_ge(s_gain, 1)
        dve.tensor_scalar(GQ[:, :], GAIN[:, G_Q:G_Q + 1], HD ** -0.5, None, ALU.mult)
        dve.wait_ge(s_stt, 1)
        dve.tensor_copy(ST[:, :, :], PS[:, 7, 128:256].rearrange("p (k n) -> p k n", k=KT)).then_inc(s_st, 1)

        def low_a(n, slot):
            dve.wait_ge(a_high, n + 1)
            dve.tensor_tensor(WL[:, slot, :, :], WR[:, slot, :, :], WH[:, slot, :, :].bitcast(F32),
                              ALU.subtract).then_inc(a_split, 1)

        for t in range(1, NT):
            if t + 1 < NT:
                norm_scale(t + 1, 0)
            norm_low(t, 0)
            if t == 3:
                low_a(0, 0)
        low_a(1, 1)
        dve.wait_ge(s_lf, 16)
        one = CT[:, C_ONE:C_ONE + 1].to_broadcast([P, PAGE])
        for h in range(H):
            dve.tensor_tensor_scan(CS[:, h, :], one, LF[:, :, h], 0.0, ALU.mult, ALU.add).then_inc(s_cs, 1)
        ch.link(dve.memset(EXT[:, 0:2], 0.0))
        done = ch.n

        def low_slab(n, s):
            dve.wait_ge(l_high, n + 1)
            dve.tensor_tensor(slab_l[s], WRA, slab_h[s].bitcast(F32), ALU.subtract).then_inc(l_split, 1)

        def mixer(i, last):
            ch.loop(i, LINKS["dve_a"], done)
            for q in range(4):
                if not (last and q >= 2):
                    low_a(4 * i + q + 2, q % 2)
                pr, sa = both(2 * q)
                if q == 1:
                    st = ST[:, bass.ds(i, 1), :].rearrange("p a (b s) -> p (a b) s", b=NB)
                    dve.tensor_copy(EXTS[:, :, 0:2], st)
                    dve.wait_ge(a_c, i + 1)
                    dve.wait_ge(a_proj, 4 * i + 2)
                    dve.tensor_tensor(prompt2(EXT[:, 2:SEQ + 2]), pr, prompt2(SQ[:, 0:SEQ]), ALU.mult)
                    dve.tensor_tensor(EXTS[:, :, 2:NQ + 2], sa.rearrange("p (b q) -> p b q", b=NB),
                                      SQ[:, SEQ:TOK].rearrange("p (b q) -> p b q", b=NB), ALU.mult).then_inc(a_v, 1)
                    dve.wait_ge(a_v, i + 1)
                    dve.wait_ge(a_g, i)
                    ch.link(dve.tensor_copy(CST[:, bass.ds(i, 1), 0:2].rearrange("p a n -> p (a n)"), EXT[:, SEQ:SEQ + 2]))
                    ch.link(dve.tensor_copy(
                        CST[:, bass.ds(i, 1), 2:18].rearrange("p a (b s) -> p (a b) s", b=NB), EXTS[:, :, NQ:NQ + 2]))
                    cvp = RR[:, 0:SEQ]
                    cvs = RR[:, SEQ:TOK].rearrange("p (b q) -> p b q", b=NB)
                    for j in range(CONV_W):
                        w = GAIN[:, bass.ds(G_CONV + j * KT + i, 1)]
                        if j == 0:
                            ch.link(dve.tensor_scalar(cvp, EXT[:, 0:SEQ], w, None, ALU.mult))
                            ch.link(dve.tensor_scalar(cvs, EXTS[:, :, 0:NQ], w, None, ALU.mult))
                        else:
                            ch.link(dve.scalar_tensor_tensor(cvp, EXT[:, j:j + SEQ], w, cvp, ALU.mult, ALU.add))
                            ins = dve.scalar_tensor_tensor(cvs, EXTS[:, :, j:j + NQ], w, cvs, ALU.mult, ALU.add)
                            if j == 1:
                                ch.link(ins)
                            else:
                                ins.then_inc(a_cv, 1)
                if q == 3:
                    if last:
                        low_slab(0, 1)
                    dve.wait_ge(a_proj, 4 * i + 4)
                    dve.wait_ge(a_cvz, i + 1)
                    ch.link(dve.tensor_tensor(prompt2(VT[:, 0:SEQ]), pr, prompt2(RR[:, 0:SEQ]), ALU.mult))
                    dve.tensor_tensor(VT[:, SEQ:TOK], sa, RR[:, SEQ:TOK], ALU.mult).then_inc(a_g, 1)
                    dve.wait_ge(a_gh, i + 1)
                    gl = GL[:, bass.ds(i, 1), :].rearrange("p a n -> p (a n)")
                    gh = GH[:, bass.ds(i, 1), :].rearrange("p a n -> p (a n)")
                    dve.tensor_tensor(gl, VT[:, :], gh.bitcast(F32), ALU.subtract).then_inc(a_gl, 1)
            ch.end()

        with dve.Fori(0, KT - 1) as i:
            mixer(i, False)
        mixer(KT - 1, True)
        ch.base, ch.n = 0, done + LINKS["dve_a"] * KT

        def out_tile(n, g, bank, t):
            dve.wait_ge(l_tile, n + 1)
            r = rows(t)
            x = X[0:r, t, bass.ds(g * SLAB, SLAB)]
            dve.tensor_tensor(x, PS[0:r, bank, 0:SLAB], x, ALU.add).then_inc(l_evac, 1)

        def low_b(n, slot, to=None):
            h, lo = to or (WH[:, slot, :, :], WL[:, slot, :, :])
            dve.wait_ge(b_high, n + 1)
            dve.tensor_tensor(lo, WR[:, slot, :, :], h.bitcast(F32), ALU.subtract).then_inc(b_split, 1)

        dve.wait_ge(s_rtot, 1)
        dve.tensor_tensor(CS[:, :, :], PS[:, 7, 0:H].unsqueeze(2).to_broadcast([P, H, PAGE]), CS[:, :, :],
                          ALU.subtract).then_inc(s_sfx, 1)
        low_slab(1, 0)
        with dve.Fori(0, NSLAB // 2 - 1) as j:
            for s in range(2):
                for t in range(NT):
                    out_tile(5 * s + t + 10 * j, 2 * j + s, (5 * s + t) % 8, t)
                low_slab(2 * j + s + 2, 1 - s)
        for t in range(NT):
            out_tile(5 * (NSLAB - 2) + t, NSLAB - 2, t, t)
        dve.wait_ge(s_wfh, 1)
        dve.tensor_tensor(WFL[:, :, :], WFR[:, :, :], WFH[:, :, :].bitcast(F32), ALU.subtract).then_inc(s_wfl, 1)
        low_b(0, 0, first_q[0])
        low_b(1, 1, first_q[1])
        for t in range(NT + 3):
            if t >= 3:
                norm_low(t - 3, 1)
            if t < NT:
                out_tile(5 * (NSLAB - 1) + t, NSLAB - 1, (5 + t) % 8, t)
            if 1 <= t <= NT:
                norm_scale(t - 1, 1)
        dve.wait_ge(s_fp, 1)
        ch.link(dve.tensor_scalar(prompt2(FA[:, 0:SEQ]), PS[0:H, 6:8, 0:HALF], FBIAS[:, 0:1], None, ALU.add))
        ch.link(dve.tensor_scalar(FA[:, SEQ:TOK], PS[0:H, 7, HALF:TAIL], FBIAS[:, 0:1], None, ALU.add))
        ch.link(dve.tensor_scalar(FN[:, :], FA[:, :], -1.0, None, ALU.mult))
        dve.tensor_tensor(FN[:, :], FN[:, :], FA[:, :], ALU.min).then_inc(s_fneg, 1)
        dve.wait_ge(s_fe, 1)
        dve.scalar_tensor_tensor(FL[:, :], FA[:, :], 0.0, FE[:, :], ALU.min, ALU.subtract).then_inc(s_fl, 1)
        dve.wait_ge(s_fl, 1)
        dve.wait_ge(s_gt, 1)
        ch.link(dve.tensor_tensor_scan(FT[:, 0:SEQ], CT[0:H, C_ONE:C_ONE + 1].to_broadcast([H, SEQ]), FL[:, 0:SEQ],
                                       0.0, ALU.mult, ALU.add))
        dve.tensor_tensor_scan(FT[:, SEQ:TOK], CT[0:H, C_RST:C_RST + NS], FL[:, SEQ:TOK], 0.0,
                               ALU.mult, ALU.add).then_inc(s_ft, 1)

        dve.wait_ge(s_zero, 1)

        def query(m, s):
            low_b(m + 2, s)
            dve.wait_ge(q_rr, m + 1)
            pr, sa = both(C0 * s)
            dve.scalar_tensor_tensor(prompt2(QF[:, bass.ds(m, 1), 0:SEQ].rearrange("p a n -> p (a n)")), pr, GQ[:, 0:1],
                                     prompt2(RR[:, 0:SEQ]), ALU.mult, ALU.mult)
            for e in range(2):
                h = slice(64 * e, 64 * e + 64)
                c = 16 * s + 8 * e
                ins = dve.scalar_tensor_tensor(
                    QZ[h, :, bass.ds(m, 1), c:c + NQ].rearrange("p b a q -> p (b a) q"),
                    sa[h].rearrange("p (b q) -> p b q", b=NB), GQ[h, 0:1],
                    RR[h, SEQ:TOK].rearrange("p (b q) -> p b q", b=NB), ALU.mult, ALU.mult)
            ins.then_inc(q_out, 1)

        with dve.Fori(0, KT // 2 - 1) as j:
            for s in range(2):
                query(2 * j + s, s)
        query(KT - 2, 0)
        dve.wait_ge(s_fn, 1)
        ch.link(dve.tensor_copy(LFN[:, 0:QB, :], PS[:, T0, 0:QB * H].rearrange("p (t h) -> p t h", h=H)))
        ch.link(dve.tensor_copy(LFN[0:NS, QB, :], PS[0:NS, T0, QB * H:NT * H]))
        dve.tensor_copy(FQN[:, :, :], PS[:, T0, 128:128 + QB * H].rearrange("p (t h) -> p t h", h=H)).then_inc(s_fnr, 1)
        query(KT - 1, 1)
        dve.wait_ge(s_ck, 16)
        qd = CT[:, C_QD:C_QD + NS]
        ch.link(dve.tensor_tensor(KS[:, 0, :], CK[:, :], qd, ALU.mult))
        ch.link(dve.tensor_reduce(CQ[:, :], KS[:, 0, :].rearrange("p (b q) -> p b q", b=NB), AX, ALU.add))

        done_b = ch.n

        def heads(i, last):
            ch.loop(i, LINKS["dve_b"], done_b)
            t1 = [0]

            def turned1(out, src):
                dve.wait_ge(b_t1, 24 * i + t1[0] + 1)
                t1[0] += 1
                return dve.tensor_copy(out, src)

            def add_suffix(u):
                free, bank = ((b_c0f, C0), (b_c1f, C1))[u % 2]
                dve.tensor_tensor_reduce(
                    SS[:, u * 256:(u + 1) * 256], PS[:, bank, 0:256],
                    SFX[:, (u // 2) % 2, (u % 2) * 256:(u % 2) * 256 + 256],
                    1.0, NEG, ALU.add, ALU.max, TINY[:, 4 + u:5 + u]).then_inc(free, 1)

            for k in range(NPG):
                c = (k % 2) * PAGE
                if k % 2 and k >= 3:
                    u = k // 2 - 1
                    if u % 2 == 0:
                        dve.wait_ge(b_sfx[(u // 2) % 2], (2 * i + u // 4 + 1) * 16)
                    dve.wait_ge((b_c0, b_c1)[u % 2], 8 * i + u // 2 + 1)
                if k == 6:
                    dve.wait_ge(b_proj, KT + 3 * i + 1)
                    pr, sa = both(D0)
                    gk = GAIN[:, G_K:G_K + 1]
                    dve.tensor_scalar(prompt2(KN_T[:, 0:SEQ]), pr, gk, None, ALU.mult)
                    dve.tensor_scalar(KN_T[:, SEQ:TOK], sa, gk, None, ALU.mult).then_inc(b_ddve, 1)
                turned1(KTS[k // 2 % 2][:, 4:8, c:c + PAGE],
                        PS[:, T1, :].rearrange("p (k n) -> p k n", k=4)).then_inc(b_t1f, 1)
                if k % 2 and k >= 3:
                    add_suffix(k // 2 - 1)
                if k == 11:
                    low_b(KT + 3 * i + 2, 1)
                if k == 13:
                    dve.wait_ge(b_normed, i + 1)
                    dve.tensor_copy(KS[:, bass.ds(i, 1), :].rearrange("p a n -> p (a n)"), KN_T[:, SEQ:TOK]).then_inc(b_kst, 1)
            dve.wait_ge(s_fnr, 1)
            dve.wait_ge(b_c1, 8 * i + 4)
            add_suffix(NPG // 2 - 1)
            dve.wait_ge(b_c0f, 8 * i + 4)
            dve.wait_ge(b_c1f, 8 * i + 4)
            cq = CQ[:, bass.ds(i, 1)]
            ms = MS[:, bass.ds(i, 1)]
            ch.link(dve.tensor_reduce(TINY[:, 12:13], TINY[:, 4:12], AX, ALU.max))
            ch.link(dve.tensor_tensor(ms, TINY[:, 12:13], cq, ALU.add))
            dve.tensor_tensor(TINY[:, 13:14], cq, ms, ALU.subtract).then_inc(b_nbs, 1)
            dve.wait_ge(b_kso, 16 * i)
            turned1(KN[0:NS, QB, :], PS[0:NS, T1, 0:P]).then_inc(b_t1f, 1)
            turned1(VS[:, bass.ds(i * P, P)], PS[0:NS, T1, 0:P]).then_inc(b_t1f, 1)

            if not last:
                low_b(KT + 3 * i + 3, 0)

            def block_max(r):
                w = (QB - r) * P
                c = 20 + 20 * (r % 2)
                dve.wait_ge(b_c0, 8 * i + 4 + r + 1)
                dve.wait_ge(b_c1, 8 * i + 4 + r + 1)
                if r >= 2:
                    dve.wait_ge(b_t0, 24 * i + 19 + r)
                    dve.wait_ge(b_t1, 24 * i + 19 + r)
                fq = TINY[:, c + 10:c + 12]
                dve.tensor_copy(fq, FQN[:, QB - 1 - r, bass.ds(2 * i, 2)]).then_inc(b_fq, 1)
                for e, (free, bank) in enumerate(((b_c0f, C0), (b_c1f, C1))):
                    dve.tensor_tensor_reduce(PB[r % 2][:, e, 0:w], PS[:, bank, 0:w], FB[:, e, 0:w], 1.0, NEG,
                                             ALU.subtract, ALU.max, TINY[:, c + e:c + e + 1]).then_inc(free, 1)
                dve.wait_ge(b_fq, 4 * i + r + 1)
                dve.wait_ge(b_c0f, 8 * i + 4 + r + 1)
                dve.wait_ge(b_c1f, 8 * i + 4 + r + 1)
                ch.link(dve.tensor_tensor(TINY[:, c + 2:c + 4], TINY[:, c:c + 2], fq, ALU.add))
                dve.tensor_tensor(TINY[:, c + 4:c + 6], fq, TINY[:, c + 2:c + 4], ALU.subtract).then_inc(b_nbp, 1)

            def block_divide(r):
                w = (QB - r) * P
                c = 20 + 20 * (r % 2)
                dve.wait_ge(b_ep, 8 * i + 2 * r + 2)
                ch.link(dve.reciprocal(TINY[:, c + 8:c + 10], TINY[:, c + 6:c + 8]))
                for e in range(2):
                    dve.tensor_scalar(PB[r % 2][:, e, 0:w], PB[r % 2][:, e, 0:w], TINY[:, c + 8 + e:c + 9 + e], None,
                                      ALU.mult).then_inc(b_pn, 1)

            def block_turned(r):
                w = (QB - r) * P
                turned1(PT[:, 1, 0:QB - r, :], PS[:, T1, 0:w].rearrange("p (k n) -> p k n", n=P)).then_inc(b_t1f, 1)

            dve.wait_ge(b_fb, 16 * (i + 1))
            block_max(0)
            for g in (1, 3):
                turned1(PTS[:, 4 * g:4 * g + 4, :], PS[:, T1, :].rearrange("p (k n) -> p k n", k=4)).then_inc(b_t1f, 1)
            dve.wait_ge(b_es, 4 * i + 4)
            dve.tensor_reduce(LS[:, bass.ds(i, 1)], TINY[:, 16:20], AX, ALU.add).then_inc(b_lp, 1)
            block_max(1)
            block_divide(0)
            block_turned(0)
            block_max(2)
            block_divide(1)
            block_turned(1)
            block_divide(2)
            block_max(3)
            pr, sa = both(D0)
            dve.wait_ge(b_zl, i + 1)
            dve.scalar_tensor_tensor(prompt2(SZ[:, 0:SEQ]), pr, 0.0, prompt2(SZ[:, 0:SEQ]), ALU.min, ALU.subtract)
            dve.scalar_tensor_tensor(SZ[:, SEQ:TOK], sa, 0.0, SZ[:, SEQ:TOK], ALU.min, ALU.subtract).then_inc(b_zm, 1)
            block_turned(2)
            block_divide(3)
            block_turned(3)
            dve.wait_ge(b_ze, i + 1)
            dve.tensor_tensor(SZS[:, bass.ds(i, 1), :].rearrange("p a n -> p (a n)"), sa, SZ[:, SEQ:TOK], ALU.mult)
            dve.tensor_tensor(prompt2(SZ[:, 0:SEQ]), pr, prompt2(SZ[:, 0:SEQ]), ALU.mult).then_inc(b_sz, 1)
            if not last:
                low_b(KT + 3 * i + 4, 1)
            assert t1[0] == 24
            dve.wait_ge(b_po, i + 1)
            dve.wait_ge(b_sz, i + 1)
            dve.tensor_tensor(SQ[:, 0:SEQ], PS[:, OP, :], SZ[:, 0:SEQ], ALU.mult).then_inc(b_gf, 1)
            dve.wait_ge(b_gh, i + 1)
            gl = GL[:, bass.ds(i, 1), 0:SEQ].rearrange("p a n -> p (a n)")
            gh = GH[:, bass.ds(i, 1), 0:SEQ].rearrange("p a n -> p (a n)")
            dve.tensor_tensor(gl, SQ[:, 0:SEQ], gh.bitcast(F32), ALU.subtract).then_inc(b_gl, 1)
            ch.end()

        with dve.Fori(0, NB - 1) as i:
            heads(i, False)
        heads(NB - 1, True)
        ch.base, ch.n = 0, done_b + LINKS["dve_b"] * NB

        low_slab(NSLAB, 0)
        nm = CT[:, C_NM:C_NM + NB * NS].rearrange("p (b n) -> p b n", b=NB)
        ch.link(dve.tensor_tensor(NBI[:, :, :], nm, CK[:, :].unsqueeze(1).to_broadcast([P, NB, NS]), ALU.subtract))
        dve.wait_ge(m_s, 1)
        ch.link(dve.tensor_tensor(SN[:, :, :], PS[:, C0, :].rearrange("p (b n) -> p b n", b=NB), NBI[:, :, :], ALU.add))
        tn = TINY
        ch.link(dve.tensor_reduce(tn[:, 4:12], SN[:, :, :], AX, ALU.max))
        ch.link(dve.tensor_tensor(tn[:, 4:12], tn[:, 4:12], CQ[:, :], ALU.add))
        ch.link(dve.tensor_tensor(tn[:, 4:12], tn[:, 4:12], MS[:, :], ALU.max))
        ch.link(dve.tensor_tensor(tn[:, 40:48], MS[:, :], tn[:, 4:12], ALU.subtract))
        dve.tensor_tensor(tn[:, 48:56], CQ[:, :], tn[:, 4:12], ALU.subtract).then_inc(m_exp, 1)
        dve.wait_ge(m_a, 1)
        ch.link(dve.tensor_tensor(LS[:, :], LS[:, :], tn[:, 40:48], ALU.mult))
        dve.wait_ge(m_p, NB)
        ch.link(dve.tensor_tensor(LS[:, :], LS[:, :], tn[:, 56:64], ALU.add))
        ch.link(dve.reciprocal(LS[:, :], LS[:, :]))
        base = NT * NSLAB

        def early_tile(n):
            out_tile(base + n, EARLY[n][0], n % 2, EARLY[n][1])

        dve.wait_ge(s_hld, 16 * NT)
        early_tile(0)
        dve.wait_ge(m_t, 2)
        dve.tensor_copy(PNT[:, 4:8, :], PS[0:NS, T1, :].rearrange("p (k n) -> p k n", k=4)).then_inc(m_td, 1)
        early_tile(1)
        low_slab(NSLAB + 1, 1)
        early_tile(2)
        for b in range(NB):
            dve.wait_ge(m_pv, b // 2 + 1)
            ch.link(dve.scalar_tensor_tensor(OM[:, b, :], OPAST[:, b, :], tn[:, 40 + b:41 + b],
                                             PS[:, C0 + b // 2, (b % 2) * 256:(b % 2) * 256 + 256], ALU.mult, ALU.add))
            dve.tensor_scalar(OM[:, b, :], OM[:, b, :], LS[:, b:b + 1], None, ALU.mult).then_inc(m_om, 1)
        for n in (3, 4, 5):
            early_tile(n)
        for b in range(0, NB, 2):
            dve.wait_ge(m_ot, b // 2 + 1)
            for a in range(2):
                for e in range(2):
                    pr = slice(64 * e, 64 * e + 64)
                    src = PS[pr, T0 + b // 2, :].rearrange(
                        "p (b a j c) -> p a b j c", b=2, a=2, j=4)[:, a, :, :, 8 * (2 * a + e):8 * (2 * a + e) + NQ]
                    out, gate = (z[pr, :, b * NQ:(b + 2) * NQ].rearrange("p (j a) (b q) -> p a b j q", a=2, b=2)[:, a]
                                 for z in (GS, SZS))
                    ins = dve.tensor_tensor(out, src, gate, ALU.mult)
        ins.then_inc(m_gs, 1)
        dve.wait_ge(m_gh, 1)
        dve.tensor_tensor(GL[:, :, SEQ:TOK], GS[:, :, :], GH[:, :, SEQ:TOK].bitcast(F32), ALU.subtract).then_inc(m_gl, 1)
        for n in range(6, 10):
            early_tile(n)
            if n == 8:
                low_slab(NSLAB + 2, 0)
        for s in range(2):
            for t in range(NT):
                out_tile(5 * (2 + s) + t + base, 2 + s, (5 * s + t) % 8, t)
                if s == 0 and t == 2:
                    low_slab(NSLAB + 3, 1)

    @block.tensor
    def _(pe):
        def turn(out, src, r=P):
            return pe.transpose(out, src, CT[0:r, C_ID:C_ID + r])

        pe.wait_ge(s_const, 16)

        def norm_turn(t, phase):
            n = NT * phase + t
            b = NORM_BANKS[n]
            pe.wait_ge(s_xs, n + 1)
            if n in NORM_BANKS_FREE:
                pe.wait_ge(s_xl, NORM_BANKS_FREE[n])
            for k in range(KT):
                mm = turn(PS[:, b + k // 4, (k % 4) * P:(k % 4) * P + rows(t)], XS[n % 2][0:rows(t), k * P:(k + 1) * P], rows(t))
            mm.then_inc(s_xt, 1)

        norm_turn(0, 0)
        norm_turn(1, 0)
        pe.wait_ge(s_rows, 16 * 9)
        turn(PS[:, 6, 0:G_ALL], GR[:, :], G_ALL).then_inc(s_gt, 1)
        for k in range(KT):
            mm = turn(PS[:, 7, 128 + 16 * k:144 + 16 * k], STN[:, k * P:(k + 1) * P], 2 * NB)
        mm.then_inc(s_stt, 1)
        for t in range(2, NT):
            norm_turn(t, 0)
        def piece(slot, k, bank, weights=None, halves=(0, 1)):
            wh, wl = weights or (WH[:, slot, :, :], WL[:, slot, :, :])
            for n, (w, x) in enumerate(((wh, XH), (wh, XL), (wl, XH))):
                for h in halves:
                    c = (slice(0, HALF), slice(HALF, TOK))[h]
                    mm = pe.matmul(PS[:, bank + h, 0:c.stop - c.start], w[:, k, :], x[:, k, c],
                                   start=(k == 0 and n == 0), stop=(k == KT - 1 and n == 2))
            return mm

        pe.wait_ge(s_xl, NT)
        pe.wait_ge(s_st, 1)

        def mixer(i):
            for q in range(4):
                pe.wait_ge(a_split, 4 * i + q + 1)
                pe.wait_ge((a_c, a_v, a_z, a_g)[q], i)
                for k in range(KT):
                    mm = piece(q % 2, k, 2 * q)
                mm.then_inc(a_proj, 1)

        with pe.Fori(0, KT) as i:
            mixer(i)
        def out_tile(w, t, bank, last_gated=None):
            r = rows(t)
            for k in range(KT):
                if last_gated and k == KT - 1:
                    pe.wait_ge(*last_gated)
                for p, (wp, x) in enumerate(((slab_h[w], GH), (slab_h[w], GL), (slab_l[w], GH))):
                    mm = pe.matmul(PS[0:r, bank, 0:SLAB], x[:, k, toks(t)], wp[:, k, :],
                                   start=(k == 0 and p == 0), stop=(k == KT - 1 and p == 2))
            mm.then_inc(l_tile, 1)

        def out_slab(g, s, n, w):
            pe.wait_ge(l_split, g + 1)
            for t in range(NT):
                pe.wait_ge(l_evac, n + t - 1)
                out_tile(w, t, (5 * s + t) % 8)

        pe.wait_ge(l_split, 1)
        pe.wait_ge(a_gl, KT - 1)
        pe.wait_ge(a_v, KT)
        out_tile(1, 0, 0, (a_gl, KT))
        pe.wait_ge(s_cs, H)
        pe.matmul(PS[:, 7, 0:H], CT[:, C_TRI:C_TRI + P], CS[:, :, PAGE - 1], start=True, stop=True).then_inc(s_rtot, 1)
        for t in range(1, NT):
            out_tile(1, t, t)
        pe.wait_ge(s_sfx, 1)
        out_slab(1, 1, 5, 0)
        out_slab(2, 0, 10, 1)
        pe.wait_ge(l_split, NSLAB)
        for t in range(NT):
            pe.wait_ge(l_evac, 15 + t - 1)
            out_tile(0, t, (5 + t) % 8)
            if t >= 2:
                norm_turn(t - 2, 1)
        def forget_gates(h):
            c = (slice(0, HALF), slice(HALF, TOK))[h]
            for k in range(KT):
                for w, x in ((WFH, XH), (WFH, XL), (WFL, XH)):
                    mm = pe.matmul(PS[0:H, 6 + h, 0:c.stop - c.start], w[:, k, :], x[:, k, c],
                                   start=(k == 0 and w is WFH and x is XH), stop=(k == KT - 1 and w is WFL))
            return mm

        pe.wait_ge(s_wfl, 1)
        pe.wait_ge(s_xl, NT + 2)
        forget_gates(0)
        norm_turn(3, 1)
        norm_turn(4, 1)
        def q_sum():
            pe.matmul(PS[:, OS, 0:NS], CT[:, C_ONESB:C_ONESB + P], SQ[:, SEQ:TOK], start=True, stop=True)
            pe.matmul(PS[:, OP, :], CT[:, C_ONESB:C_ONESB + P], SQ[:, 0:SEQ], start=True, stop=True).then_inc(q_ss, 1)

        def query(m, s, weights=None):
            pe.wait_ge(b_split, m + 1)
            pe.wait_ge(q_out, m - 1)
            for k in range(KT):
                mm = piece(s, k, C0 * s, weights)
                if k == 2:
                    if weights:
                        pe.wait_ge(s_fneg, 1)
                    pe.wait_ge(q_sq, m)
                    pe.wait_ge(q_rr, m - 1)
                    q_sum()
            mm.then_inc(b_proj, 1)

        pe.wait_ge(b_split, 1)
        for k in range(KT):
            piece(0, k, D0, first_q[0], (0,))
        pe.wait_ge(s_xl, 2 * NT)
        for k in range(KT):
            mm = turn(PS[0:18, T0 + k // 4, (k % 4) * P:(k % 4 + 1) * P], CST[:, k, :])
        mm.then_inc(s_ctt, 1)
        forget_gates(1).then_inc(s_fp, 1)
        for k in range(KT):
            mm = piece(0, k, D0, first_q[0], (1,))
        mm.then_inc(b_proj, 1)
        query(1, 1, first_q[1])
        with pe.Fori(1, KT // 2 - 1) as j:
            for s in range(2):
                query(2 * j + s, s)
        query(KT - 2, 0)
        pe.wait_ge(s_ft, 1)
        pe.wait_ge(s_co, 1)
        for t in range(NT):
            turn(PS[0:rows(t), T0, t * H:(t + 1) * H], FL[:, toks(t)], H)
        for t in range(QB):
            mm = turn(PS[:, T0, 128 + t * H:128 + (t + 1) * H], FT[:, toks(t)], H)
        mm.then_inc(s_fn, 1)
        query(KT - 1, 1)
        pe.wait_ge(q_sq, KT)
        pe.wait_ge(q_rr, KT - 1)
        q_sum()
        pe.wait_ge(s_fnr, 1)

        def heads(i):
            t0, t1 = [0], [0]

            def free0():
                pe.wait_ge(b_t0f, 24 * i + t0[0])
                t0[0] += 1

            def free1():
                pe.wait_ge(b_t1f, 24 * i + t1[0])
                t1[0] += 1

            def project(q, ks):
                if ks[0] == 0:
                    pe.wait_ge(b_split, KT + 3 * i + (2, 1, 3)[q])
                    if q == 0:
                        pe.wait_ge(b_sz, i)
                    else:
                        pe.wait_ge(b_dact, 2 * i + q)
                    if q == 1:
                        pe.wait_ge(b_ddve, i + 1)
                for k in ks:
                    mm = piece((1, 0, 1)[q], k, D0)
                if ks[-1] == KT - 1:
                    mm.then_inc(b_proj, 1)

            def unit_scores(u):
                full, free, bank = ((b_c0, b_c0f, C0), (b_c1, b_c1f, C1))[u % 2]
                if u == 0:
                    pe.wait_ge(b_qc, i + 1)
                    pe.wait_ge(q_out, KT)
                pe.wait_ge(free, 8 * i + u // 2)
                pe.wait_ge(b_t0f, 24 * i + 2 * u + 2)
                pe.wait_ge(b_t1f, 24 * i + 2 * u + 2)
                for pp in range(2):
                    for j in range(4):
                        mm = pe.matmul(PS[32 * j:32 * j + 32, bank, 0:256], QC[:, 2 * j + pp, :],
                                       KTS[u % 2][:, 2 * j + pp, :],
                                       start=(pp == 0), stop=(pp == 1), tile_position=(0, 32 * j))
                mm.then_inc(full, 1)

            for k in range(NPG):
                pe.wait_ge(b_page[k % RING], (4 * i + k // RING + 1) * 16)
                page = ring[:, k % RING, :]
                free0()
                for p in range(4):
                    mm = turn(PS[:, T0, p * P:(p + 1) * P], page[:, p * P:(p + 1) * P])
                mm.then_inc(b_t0, 1)
                free1()
                for p in range(4):
                    mm = turn(PS[:, T1, p * P:(p + 1) * P], page[:, (4 + p) * P:(5 + p) * P])
                mm.then_inc(b_t1, 1)
                if k == 9:
                    pe.wait_ge(b_dact, 2 * i + 1)
                    pe.wait_ge(b_gf, i)
                    pe.wait_ge(b_sot, i)
                    pe.matmul(PS[:, OS, 0:NS], CT[:, C_ONESB:C_ONESB + P], SQ[:, SEQ:TOK], start=True, stop=True)
                    pe.matmul(PS[:, OP, :], CT[:, C_ONESB:C_ONESB + P], SQ[:, 0:SEQ], start=True, stop=True).then_inc(b_ss, 1)
                if k < 6:
                    project(0, ([0, 1], [2, 3], [4], [5], [6], [7])[k])
                if 7 <= k < 15:
                    project(1, [k - 7])
                if k % 2 == 0 and k >= 2:
                    unit_scores(k // 2 - 1)

            def block_scores(r):
                s = QB - 1 - r
                w = (s + 1) * P
                pe.wait_ge(b_c0f, 8 * i + 4 + r)
                pe.wait_ge(b_c1f, 8 * i + 4 + r)
                heads2 = ((slice(0, 64), C0, b_c0), (slice(64, 128), C1, b_c1))
                if s:
                    for pr, bank, full in heads2:
                        pe.matmul(PS[:, bank, 0:w - P], QT[pr, toks(s)], KN_T[pr, 0:w - P], start=True, stop=True)
                for pr, bank, full in heads2:
                    pe.matmul(PS[:, bank, w - P:w], QT[pr, toks(s)], KN_T[pr, toks(s)], start=True, stop=False)
                for pr, bank, full in heads2:
                    pe.matmul(PS[:, bank, w - P:w], IDB[:, :], CMB[:, :], start=False, stop=True).then_inc(full, 1)

            def block_turn(r):
                for e in range(2):
                    pe.wait_ge(b_pn, 8 * i + 2 * r + e + 1)
                    (free0, free1)[e]()
                    for kb in range(QB - r):
                        mm = turn(PS[:, T0 + e, kb * P:(kb + 1) * P], PB[r % 2][:, e, kb * P:(kb + 1) * P])
                    mm.then_inc((b_t0, b_t1)[e], 1)

            def block_out(r):
                s = QB - 1 - r
                pe.wait_ge(b_t0f, 24 * i + 21 + r)
                pe.wait_ge(b_t1f, 24 * i + 21 + r)
                for kb in range(s + 1):
                    for e in range(2):
                        mm = pe.matmul(PS[64 * e:64 * e + 64, OP, toks(s)], VN[:, kb, 64 * e:64 * e + 64],
                                       PT[:, e, kb, :], start=(kb == 0), stop=(kb == s))
                if r == QB - 1:
                    mm.then_inc(b_po, 1)

            project(2, [0])
            unit_scores(NPG // 2 - 1)
            project(2, [1])
            pe.wait_ge(b_normed, i + 1)
            for src in (KN_T, VT):
                free0()
                free1()
                for t in range(QB):
                    mm = turn(PS[:, T0, t * P:(t + 1) * P], src[:, toks(t)])
                mm.then_inc(b_t0, 1)
                turn(PS[0:NS, T1, 0:P], src[:, SEQ:TOK]).then_inc(b_t1, 1)
                if src is KN_T:
                    project(2, [2])
            pe.wait_ge(b_qt, i + 1)
            block_scores(0)
            project(2, [3])
            for g in range(4):
                pe.wait_ge(b_es, 4 * i + g + 1)
                (free0, free1)[g % 2]()
                for p in range(4):
                    c = (4 * g + p) * P
                    mm = turn(PS[:, T0 + g % 2, p * P:(p + 1) * P], SS[:, c:c + P])
                mm.then_inc((b_t0, b_t1)[g % 2], 1)
                if g == 1:
                    project(2, [4])
            steps = {0: [(block_scores, 1)], 3: [(block_turn, 0)], 4: [(block_scores, 2)], 5: [(block_out, 0)],
                     7: [(block_turn, 1)], 8: [(block_scores, 3), (block_out, 1)], 10: [(block_turn, 2)],
                     12: [(block_out, 2)], 13: [(block_turn, 3)], 15: [(block_out, 3)]}
            for k in range(NPG):
                for step, r in steps.get(k, []):
                    step(r)
                if k in (1, 2, 4):
                    project(2, [{1: 5, 2: 6, 4: 7}[k]])
                n = NPG + k
                pe.wait_ge(b_page[n % RING], (4 * i + n // RING + 1) * 16)
                if k == 0:
                    pe.wait_ge(b_ln, i + 1)
                if k % 4 == 0:
                    g = k // 4
                    pe.wait_ge((b_t0f, b_t1f)[g % 2], 24 * i + 19 + g // 2)
                for j in range(4):
                    mm = pe.matmul(PS[32 * j:32 * j + 32, OS, 0:4 * HD], PTS[:, k, 32 * j:32 * j + 32],
                                   ring[:, n % RING, 4 * HD * j:4 * HD * (j + 1)],
                                   start=(k == 0), stop=(k == NPG - 1), tile_position=(0, 32 * j))
                mm.then_inc(b_used, 1)
            assert t0[0] == t1[0] == 24

        with pe.Fori(0, NB) as i:
            heads(i)

        pe.wait_ge(b_kst, NB)
        pe.wait_ge(b_c0f, 8 * NB)
        pe.wait_ge(b_c1f, 8 * NB)
        pe.wait_ge(b_gf, NB)
        pe.wait_ge(b_sz, NB)
        for b in range(NB):
            for pp in range(2):
                for j in range(4):
                    mm = pe.matmul(PS[32 * j:32 * j + 32, C0, b * NS:(b + 1) * NS], QZ[:, b, 2 * j + pp, :],
                                   KS[:, 2 * j + pp, :], start=(pp == 0), stop=(pp == 1), tile_position=(0, 32 * j))
        mm.then_inc(m_s, 1)

        def early_tile(n):
            if n in (0, 4):
                pe.wait_ge(l_split, NSLAB + n // 4 + 1)
            if n == 7:
                pe.wait_ge(m_gl, 1)
            if n >= 2:
                pe.wait_ge(l_evac, NT * NSLAB + n - 1)
            out_tile(*EARLY[n], n % 2)

        pe.wait_ge(b_gl, NB)
        early_tile(0)
        early_tile(1)
        for b in range(NB):
            pe.wait_ge(m_p, b + 1)
            mm = turn(PS[0:NS, T0 + b // 4, (b % 4) * P:(b % 4 + 1) * P], SN[:, b, :])
            if b % 4 == 3:
                mm.then_inc(m_t, 1)
        early_tile(2)
        pe.wait_ge(m_ta, 1)
        pe.wait_ge(m_td, 1)
        pe.wait_ge(b_sot, NB)
        for b in range(NB):
            for j in range(4):
                mm = pe.matmul(PS[32 * j:32 * j + 32, C0 + b // 2, (b % 2) * 256:(b % 2) * 256 + 256],
                               PNT[:, b, 32 * j:32 * j + 32], VS[:, 4 * HD * j:4 * HD * (j + 1)],
                               start=True, stop=True, tile_position=(0, 32 * j))
            if b % 2:
                mm.then_inc(m_pv, 1)
        for n in (3, 4, 5):
            early_tile(n)
        for b in range(NB):
            pe.wait_ge(m_om, b + 1)
            for a in range(2):
                mm = turn(PS[:, T0 + b // 2, (2 * (b % 2) + a) * P:(2 * (b % 2) + a + 1) * P],
                          OM[:, b, a * P:(a + 1) * P])
            if b % 2:
                mm.then_inc(m_ot, 1)
        for n in (6, 7, 8, 9):
            early_tile(n)
        for s in range(2):
            out_slab(NSLAB + 2 + s, s, NT * NSLAB + 10 + 5 * s, s)


_INS = ['x_prompt', 'x_sample', 'state_conv', 'cache_k', 'cache_v', 'cache_logf', 'page_table',
        'a_norm', 'a_w_in', 'a_conv', 'a_w_out', 'kv_norm', 'kv_w', 'kv_fbias', 'k_norm',
        'b_norm', 'b_w_in', 'q_norm', 'b_w_out']
_OUTS = [('y_prompt', (1, SEQ, D)), ('y_sample', (NB, NQ, D)), ('conv_prompt', (1, 1, CONV_W - 1, D)),
         ('conv_sample', (1, NB, CONV_W - 1, D)), ('k_prompt', (1, SEQ, H, HD)), ('v_prompt', (1, SEQ, H, HD)),
         ('logf_prompt', (1, SEQ, H)), ('k_sample', (NB, NQ, H, HD)), ('v_sample', (NB, NQ, H, HD)),
         ('logf_sample', (NB, NQ, H))]


def constants():
    import numpy as np

    c = np.zeros((P, C_ALL), np.float32)
    p = np.arange(P)
    c[:, C_ID:C_ID + P] = np.eye(P)
    c[:, C_ONESB:C_ONESB + P] = p[:, None] // HD == p[None] // HD
    same = p[:, None] // NPG == p[None] // NPG
    c[:, C_TRI:C_TRI + P] = same & (p[:, None] >= p[None])
    c[:, C_CM:C_CM + P] = np.where(p[None] <= p[:, None], 0.0, NEG)
    key = np.arange(NS)
    for b in range(NB):
        ok = (key[None] // NQ == b) & (key[None] % NQ <= p[:, None] % NQ)
        c[:, C_NM + b * NS:C_NM + (b + 1) * NS] = np.where(ok, 0.0, NEG)
    c[:, C_QD:C_QD + NS] = key[None] % NQ == p[:, None] % NQ
    c[:, C_RST:C_RST + NS] = key[None] % NQ != 0
    c[:, C_ONE] = 1.0
    return c


def kernel(**inputs):
    import numpy as _np
    import concourse.bacc as _bacc
    from concourse import mybir as _mybir
    from concourse.bass_utils import run_bass_kernel_spmd as _run

    nc = _bacc.Bacc("TRN2", target_bir_lowering=False, num_devices=1, dynamic_dma_scratch_size=4096)
    arrays, args = {}, {}
    given = {n: _np.ascontiguousarray(inputs[n]) for n in _INS}
    given["table"] = constants()
    for name, a in given.items():
        arrays[f"in_{name}"] = a
        args[name] = nc.dram_tensor(f"in_{name}", a.shape, _mybir.dt.from_np(a.dtype), kind="ExternalInput").ap()
    for name, shape in _OUTS:
        args[name] = nc.dram_tensor(f"out_{name}", shape, _mybir.dt.float32, kind="ExternalOutput").ap()
    with ExitStack() as ctx:
        build(nc, ctx, **args)
    r = _run(nc, [arrays], core_ids=[0])
    return tuple(r.results[0][f"out_{name}"] for name, _ in _OUTS)
```
